# Optimizing a Trainium2 kernel written in Bass

```python
import jax, jax.numpy as jnp
from jax import lax
import numpy as np

D_MODEL = 1024
BATCH = 1
SEQ = 1024
DEPTH = 1

CHUNK = 64
N_META = 16
EPS = 1e-6

POOL_GROUPS = 4
POOL_WINDOWS = (2, 4, 8, 16)
POOL_WIDTH = D_MODEL // 4
POOL_GDIM = POOL_WIDTH // POOL_GROUPS
CONV_WIDTH = D_MODEL // 4
CONV_KSIZE = 31
FOX_HEADS = 8
FOX_HEAD_DIM = 64
FOX_WIDTH = FOX_HEADS * FOX_HEAD_DIM
Q_BLOCK = 128
N_BRANCH = 3
IN_SPLITS = (POOL_WIDTH, CONV_WIDTH, CONV_WIDTH, FOX_WIDTH, FOX_WIDTH, FOX_WIDTH, FOX_HEADS, N_BRANCH * D_MODEL)
N_IN = sum(IN_SPLITS)
N_GROUPS = 4
EXPERTS_PER_GROUP = 4
N_EXPERTS = N_GROUPS * EXPERTS_PER_GROUP
TOP_K = 2
EXPERT_HIDDEN = D_MODEL // 4


def rms_norm(x, g):
    xf = x.astype(jnp.float32)
    y = xf * lax.rsqrt(jnp.mean(xf * xf, axis=-1, keepdims=True) + EPS)
    return (y * g.astype(jnp.float32)).astype(x.dtype)

def layer_norm(x, g, b):
    xf = x.astype(jnp.float32)
    mu = jnp.mean(xf, axis=-1, keepdims=True)
    var = jnp.mean(jnp.square(xf - mu), axis=-1, keepdims=True)
    y = (xf - mu) * lax.rsqrt(var + EPS)
    return (y * g.astype(jnp.float32) + b.astype(jnp.float32)).astype(x.dtype)

def pool_mixer(a, pool_w, pool_b, pool_scale):
    B_, L, _ = a.shape
    af = a.astype(jnp.float32).reshape(B_, L, POOL_GROUPS, POOL_GDIM)
    cs = jnp.concatenate([jnp.zeros_like(af[:, :1]), jnp.cumsum(af, axis=1)], axis=1)
    t = jnp.arange(L, dtype=jnp.int32)[:, None]
    win = jnp.array(POOL_WINDOWS, dtype=jnp.int32)[None, :]
    lo = jnp.maximum(t + 1 - win, 0)
    cnt = (t + 1 - lo).astype(jnp.float32)
    grp = jnp.arange(POOL_GROUPS, dtype=jnp.int32)[None, :]
    mean = (cs[:, 1:] - cs[:, lo, grp]) / cnt[None, :, :, None]
    diff = mean - af
    y = jnp.einsum('blgc,gcd->blgd', diff, pool_w.astype(jnp.float32)) + pool_b.astype(jnp.float32)
    y = y.reshape(B_, L, POOL_WIDTH) * pool_scale.astype(jnp.float32)
    return y.astype(a.dtype)

def conv_module(bv, bg, conv_w, conv_b, ln_g, ln_b):
    glu = bv * jax.nn.sigmoid(bg)
    y = lax.conv_general_dilated(
        glu, conv_w.astype(glu.dtype)[:, None, :], window_strides=(1,),
        padding=[(CONV_KSIZE - 1, 0)], dimension_numbers=('NWC', 'WIO', 'NWC'),
        feature_group_count=CONV_WIDTH)
    y = y + conv_b.astype(y.dtype)
    y = layer_norm(y, ln_g, ln_b)
    return jax.nn.silu(y)

def forgetting_attention(q, k, v, logf):
    B_, L, H, dh = q.shape
    n_blk = -(-L // Q_BLOCK)
    Lp = n_blk * Q_BLOCK
    pad = Lp - L
    qh = jnp.pad(q.transpose(0, 2, 1, 3), ((0, 0), (0, 0), (0, pad), (0, 0)))
    kh = jnp.pad(k.transpose(0, 2, 1, 3), ((0, 0), (0, 0), (0, pad), (0, 0)))
    vh = jnp.pad(v.transpose(0, 2, 1, 3), ((0, 0), (0, 0), (0, pad), (0, 0)))
    F = jnp.cumsum(jnp.pad(logf.transpose(0, 2, 1), ((0, 0), (0, 0), (0, pad))), axis=-1)
    qb = qh.reshape(B_, H, n_blk, Q_BLOCK, dh).transpose(2, 0, 1, 3, 4)
    Fq = F.reshape(B_, H, n_blk, Q_BLOCK).transpose(2, 0, 1, 3)
    qpos = jnp.arange(Lp, dtype=jnp.int32).reshape(n_blk, Q_BLOCK)
    kpos = jnp.arange(Lp, dtype=jnp.int32)
    scale = FOX_HEAD_DIM ** -0.5

    def block(args):
        qi, Fi, pi = args
        s = jnp.einsum('bhqd,bhkd->bhqk', qi, kh, preferred_element_type=jnp.float32) * scale
        s = s + Fi[..., None] - F[:, :, None, :]
        s = jnp.where(kpos[None, :] <= pi[:, None], s, -jnp.inf)
        p = jax.nn.softmax(s, axis=-1)
        return jnp.einsum('bhqk,bhkd->bhqd', p.astype(vh.dtype), vh)

    o = lax.map(block, (qb, Fq, qpos))
    o = o.transpose(1, 0, 3, 2, 4).reshape(B_, Lp, H * dh)
    return o[:, :L]

def mixer_layer(u, w_in, b_forget, pool_w, pool_b, pool_scale, conv_w, conv_b, conv_ln_g, conv_ln_b,
                w_out_a, w_out_b, w_out_c, w_o):
    B_, L, D = u.shape
    p = u @ w_in
    a, bv, bg, q, k, v, fg, gates = jnp.split(p, [int(i) for i in np.cumsum(IN_SPLITS)[:-1]], axis=-1)
    ya = pool_mixer(a, pool_w, pool_b, pool_scale) @ w_out_a
    yb = conv_module(bv, bg, conv_w, conv_b, conv_ln_g, conv_ln_b) @ w_out_b
    logf = jax.nn.log_sigmoid((fg + b_forget).astype(jnp.float32))
    heads = lambda z: z.reshape(B_, L, FOX_HEADS, FOX_HEAD_DIM)
    yc = forgetting_attention(heads(q), heads(k), heads(v), logf) @ w_out_c
    g = jax.nn.sigmoid(gates.reshape(B_, L, N_BRANCH, D))
    merged = g[:, :, 0] * ya + g[:, :, 1] * yb + g[:, :, 2] * yc
    return merged @ w_o

def hier_moe(h, router_g, router_g_b, router_e, router_e_b, exp_w1, exp_w3, exp_w2):
    B_, L, D = h.shape
    t = h.reshape(B_ * L, D)
    T = t.shape[0]
    glog = (t @ router_g).astype(jnp.float32) + router_g_b.astype(jnp.float32)
    gprob = jax.nn.softmax(glog, axis=-1)
    _, gsel = lax.top_k(glog, 1)
    gw = jnp.take_along_axis(gprob, gsel, axis=-1)
    elog = ((t @ router_e).astype(jnp.float32) + router_e_b.astype(jnp.float32)).reshape(T, N_GROUPS, EXPERTS_PER_GROUP)
    elog_sel = jnp.take_along_axis(elog, gsel[:, :, None], axis=1)[:, 0]
    eprob = jax.nn.softmax(elog_sel, axis=-1)
    top_p, top_i = lax.top_k(eprob, TOP_K)
    top_p = top_p / jnp.sum(top_p, axis=-1, keepdims=True)
    w_grp = jnp.sum(jax.nn.one_hot(top_i, EXPERTS_PER_GROUP, dtype=jnp.float32) * top_p[..., None], axis=1)
    comb = (jax.nn.one_hot(gsel[:, 0], N_GROUPS, dtype=jnp.float32)[:, :, None] * w_grp[:, None, :] * gw[:, :, None])
    comb = comb.reshape(T, N_EXPERTS).astype(t.dtype)
    y = jnp.zeros_like(t)
    for e in range(N_EXPERTS):
        he = jax.nn.silu(t @ exp_w1[e]) * (t @ exp_w3[e])
        y = y + comb[:, e:e + 1] * (he @ exp_w2[e])
    return y.reshape(B_, L, D)

def first_inputs(seed: int = 0) -> dict:
    key = jax.random.key(seed)
    ks = jax.random.split(key, 32)
    f32 = jnp.float32
    nrm = lambda k, shape, s: (jax.random.normal(k, shape, f32) * s).astype(f32)
    D = D_MODEL
    return {
        "x": nrm(ks[0], (BATCH, SEQ, D), 1.0),
        "meta": nrm(ks[1], (N_META, D), 1.0),
        "norm1_g": 1.0 + nrm(ks[2], (DEPTH, D), 0.02),
        "w_in": nrm(ks[3], (DEPTH, D, N_IN), D ** -0.5),
        "b_forget": jax.random.uniform(ks[4], (DEPTH, FOX_HEADS), f32, 1.0, 6.0),
        "pool_w": nrm(ks[5], (DEPTH, POOL_GROUPS, POOL_GDIM, POOL_GDIM), POOL_GDIM ** -0.5),
        "pool_b": nrm(ks[6], (DEPTH, POOL_GROUPS, POOL_GDIM), 0.01),
        "pool_scale": 1.0 + nrm(ks[7], (DEPTH, POOL_WIDTH), 0.1),
        "conv_w": nrm(ks[8], (DEPTH, CONV_KSIZE, CONV_WIDTH), CONV_KSIZE ** -0.5),
        "conv_b": nrm(ks[9], (DEPTH, CONV_WIDTH), 0.01),
        "conv_ln_g": 1.0 + nrm(ks[10], (DEPTH, CONV_WIDTH), 0.02),
        "conv_ln_b": nrm(ks[11], (DEPTH, CONV_WIDTH), 0.01),
        "w_out_a": nrm(ks[12], (DEPTH, POOL_WIDTH, D), POOL_WIDTH ** -0.5),
        "w_out_b": nrm(ks[13], (DEPTH, CONV_WIDTH, D), CONV_WIDTH ** -0.5),
        "w_out_c": nrm(ks[14], (DEPTH, FOX_WIDTH, D), FOX_WIDTH ** -0.5),
        "w_o": nrm(ks[15], (DEPTH, D, D), D ** -0.5),
        "norm2_g": 1.0 + nrm(ks[16], (DEPTH, D), 0.02),
        "router_g": nrm(ks[17], (DEPTH, D, N_GROUPS), D ** -0.5),
        "router_g_b": nrm(ks[18], (DEPTH, N_GROUPS), 0.01),
        "router_e": nrm(ks[19], (DEPTH, D, N_EXPERTS), D ** -0.5),
        "router_e_b": nrm(ks[20], (DEPTH, N_EXPERTS), 0.01),
        "exp_w1": nrm(ks[21], (DEPTH, N_EXPERTS, D, EXPERT_HIDDEN), D ** -0.5),
        "exp_w3": nrm(ks[22], (DEPTH, N_EXPERTS, D, EXPERT_HIDDEN), D ** -0.5),
        "exp_w2": nrm(ks[23], (DEPTH, N_EXPERTS, EXPERT_HIDDEN, D), EXPERT_HIDDEN ** -0.5),
        "final_g": 1.0 + nrm(ks[24], (D,), 0.02),
    }

def first_block(x, meta, norm1_g, w_in, b_forget, pool_w, pool_b, pool_scale, conv_w, conv_b, conv_ln_g,
              conv_ln_b, w_out_a, w_out_b, w_out_c, w_o, norm2_g, router_g, router_g_b, router_e,
              router_e_b, exp_w1, exp_w3, exp_w2, final_g):
    B_ = x.shape[0]
    m = jnp.broadcast_to(meta.astype(x.dtype)[None], (B_, N_META, D_MODEL))
    h = jnp.concatenate([m, x], axis=1)
    for l in range(DEPTH):
        u = rms_norm(h, norm1_g[l])
        h = h + mixer_layer(u, w_in[l], b_forget[l], pool_w[l], pool_b[l], pool_scale[l], conv_w[l],
                            conv_b[l], conv_ln_g[l], conv_ln_b[l], w_out_a[l], w_out_b[l], w_out_c[l], w_o[l])
        v = rms_norm(h, norm2_g[l])
        h = h + hier_moe(v, router_g[l], router_g_b[l], router_e[l], router_e_b[l], exp_w1[l], exp_w3[l], exp_w2[l])
    return rms_norm(h[:, N_META:], final_g)


MAX_STREAM_OFFSET = 4096

D_RNN = D_MODEL
LRU_BLOCK_W = 256
LRU_BLOCKS = D_RNN // LRU_BLOCK_W
CONV_W = 4
LRU_C = 8.0

MLA_HEADS = 16
V_HEAD = D_MODEL // MLA_HEADS
QK_NOPE = 64
QK_ROPE = 32
QK_HEAD = QK_NOPE + QK_ROPE
Q_LORA = 768
KV_LORA = 256
ROPE_THETA = 10000.0

N_BRANCH_2 = 2
IN_SPLITS_2 = (D_RNN, D_RNN, Q_LORA, KV_LORA, QK_ROPE, N_BRANCH_2 * D_MODEL)
D_IN = sum(IN_SPLITS_2)

EXPERTS_PER_GROUP_2 = 8
N_EXPERTS_2 = N_GROUPS * EXPERTS_PER_GROUP_2
D_EXPERT = 256
MOE_BLOCK = 128


def rms_norm_2(x, g):
    xf = x.astype(jnp.float32)
    y = xf * lax.rsqrt(jnp.mean(xf * xf, axis=-1, keepdims=True) + EPS)
    return (y * g.astype(jnp.float32)).astype(x.dtype)

def causal_conv(x, w, b):
    y = lax.conv_general_dilated(
        x, w[:, None, :].astype(x.dtype), window_strides=(1,),
        padding=[(CONV_W - 1, 0)], dimension_numbers=('NWC', 'WIO', 'NWC'),
        feature_group_count=x.shape[-1])
    return y + b.astype(x.dtype)

def rg_lru(x, wa, ba, wx, bx, lam):
    B, S, _ = x.shape
    xb = x.reshape(B, S, LRU_BLOCKS, LRU_BLOCK_W)
    r = jax.nn.sigmoid((jnp.einsum('bshi,hij->bshj', xb, wa).reshape(B, S, D_RNN) + ba).astype(jnp.float32))
    i = jax.nn.sigmoid((jnp.einsum('bshi,hij->bshj', xb, wx).reshape(B, S, D_RNN) + bx).astype(jnp.float32))
    log_a = -LRU_C * r * jax.nn.softplus(-lam.astype(jnp.float32))
    a = jnp.exp(log_a)
    mult = jnp.sqrt(-jnp.expm1(2.0 * log_a))
    b = mult * (i * x.astype(jnp.float32))

    def combine(left, right):
        a_l, b_l = left
        a_r, b_r = right
        return a_l * a_r, a_r * b_l + b_r

    _, h = lax.associative_scan(combine, (a, b), axis=1)
    return h.astype(x.dtype)

def rope(x, pos):
    half = QK_ROPE // 2
    freq = ROPE_THETA ** (-jnp.arange(half, dtype=jnp.float32) / half)
    ang = pos.astype(jnp.float32)[:, :, None, None] * freq
    cos, sin = jnp.cos(ang), jnp.sin(ang)
    x1 = x[..., :half].astype(jnp.float32)
    x2 = x[..., half:].astype(jnp.float32)
    return jnp.concatenate([x1 * cos - x2 * sin, x1 * sin + x2 * cos], axis=-1).astype(x.dtype)

def chunk_causal_attention(q, k, v):
    B, S, H, _ = q.shape
    scale = QK_HEAD ** -0.5
    outs = []
    for blk in range(S // Q_BLOCK):
        q0 = blk * Q_BLOCK
        k_end = q0 + Q_BLOCK
        qb = q[:, q0:k_end]
        s = jnp.einsum('bqhd,bkhd->bhqk', qb, k[:, :k_end]).astype(jnp.float32) * scale
        q_chunk = (q0 + jnp.arange(Q_BLOCK)) // CHUNK
        k_chunk = jnp.arange(k_end) // CHUNK
        mask = k_chunk[None, :] <= q_chunk[:, None]
        s = jnp.where(mask, s, -jnp.inf)
        p = jax.nn.softmax(s, axis=-1).astype(v.dtype)
        outs.append(jnp.einsum('bhqk,bkhd->bqhd', p, v[:, :k_end]))
    return jnp.concatenate(outs, axis=1).reshape(B, S, H * V_HEAD)

def mla(q_c, kv_c, k_pe, pos, q_a_g, w_uq, kv_a_g, w_ukv, q_norm_g, k_norm_g):
    B, S, _ = q_c.shape
    q = (rms_norm_2(q_c, q_a_g) @ w_uq).reshape(B, S, MLA_HEADS, QK_HEAD)
    kv = (rms_norm_2(kv_c, kv_a_g) @ w_ukv).reshape(B, S, MLA_HEADS, QK_NOPE + V_HEAD)
    k_nope, v = kv[..., :QK_NOPE], kv[..., QK_NOPE:]
    k_pe_h = jnp.broadcast_to(k_pe[:, :, None, :], (B, S, MLA_HEADS, QK_ROPE))
    k = jnp.concatenate([k_nope, k_pe_h], axis=-1)
    q = rms_norm_2(q, q_norm_g)
    k = rms_norm_2(k, k_norm_g)
    q = jnp.concatenate([q[..., :QK_NOPE], rope(q[..., QK_NOPE:], pos)], axis=-1)
    k = jnp.concatenate([k[..., :QK_NOPE], rope(k[..., QK_NOPE:], pos)], axis=-1)
    return chunk_causal_attention(q, k, v)

def hier_moe_2(x, wg, bg, we, be, w_gate, w_up, w_down):
    B, S, D = x.shape
    T = B * S
    xt = x.reshape(T, D)
    xf = xt.astype(jnp.float32)
    g_logits = xf @ wg.astype(jnp.float32) + bg.astype(jnp.float32)
    g_prob = jax.nn.softmax(g_logits, axis=-1)
    grp = jnp.argmax(g_logits, axis=-1)
    p_grp = jnp.take_along_axis(g_prob, grp[:, None], axis=1)
    e_logits = (xf @ we.astype(jnp.float32) + be.astype(jnp.float32)).reshape(T, N_GROUPS, EXPERTS_PER_GROUP_2)
    e_in = jnp.take_along_axis(e_logits, grp[:, None, None], axis=1)[:, 0]
    top_v, top_i = lax.top_k(e_in, TOP_K)
    combine = p_grp * jax.nn.softmax(top_v, axis=-1)
    expert = grp[:, None] * EXPERTS_PER_GROUP_2 + top_i

    A = T * TOP_K
    e_flat = expert.reshape(A)
    tok_flat = jnp.arange(A, dtype=jnp.int32) // TOP_K
    c_flat = combine.reshape(A)
    order = jnp.argsort(e_flat)
    e_sorted = e_flat[order]
    counts = jnp.bincount(e_flat, length=N_EXPERTS_2)
    padded = (counts + MOE_BLOCK - 1) // MOE_BLOCK * MOE_BLOCK
    starts = jnp.cumsum(counts) - counts
    p_ends = jnp.cumsum(padded)
    p_starts = p_ends - padded
    dest = p_starts[e_sorted] + (jnp.arange(A) - starts[e_sorted])
    P = A + N_EXPERTS_2 * MOE_BLOCK
    n_blk = P // MOE_BLOCK
    tok_pad = jnp.full((P,), T, jnp.int32).at[dest].set(tok_flat[order])
    c_pad = jnp.zeros((P,), jnp.float32).at[dest].set(c_flat[order])
    blk_expert = jnp.clip(jnp.searchsorted(p_ends, jnp.arange(n_blk) * MOE_BLOCK, side='right'), 0, N_EXPERTS_2 - 1)
    x_pad = jnp.concatenate([xt, jnp.zeros((1, D), xt.dtype)], axis=0)[tok_pad].reshape(n_blk, MOE_BLOCK, D)

    def expert_block(args):
        xb, e = args
        hb = jax.nn.silu(xb @ w_gate[e]) * (xb @ w_up[e])
        return hb @ w_down[e]

    y = lax.map(expert_block, (x_pad, blk_expert)).reshape(P, D).astype(jnp.float32) * c_pad[:, None]
    out = jax.ops.segment_sum(y, tok_pad, num_segments=T + 1)[:T]
    return out.astype(x.dtype).reshape(B, S, D)

def second_inputs(seed: int = 0) -> dict:
    key = jax.random.key(seed)
    ks = jax.random.split(key, 28)
    L = DEPTH

    def nrm(k, shape, s):
        return jax.random.normal(k, shape, jnp.float32) * s

    def gain(k, n):
        return 1.0 + 0.05 * jax.random.normal(k, (L, n), jnp.float32)

    x = jax.random.normal(ks[0], (BATCH, SEQ, D_MODEL), jnp.float32)
    offset = jax.random.randint(ks[1], (BATCH, 1), 0, MAX_STREAM_OFFSET, dtype=jnp.int32)
    positions = offset + jnp.arange(SEQ, dtype=jnp.int32)[None, :]
    a0 = jax.random.uniform(ks[2], (L, D_RNN), jnp.float32, 0.9, 0.999)
    s0 = a0 ** (1.0 / LRU_C)
    lru_lambda = jnp.log(s0) - jnp.log1p(-s0)
    return {
        "x": x,
        "positions": positions,
        "norm_mix_g": gain(ks[3], D_MODEL),
        "w_in": nrm(ks[4], (L, D_MODEL, D_IN), D_MODEL ** -0.5),
        "conv_w": nrm(ks[5], (L, CONV_W, D_RNN), CONV_W ** -0.5),
        "conv_b": nrm(ks[6], (L, D_RNN), 0.02),
        "lru_wa": nrm(ks[7], (L, LRU_BLOCKS, LRU_BLOCK_W, LRU_BLOCK_W), LRU_BLOCK_W ** -0.5),
        "lru_ba": nrm(ks[8], (L, D_RNN), 0.02),
        "lru_wx": nrm(ks[9], (L, LRU_BLOCKS, LRU_BLOCK_W, LRU_BLOCK_W), LRU_BLOCK_W ** -0.5),
        "lru_bx": nrm(ks[10], (L, D_RNN), 0.02),
        "lru_lambda": lru_lambda,
        "q_a_g": gain(ks[11], Q_LORA),
        "w_uq": nrm(ks[12], (L, Q_LORA, MLA_HEADS * QK_HEAD), Q_LORA ** -0.5),
        "kv_a_g": gain(ks[13], KV_LORA),
        "w_ukv": nrm(ks[14], (L, KV_LORA, MLA_HEADS * (QK_NOPE + V_HEAD)), KV_LORA ** -0.5),
        "q_norm_g": gain(ks[15], QK_HEAD),
        "k_norm_g": gain(ks[16], QK_HEAD),
        "w_out": nrm(ks[17], (L, D_MODEL, D_MODEL), D_MODEL ** -0.5),
        "norm_ffn_g": gain(ks[18], D_MODEL),
        "router_group_w": nrm(ks[19], (L, D_MODEL, N_GROUPS), D_MODEL ** -0.5),
        "router_group_b": nrm(ks[20], (L, N_GROUPS), 0.01),
        "router_expert_w": nrm(ks[21], (L, D_MODEL, N_EXPERTS_2), D_MODEL ** -0.5),
        "router_expert_b": nrm(ks[22], (L, N_EXPERTS_2), 0.01),
        "w_gate": nrm(ks[23], (L, N_EXPERTS_2, D_MODEL, D_EXPERT), D_MODEL ** -0.5),
        "w_up": nrm(ks[24], (L, N_EXPERTS_2, D_MODEL, D_EXPERT), D_MODEL ** -0.5),
        "w_down": nrm(ks[25], (L, N_EXPERTS_2, D_EXPERT, D_MODEL), D_EXPERT ** -0.5),
    }

def second_block(x, positions, norm_mix_g, w_in, conv_w, conv_b, lru_wa, lru_ba, lru_wx, lru_bx,
              lru_lambda, q_a_g, w_uq, kv_a_g, w_ukv, q_norm_g, k_norm_g, w_out, norm_ffn_g,
              router_group_w, router_group_b, router_expert_w, router_expert_b,
              w_gate, w_up, w_down):
    B, S, _ = x.shape
    split_points = np.cumsum(IN_SPLITS_2)[:-1].tolist()
    h = x
    for l in range(DEPTH):
        u = rms_norm_2(h, norm_mix_g[l])
        proj = u @ w_in[l]
        x_rnn, g_rnn, q_c, kv_c, k_pe, gate_logits = jnp.split(proj, split_points, axis=-1)
        xa = causal_conv(x_rnn, conv_w[l], conv_b[l])
        ya = rg_lru(xa, lru_wa[l], lru_ba[l], lru_wx[l], lru_bx[l], lru_lambda[l]) * jax.nn.gelu(g_rnn)
        yb = mla(q_c, kv_c, k_pe, positions, q_a_g[l], w_uq[l], kv_a_g[l], w_ukv[l], q_norm_g[l], k_norm_g[l])
        gates = jax.nn.sigmoid(gate_logits.astype(jnp.float32)).reshape(B, S, N_BRANCH_2, D_MODEL)
        merged = gates[:, :, 0] * ya.astype(jnp.float32) + gates[:, :, 1] * yb.astype(jnp.float32)
        h = h + merged.astype(h.dtype) @ w_out[l]
        h = h + hier_moe_2(rms_norm_2(h, norm_ffn_g[l]), router_group_w[l], router_group_b[l],
                         router_expert_w[l], router_expert_b[l], w_gate[l], w_up[l], w_down[l])
    return h


def setup_inputs(seed=0):
    out = dict(first_inputs(seed))
    for name, value in second_inputs(seed + 1).items():
        if name != "x":
            out[name + "_2"] = value
    return out


def reference(
    x, meta, norm1_g, w_in, b_forget, pool_w, pool_b, pool_scale, conv_w, conv_b, conv_ln_g,
    conv_ln_b, w_out_a, w_out_b, w_out_c, w_o, norm2_g, router_g, router_g_b, router_e,
    router_e_b, exp_w1, exp_w3, exp_w2, final_g, positions_2, norm_mix_g_2, w_in_2, conv_w_2,
    conv_b_2, lru_wa_2, lru_ba_2, lru_wx_2, lru_bx_2, lru_lambda_2, q_a_g_2, w_uq_2, kv_a_g_2,
    w_ukv_2, q_norm_g_2, k_norm_g_2, w_out_2, norm_ffn_g_2, router_group_w_2, router_group_b_2,
    router_expert_w_2, router_expert_b_2, w_gate_2, w_up_2, w_down_2,
):
    x = first_block(
        x, meta, norm1_g, w_in, b_forget, pool_w, pool_b, pool_scale, conv_w, conv_b, conv_ln_g,
        conv_ln_b, w_out_a, w_out_b, w_out_c, w_o, norm2_g, router_g, router_g_b, router_e,
        router_e_b, exp_w1, exp_w3, exp_w2, final_g,
    )
    return second_block(
        x, positions_2, norm_mix_g_2, w_in_2, conv_w_2, conv_b_2, lru_wa_2, lru_ba_2, lru_wx_2,
        lru_bx_2, lru_lambda_2, q_a_g_2, w_uq_2, kv_a_g_2, w_ukv_2, q_norm_g_2, k_norm_g_2,
        w_out_2, norm_ffn_g_2, router_group_w_2, router_group_b_2, router_expert_w_2,
        router_expert_b_2, w_gate_2, w_up_2, w_down_2,
    )


_drawn_inputs = setup_inputs


def setup_inputs(seed=0):
    import zlib

    import numpy as np

    out = dict(_drawn_inputs(seed))
    spreads = {}
    factors = {'router_g_b': 3.791,
     'router_e_b': 6.258,
     'lru_ba_2': 54.642,
     'lru_bx_2': 33.655,
     'q_a_g_2': 4.033,
     'kv_a_g_2': 3.708,
     'q_norm_g_2': 4.871,
     'k_norm_g_2': 4.809,
     'router_group_b_2': 17.303,
     'router_expert_b_2': 13.926}
    for name, (base, spread) in spreads.items():
        noise = np.random.default_rng([zlib.crc32(name.encode()), seed]).standard_normal(out[name].shape)
        drawn = base * np.exp(spread * noise) if base else spread * noise
        out[name] = __import__('jax').numpy.asarray(drawn.astype(out[name].dtype))
    for name, factor in factors.items():
        out[name] = (out[name] * factor).astype(out[name].dtype)
    return out
```

```python
from contextlib import ExitStack, contextmanager

import concourse.bass as bass
from concourse import mybir

F32 = mybir.dt.float32
F32R = mybir.dt.float32r
BF16 = mybir.dt.bfloat16
I32 = mybir.dt.int32
U32 = mybir.dt.uint32
ALU = mybir.AluOpType
ACT = mybir.ActivationFunctionType
AX = mybir.AxisListType

P = 128
D = 1024
KD = D // P
S = 1024
NT = S // P
META = 16
BANK = 512
HALVES = [(0, BANK), (BANK, S)]
EPS = 1e-6
MASKED = -1e30
ROUND = 12582912.0

POOL_W, CONV_W1, TAPS = 256, 256, 31
C_Q1, C_K1, C_V1, C_FG, C_G1 = 768, 1280, 1792, 2304, 2312
H1, DH = 8, 64
T1 = S + META
PIECES1 = [(0, 352), (352, 704), (704, T1)]
NE1 = 16
C_XR, C_GR, C_QC, C_KPE, C_GT = 0, 1024, 2048, 3072, 3104
QL, KVL, ROPE = 768, 256, 32
H2, QKN, QKH, VH = 16, 64, 96, 64
LRU_C = 8.0
NE2 = 32
NG = 4
HID = 256
ONE_ROW = 96


class Steps:

    def __init__(self, eng, sem):
        self.eng, self.sem, self.total, self.base, self.n = eng, sem, 0, 0, 0

    def __call__(self, ins):
        ins.then_inc(self.sem, 1)
        self.n += 1
        self.eng.wait_ge(self.sem, self.base + self.n)

    def enter(self, i, per):
        self.base, self.n = i * per + self.total, 0

    def leave(self, passes, per):
        assert self.n == per, (self.n, per)
        self.total += passes * per
        self.base, self.n = self.total, 0


class Stage:

    def __init__(self, nc, name, ctx):
        self.nc, self.name, self.ctx, self.sems = nc, name, ctx, []

    def sb(self, name, shape, dt=F32):
        return self.ctx.enter_context(self.nc.sbuf_tensor(f"{self.name}_{name}", shape, dt))

    def ps(self, name, shape=(P, BANK), dt=F32):
        return self.ctx.enter_context(self.nc.psum_tensor(f"{self.name}_{name}", list(shape), dt))

    def banks(self, name, n):
        return [self.ps(f"{name}{i}") for i in range(n)]

    def sem(self, name):
        s = self.nc.alloc_semaphore(f"{self.name}_{name}")
        self.sems.append(s)
        return s

    def sem_n(self, name, n=2):
        return [self.sem(f"{name}{i}") for i in range(n)]


@contextmanager
def stage(nc, name):
    with ExitStack() as ctx:
        st = Stage(nc, name, ctx)
        yield st
    if st.sems:
        nc.clear_and_free_semaphores(st.sems)
        nc.all_engine_barrier()


def products(pe, out, pairs):
    for n, (lhsT, rhs) in enumerate(pairs):
        last = pe.matmul(out, lhsT, rhs, start=(n == 0), stop=(n == len(pairs) - 1))
    return last


def row_of(ap, n):
    return ap.rearrange("(c p) -> c p", c=n)


def chunked(ap):
    return ap.rearrange("(c p) n -> p c n", p=P)



def constants(nc, st0, rows):
    ident = st0.sb("ident", [P, P])
    identb = st0.sb("identb", [P, P], BF16)
    ones = st0.sb("ones", [P, P])
    zeros = st0.sb("zeros", [P, 1])
    causal_qk = st0.sb("causal_qk", [P, P], BF16)
    causal_kq = st0.sb("causal_kq", [P, P], BF16)
    chunk_qk = st0.sb("chunk_qk", [P, P], BF16)
    chunk_kq = st0.sb("chunk_kq", [P, P], BF16)
    groups = [[], []]
    used = [0, 0]
    where = {}
    for name, ap, n, w in rows:
        g = 0 if used[0] + n <= P else 1
        groups[g].append((used[g], n, w, ap))
        where[name] = (g, used[g], n)
        used[g] += n
        assert used[g] <= P
    cols = [st0.sb(f"cols{g}", [P, P]) for g in range(2)]
    with stage(nc, "const") as st:
        stack = [st.sb(f"stack{g}", [P, P]) for g in range(2)]
        turned = [st.ps(f"turned{g}", (P, P)) for g in range(2)]
        s_zero = st.sem("zeroed")
        s_rows = st.sem("rows_loaded")
        s_one = st.sem("ident_ready")
        s_turn = st.sem("turned")
        s_cols = st.sem("cols_ready")
        with nc.Block() as block:
            @block.vector
            def _(dve):
                for g in range(2):
                    dve.memset(stack[g][:], 0.0).then_inc(s_zero, 1)
                dve.memset(ones[:], 1.0)
                dve.memset(zeros[:], 0.0)
                dve.memset(chunk_qk[:], 0.0).then_inc(s_cols, 1)
                dve.memset(chunk_kq[:], 0.0).then_inc(s_cols, 1)
                dve.wait_ge(s_cols, 2)
                dve.memset(chunk_qk[0:64, 64:P], MASKED)
                dve.memset(chunk_kq[64:P, 0:64], MASKED)
                for g in range(2):
                    dve.wait_ge(s_turn, g + 1)
                    dve.tensor_copy(cols[g][:], turned[g][:]).then_inc(s_cols, 1)
                dve.wait_ge(s_cols, 4)
                g, at, _ = where["qk_g"]
                qk = cols[g][:, at:at + 2]
                dve.memset(qk[QKN:QKH, :], 1.0).then_inc(s_cols, 1)
                dve.wait_ge(s_cols, 5)
                dve.tensor_scalar(qk[:, 0:1], qk[:, 0:1], float(QKH) ** -0.5, None, ALU.mult)

            @block.sync
            def _(sp):
                sp.wait_ge(s_zero, 2)
                for g in range(2):
                    for at, n, w, ap in groups[g]:
                        sp.dma_start(stack[g][at:at + n, 0:w], ap).then_inc(s_rows, 16)

            @block.gpsimd
            def _(pool):
                own = Steps(pool, st.sem("pool_step"))
                own(pool.memset(ident[:], 0.0))
                pool.affine_select(out=ident[:], in_=ident[:], compare_op=ALU.not_equal, fill=1.0,
                                   base=0, pattern=[[-1, P]], channel_multiplier=1).then_inc(s_one, 1)
                pool.wait_ge(s_one, 1)
                pool.tensor_copy(identb[:], ident[:])
                own(pool.memset(causal_qk[:], 0.0))
                pool.affine_select(out=causal_qk[:], in_=causal_qk[:], compare_op=ALU.is_ge,
                                   fill=MASKED, base=0, pattern=[[-1, P]], channel_multiplier=1)
                own(pool.memset(causal_kq[:], 0.0))
                pool.affine_select(out=causal_kq[:], in_=causal_kq[:], compare_op=ALU.is_ge,
                                   fill=MASKED, base=0, pattern=[[1, P]], channel_multiplier=-1)

            @block.tensor
            def _(pe):
                pe.wait_ge(s_one, 1)
                pe.wait_ge(s_rows, 16 * len(rows))
                for g in range(2):
                    pe.transpose(turned[g][:], stack[g][:], ident[:]).then_inc(s_turn, 1)
    out = {}
    for name, (g, at, n) in where.items():
        out[name] = cols[g][:, at:at + n]
    g, at, _ = where["qk_g"]
    out["qk_g"] = cols[g][:, at:at + 2]
    g, at, n = where["latent_g"]
    assert where["kv_a_g"][:2] == (g, at + n) and where["k_g"][:2] == (where["qk_g"][0], where["qk_g"][1] + 1)
    out["latent_g"] = cols[g][:, at:at + (QL + KVL) // P]
    return dict(ident=ident, identb=identb, ones=ones, zeros=zeros,
                causal=(causal_qk, causal_kq), chunk=(chunk_qk, chunk_kq)), out



def norm_to_features(nc, cst, name, load, gain, uT, first):
    n = len(load)
    with stage(nc, name) as st:
        x = st.sb("x", [P, n, D])
        junk = st.sb("squares", [P, D])
        ss = st.sb("sums", [P, n])
        ms = st.sb("mean", [P, n])
        root = st.sb("root", [P, n])
        inv = st.sb("inverse", [P, n])
        turn = st.banks("turn", 4)
        s_x = st.sem_n("x_loaded", n)
        s_sum = st.sem("sums_ready")
        s_mean = st.sem("mean_ready")
        s_root = st.sem("root_ready")
        s_inv = st.sem("inverse_ready")
        s_norm = st.sem("tile_scaled")
        s_turn = st.sem("turned")
        s_out = st.sem_n("bank_free")
        s_clear = st.sem("cleared")
        with nc.Block() as block:
            @block.sync
            def _(sp):
                for t, (ap, rows) in enumerate(load):
                    sp.dma_start(x[0:rows, t, :], ap).then_inc(s_x[t], 16)

            def evict(eng, half):
                for t, (_, rows) in enumerate(load):
                    eng.wait_ge(s_turn, 2 * t + half + 1)
                    at = first + sum(r for _, r in load[:t])
                    for c in range(4):
                        f = 4 * half + c
                        src = turn[2 * (t % 2) + half][:, c * P:c * P + rows]
                        dst = uT[:, f, at:at + rows]
                        if half:
                            last = eng.activation(dst, src, ACT.Copy, scale=gain[:, f:f + 1])
                        else:
                            last = eng.tensor_scalar(dst, src, gain[:, f:f + 1], None, ALU.mult)
                    last.then_inc(s_out[half], 1)

            @block.scalar
            def _(act):
                act.wait_ge(s_clear, 1)
                for t, (_, rows) in enumerate(load):
                    act.wait_ge(s_x[t], 16)
                    if t:
                        act.wait_ge(s_sum, t)
                    act.activation(junk[0:rows, :], x[0:rows, t, :], ACT.Square,
                                   accum_out=ss[0:rows, t:t + 1]).then_inc(s_sum, 1)
                act.wait_ge(s_mean, 1)
                act.activation(root[:], ms[:], ACT.Sqrt).then_inc(s_root, 1)
                evict(act, 1)

            @block.vector
            def _(dve):
                dve.memset(ss[:], 0.0).then_inc(s_clear, 1)
                dve.wait_ge(s_sum, n)
                dve.tensor_scalar(ms[:], ss[:], 1.0 / D, EPS, ALU.mult, ALU.add).then_inc(s_mean, 1)
                dve.wait_ge(s_root, 1)
                dve.reciprocal(inv[:], root[:]).then_inc(s_inv, 1)
                dve.wait_ge(s_inv, 1)
                for t, (_, rows) in enumerate(load):
                    dve.tensor_scalar(x[0:rows, t, :], x[0:rows, t, :], inv[0:rows, t:t + 1], None,
                                      ALU.mult).then_inc(s_norm, 1)
                evict(dve, 0)

            @block.tensor
            def _(pe):
                for t, (_, rows) in enumerate(load):
                    pe.wait_ge(s_norm, t + 1)
                    for half in range(2):
                        if t >= 2:
                            pe.wait_ge(s_out[half], t - 1)
                        for c in range(4):
                            f = 4 * half + c
                            last = pe.transpose(turn[2 * (t % 2) + half][:, c * P:c * P + rows],
                                                x[0:rows, t, f * P:(f + 1) * P],
                                                cst["ident"][0:rows, 0:rows])
                        last.then_inc(s_turn, 1)


def project_features(nc, name, w, c0, chunks, uT, pieces, out):
    src = chunked(w)
    npc = len(pieces)
    share = [(npc + 1) // 2, npc // 2]
    with stage(nc, name) as st:
        wb = [st.sb(f"w{p}", [P, KD, P]) for p in range(2)]
        acc = [st.banks(f"acc{p}_", npc) for p in range(2)]
        s_w = st.sem_n("w_loaded")
        s_acc = st.sem_n("acc_ready")
        s_free = [st.sem_n("free_by_dve"), st.sem_n("free_by_act")]
        with nc.Block() as block:
            @block.sync
            def _(sp):
                with sp.Fori(0, chunks // 2) as i:
                    for p in range(2):
                        sp.wait_ge(s_acc[p], npc * i + 1)
                        sp.dma_start(wb[p][:], src[:, :, bass.ds(c0 + P * (2 * i + p), P)]).then_inc(s_w[p], 16)

            @block.tensor
            def _(pe):
                for p in range(2):
                    pe.sem_inc(s_acc[p], 1)
                with pe.Fori(0, chunks // 2) as i:
                    for p in range(2):
                        pe.wait_ge(s_w[p], 16 * i + 16)
                        for n, (a, b) in enumerate(pieces):
                            pe.wait_ge(s_free[n % 2][p], share[n % 2] * i + n // 2 + 1)
                            products(pe, acc[p][n][:, 0:b - a],
                                     [(wb[p][:, k, :], uT[:, k, a:b]) for k in range(KD)]).then_inc(s_acc[p], 1)

            def copy_out(eng, e):
                for p in range(2):
                    eng.sem_inc(s_free[e][p], share[e])
                with eng.Fori(0, chunks // 2) as i:
                    for p in range(2):
                        for n in range(e, npc, 2):
                            a, b = pieces[n]
                            eng.wait_ge(s_acc[p], npc * i + n + 2)
                            dst = out[:, bass.ds(2 * i + p, 1), a:b].rearrange("p a t -> p (a t)")
                            if e:
                                ins = eng.copy(dst, acc[p][n][:, 0:b - a])
                            else:
                                ins = eng.tensor_copy(dst, acc[p][n][:, 0:b - a])
                            ins.then_inc(s_free[e][p], 1)

            @block.vector
            def _(dve):
                copy_out(dve, 0)

            @block.scalar
            def _(act):
                copy_out(act, 1)


def project_tokens(nc, name, w, c0, width, uT, tiles, out):
    with stage(nc, name) as st:
        wb = st.sb("w", [P, KD, width])
        acc = st.banks("acc", 4)
        s_w = st.sem("w_loaded")
        s_acc = st.sem("acc_ready")
        s_free = st.sem("acc_free")
        with nc.Block() as block:
            @block.sync
            def _(sp):
                with nc.allow_non_contiguous_dma(reason="narrow weight columns"):
                    sp.dma_start(wb[:], chunked(w)[:, :, c0:c0 + width]).then_inc(s_w, 16)

            @block.tensor
            def _(pe):
                pe.wait_ge(s_w, 16)
                for t, (at, rows) in enumerate(tiles):
                    if t >= 4:
                        pe.wait_ge(s_free, t - 3)
                    products(pe, acc[t % 4][0:rows, 0:width],
                             [(uT[:, k, at:at + rows], wb[:, k, :]) for k in range(KD)]).then_inc(s_acc, 1)

            @block.vector
            def _(dve):
                for t, (at, rows) in enumerate(tiles):
                    dve.wait_ge(s_acc, t + 1)
                    dve.tensor_copy(out[0:rows, t, :], acc[t % 4][0:rows, 0:width]).then_inc(s_free, 1)



def forget_sums(nc, w_in, b_forget, uT, neg_f):
    with stage(nc, "forget") as st:
        wb = st.sb("w", [P, KD, H1])
        bias = st.sb("bias", [H1, 1])
        z, e, neg, one = (st.sb(n, [H1, T1]) for n in ("z", "e", "neg", "one"))
        acc = st.banks("acc", 3)
        s_in = st.sem("loaded")
        s_acc = st.sem("acc_ready")
        s_e = st.sem("exponent_ready")
        s_ln = st.sem("log_ready")
        s_neg = st.sem("sums_ready")
        s_out = st.sem("stored")
        with nc.Block() as block:
            @block.sync
            def _(sp):
                with nc.allow_non_contiguous_dma(reason="eight weight columns"):
                    sp.dma_start(wb[:], chunked(w_in)[:, :, C_FG:C_FG + H1]).then_inc(s_in, 16)
                    sp.dma_start(bias[:], b_forget.rearrange("a h -> h a")).then_inc(s_in, 16)
                sp.wait_ge(s_neg, 1)
                sp.dma_start(neg_f, neg[:]).then_inc(s_out, 16)
                sp.wait_ge(s_out, 16)

            @block.tensor
            def _(pe):
                pe.wait_ge(s_in, 32)
                for n, (a, b) in enumerate(PIECES1):
                    products(pe, acc[n][0:H1, 0:b - a],
                             [(wb[:, k, :], uT[:, k, a:b]) for k in range(KD)]).then_inc(s_acc, 1)

            @block.vector
            def _(dve):
                own = Steps(dve, st.sem("dve_step"))
                dve.memset(one[:], 1.0)
                dve.wait_ge(s_in, 32)
                for n, (a, b) in enumerate(PIECES1):
                    dve.wait_ge(s_acc, n + 1)
                    own(dve.tensor_scalar(z[:, a:b], acc[n][0:H1, 0:b - a], bias[:], None, ALU.add))
                own(dve.tensor_scalar(neg[:], z[:], -1.0, None, ALU.mult))
                dve.tensor_tensor(e[:], z[:], neg[:], ALU.min).then_inc(s_e, 1)
                dve.wait_ge(s_ln, 2)
                own(dve.tensor_scalar(z[:], z[:], 0.0, None, ALU.min))
                own(dve.tensor_tensor(z[:], e[:], z[:], ALU.subtract))
                dve.tensor_tensor_scan(neg[:], one[:], z[:], 0.0, ALU.mult, ALU.add).then_inc(s_neg, 1)

            @block.scalar
            def _(act):
                act.wait_ge(s_e, 1)
                act.activation(e[:], e[:], ACT.Exp).then_inc(s_ln, 1)
                act.wait_ge(s_ln, 1)
                act.activation(e[:], e[:], ACT.Ln, bias=1.0).then_inc(s_ln, 1)


def pool_and_conv(nc, cst, col, pool_w, pT):
    NCH = 2
    WINDOWS = (2, 4, 8, 16)
    GD = 64
    PAD = TAPS - 1 - META
    with stage(nc, "mixers") as st:
        glu = st.sb("glu", [P, NCH, PAD + T1])
        y = st.sb("y", [P, NCH, S])
        s2, s4 = st.sb("sum2", [P, T1]), st.sb("sum4", [P, T1])
        diff = st.sb("diff", [P, NCH, S])
        pw = st.sb("pool_w", [P, NCH, P])
        mean_w = st.sb("mean_w", [P, P])
        sq = st.sb("squares", [P, NCH, S])
        rt = st.sb("root", [P, S])
        ps = [st.banks(f"ps{c}_", 2) for c in range(4)]
        s_clear = st.sem("cleared")
        s_pw = st.sem("pool_w_loaded")
        s_sig = st.sem("gate_ready")
        s_diff = st.sem("diff_ready")
        s_pool = st.sem("pool_ready")
        s_y = st.sem("conv_ready")
        s_mean = st.sem("mean_ready")
        s_cent = st.sem("centred")
        s_sq = st.sem("squared")
        s_var = st.sem("variance_ready")
        s_root = st.sem("root_ready")
        s_norm = st.sem("normed")
        with nc.Block() as block:
            @block.sync
            def _(sp):
                sp.wait_ge(s_clear, 1)
                for g in range(4):
                    r = GD * (g % 2)
                    sp.dma_start(pw[r:r + GD, g // 2, r:r + GD], pool_w[g]).then_inc(s_pw, 16)

            @block.scalar
            def _(act):
                for c in range(NCH):
                    act.activation(pT[:, 4 + c, :], pT[:, 4 + c, :], ACT.Sigmoid).then_inc(s_sig, 1)
                for c in range(4):
                    act.mul(pT[:, 6 + c, :], pT[:, 6 + c, :], float(DH) ** -0.5)
                for c in range(NCH):
                    for h, (a, b) in enumerate(HALVES):
                        act.wait_ge(s_cent, 2 * c + h + 1)
                        act.activation(sq[:, c, a:b], y[:, c, a:b], ACT.Square).then_inc(s_sq, 1)
                for h, (a, b) in enumerate(HALVES):
                    act.wait_ge(s_var, 3 * h + 2)
                    act.activation(rt[:, a:b], rt[:, a:b], ACT.Sqrt).then_inc(s_root, 1)
                for c in range(NCH):
                    act.wait_ge(s_norm, c + 1)
                    act.activation(pT[:, 2 + c, META:T1], y[:, c, :], ACT.Silu,
                                   bias=col["conv_ln_b"][:, c:c + 1], scale=col["conv_ln_g"][:, c:c + 1])

            @block.vector
            def _(dve):
                own = Steps(dve, st.sem("dve_step"))
                dve.memset(pw[:], 0.0).then_inc(s_clear, 1)
                dve.memset(mean_w[:], 1.0 / CONV_W1).then_inc(s_clear, 1)
                own(dve.memset(glu[:, :, 0:PAD], 0.0))
                for c in range(NCH):
                    x = pT[:, c, :]
                    own(dve.tensor_tensor(s2[:, 1:T1], x[:, 1:T1], x[:, 0:T1 - 1], ALU.add))
                    own(dve.tensor_tensor(s4[:, 3:T1], s2[:, 3:T1], s2[:, 1:T1 - 2], ALU.add))
                    if c:
                        own(dve.tensor_tensor(s2[:, 7:T1], s4[:, 7:T1], s4[:, 3:T1 - 4], ALU.add))
                        own(dve.tensor_tensor(s4[:, 15:T1], s2[:, 15:T1], s2[:, 7:T1 - 8], ALU.add))
                    for half, s in enumerate((s2, s4)):
                        r = slice(GD * half, GD * half + GD)
                        last = dve.scalar_tensor_tensor(
                            out=diff[r, c, :], in0=s[r, META:T1], scalar=1.0 / WINDOWS[2 * c + half],
                            in1=x[r, META:T1], op0=ALU.mult, op1=ALU.subtract)
                        last.then_inc(s_diff, 1)
                    dve.wait_ge(s_diff, 2 * c + 2)
                for c in range(NCH):
                    dve.wait_ge(s_sig, c + 1)
                    own(dve.tensor_tensor(glu[:, c, PAD:], pT[:, 2 + c, :], pT[:, 4 + c, :], ALU.mult))
                for c in range(NCH):
                    for h, (a, b) in enumerate(HALVES):
                        dve.wait_ge(s_pool, 2 * c + h + 1)
                        dve.tensor_scalar(pT[:, c, META + a:META + b], ps[c][h][:], col["pool_b"][:, c:c + 1],
                                          col["pool_scale"][:, c:c + 1], ALU.add, ALU.mult)
                for j in range(TAPS):
                    for c in range(NCH):
                        w = col["conv_w"][:, NCH * j + c:NCH * j + c + 1]
                        x = glu[:, c, j:j + S]
                        if j == 0:
                            ins = dve.tensor_scalar(y[:, c, :], x, w, col["conv_b"][:, c:c + 1], ALU.mult, ALU.add)
                        else:
                            dve.wait_ge(s_y, NCH * (j - 1) + c + 1)
                            ins = dve.scalar_tensor_tensor(out=y[:, c, :], in0=x, scalar=w, in1=y[:, c, :],
                                                           op0=ALU.mult, op1=ALU.add)
                        ins.then_inc(s_y, 1)
                dve.wait_ge(s_mean, 2)
                for c in range(NCH):
                    for h, (a, b) in enumerate(HALVES):
                        dve.tensor_tensor(y[:, c, a:b], y[:, c, a:b], ps[2][h][:], ALU.subtract).then_inc(s_cent, 1)
                for h, (a, b) in enumerate(HALVES):
                    dve.wait_ge(s_var, 3 * h + 1)
                    dve.tensor_scalar(rt[:, a:b], ps[3][h][:], EPS, None, ALU.add).then_inc(s_var, 1)
                    dve.wait_ge(s_root, h + 1)
                    dve.reciprocal(rt[:, a:b], rt[:, a:b]).then_inc(s_var, 1)
                dve.wait_ge(s_var, 6)
                for c in range(NCH):
                    dve.tensor_tensor(y[:, c, :], y[:, c, :], rt[:], ALU.mult).then_inc(s_norm, 1)

            @block.tensor
            def _(pe):
                pe.wait_ge(s_pw, 64)
                for c in range(NCH):
                    pe.wait_ge(s_diff, 2 * c + 2)
                    for h, (a, b) in enumerate(HALVES):
                        pe.matmul(ps[c][h][:], pw[:, c, :], diff[:, c, a:b], start=True, stop=True).then_inc(s_pool, 1)
                pe.wait_ge(s_clear, 2)
                pe.wait_ge(s_y, NCH * TAPS)
                for h, (a, b) in enumerate(HALVES):
                    products(pe, ps[2][h][:], [(mean_w[:], y[:, c, a:b]) for c in range(NCH)]).then_inc(s_mean, 1)
                for h, (a, b) in enumerate(HALVES):
                    pe.wait_ge(s_sq, NCH + h + 1)
                    if h:
                        pe.wait_ge(s_var, 3)
                    products(pe, ps[3][h][:], [(mean_w[:], sq[:, c, a:b]) for c in range(NCH)]).then_inc(s_var, 1)



def attention(nc, cst, name, heads, off, dq, masks, load_head, loads, v, oT, bias_row):
    mask_qk, mask_kq = masks
    T = S + off
    NK = -(-T // P)
    k_max = dq + bias_row
    k_all = ONE_ROW + 1
    cuts = [0] + [c for c in (off + P * (BANK // P - (1 if off else 0)),
                              off + P * (2 * (BANK // P) - (1 if off else 0))) if c < T] + [T]
    maxima = []
    for i in range(NT):
        end = off + P * (i + 1)
        maxima += [(i, n, a, min(b, end)) for n, (a, b) in enumerate(zip(cuts, cuts[1:])) if a < end]
    units = []
    for n, (a, b) in enumerate(HALVES):
        for t in range(NK):
            d0 = P * t - off
            if d0 < b:
                units.append((n, t, max(a, d0), (max(a, d0), min(b, d0 + P)) if d0 + P > a else None))
    NM, NU = len(maxima), len(units)
    NPC = len(cuts) - 1
    R_S, R_P = 2, 4
    PER_UNIT, FIRST = 2, 3
    TURN_AT = FIRST + -(-NM // PER_UNIT) + 1
    assert NM % R_S == 0 and NU % R_S == 0 and 2 * NU % R_P == 0 and TURN_AT < NU
    with stage(nc, name) as st:
        raw = [st.sb("q", [k_all, S]), st.sb("k", [k_all, T])]
        hi = [[st.sb(f"{n}_hi{p}", [k_all, w], F32R) for p in range(2)] for n, w in (("q", S), ("k", T))]
        lo = [[st.sb(f"{n}_lo{p}", [k_all, w], F32R) for p in range(2)] for n, w in (("q", S), ("k", T))]
        v_aug = [st.sb(f"v{p}", [P, NK, P]) for p in range(2)]
        probs = [st.sb(f"probs{r}", [P, BANK]) for r in range(R_P)]
        pm = st.sb("piece_max", [P, NT, NPC])
        nm = [st.sb(f"neg_max{p}", [P, NT]) for p in range(2)]
        nm_rows = [st.sb(f"neg_rows{p}", [NT, P], F32R) for p in range(2)]
        inv = st.sb("inverse", [DH, BANK])
        ps_m = st.banks("max", R_S)
        ps_s = st.banks("scores", R_S)
        ps_o = st.banks("out", 2)
        ps_t = st.ps("turned")
        s_init = st.sem("initialised")
        s_load = st.sem("head_loaded")
        s_hi = st.sem("high_ready")
        s_lo = st.sem("low_ready")
        s_row = st.sem_n("max_row_loaded")
        s_v = st.sem_n("v_copied")
        s_mx = st.sem("max_scores_ready")
        s_mxfree = st.sem("max_bank_free")
        s_nm = st.sem("neg_max_ready")
        s_nmt = st.sem("neg_max_turned")
        s_rows = st.sem("neg_rows_ready")
        s_sc = st.sem("scores_ready")
        s_exp = st.sem("probs_ready")
        s_pv = st.sem("probs_used")
        s_outfree = st.sem_n("out_bank_free")
        with nc.Block() as block:
            @block.sync
            def _(sp):
                sp.wait_ge(s_init, 1)

                def row_of_maxima(h, p):
                    sp.wait_ge(s_rows, h + 2)
                    sp.dma_start(hi[0][p][ONE_ROW:ONE_ROW + 1, :].bitcast(F32), nm_rows[p][:].bitcast(F32)).then_inc(s_row[p], 16)

                load_head(sp, 0, 0, raw[0], raw[1], s_load)
                sp.wait_ge(s_lo, 2)
                load_head(sp, 1, 0, raw[0], raw[1], s_load)
                row_of_maxima(0, 0)

                def pair(j, last):
                    row_of_maxima(2 * j + 1, 1)
                    if not last:
                        sp.wait_ge(s_lo, 2 * (2 * j + 2))
                        load_head(sp, 0, j + 1, raw[0], raw[1], s_load)
                        row_of_maxima(2 * j + 2, 0)
                        sp.wait_ge(s_lo, 2 * (2 * j + 3))
                        load_head(sp, 1, j + 1, raw[0], raw[1], s_load)

                with sp.Fori(0, heads // 2 - 1) as j:
                    pair(j, False)
                pair(heads // 2 - 1, True)

            @block.gpsimd
            def _(pool):
                own = Steps(pool, st.sem("pool_step"))
                for p in range(2):
                    own(pool.memset(v_aug[p][:, :, DH:P], 1.0))
                for r in raw:
                    own(pool.memset(r[64:k_all, :], 0.0))
                if bias_row:
                    own(pool.memset(raw[0][DH:DH + 1, :], 1.0))
                own(pool.memset(raw[1][ONE_ROW:ONE_ROW + 1, :], 1.0))
                pool.sem_inc(s_init, 1)

                def copy_v(p, j):
                    for t in range(NK):
                        rows = min(P, T - P * t)
                        at = bass.ds((2 * j + p) * DH, DH)
                        last = pool.tensor_copy(v_aug[p][0:rows, t, 0:DH], v[0:rows, t, at])
                    last.then_inc(s_v[p], 1)

                for p in range(2):
                    copy_v(p, 0)
                with pool.Fori(0, heads // 2 - 1) as j:
                    for p in range(2):
                        pool.wait_ge(s_pv, NU * (2 * j + p + 1) + R_P)
                        copy_v(p, j + 1)

            @block.tensor
            def _(pe):
                pe.sem_inc(s_pv, R_P)

                def max_piece(h, p, m):
                    i, n, a, b = maxima[m]
                    pe.wait_ge(s_mxfree, NM * h + m + 1)
                    out = ps_m[m % R_S]
                    d = off + P * i
                    ins = pe.matmul(out[:, 0:b - a], hi[0][p][0:k_max, P * i:P * i + P],
                                    hi[1][p][0:k_max, a:b], start=True, stop=True)
                    if a <= d < b:
                        ins = pe.matmul(out[:, d - a:d - a + P], cst["identb"][:], mask_qk[:],
                                        start=False, stop=True, skip_group_check=True)
                    ins.then_inc(s_mx, 1)

                def turn_maxima(h, p):
                    pe.wait_ge(s_nm, h + 1)
                    pe.wait_ge(s_rows, h + 1)
                    pe.transpose(ps_t[0:NT, 0:P], nm[p][:], cst["ident"][:]).then_inc(s_nmt, 1)

                def scores(h, p, u):
                    n, t, first, masked = units[u]
                    a, b = HALVES[n]
                    rows = min(P, T - P * t)
                    pe.wait_ge(s_exp, NU * h + u + 1)
                    out = ps_s[u % R_S]
                    ks, qs = slice(P * t, P * t + rows), slice(first, b)
                    ins = products(pe, out[0:rows, first - a:b - a],
                                   [(hi[1][p][:, ks], hi[0][p][:, qs]), (hi[1][p][:, ks], lo[0][p][:, qs]),
                                    (lo[1][p][:, ks], hi[0][p][:, qs])])
                    if masked:
                        c0, c1 = masked
                        m0 = c0 - (P * t - off)
                        ins = pe.matmul(out[0:rows, c0 - a:c1 - a], cst["identb"][:, 0:rows],
                                        mask_kq[:, m0:m0 + c1 - c0],
                                        start=False, stop=True, skip_group_check=True)
                    ins.then_inc(s_sc, 1)

                def values(h, p, u):
                    n, t, first, _ = units[u]
                    a, b = HALVES[n]
                    rows = min(P, T - P * t)
                    if t == 0:
                        pe.wait_ge(s_outfree[n], h + 1)
                    pe.wait_ge(s_exp, NU * h + u + 1 + R_S)
                    pr = probs[(NU * p + u) % R_P]
                    pe.matmul(ps_o[n][:, first - a:b - a], v_aug[p][0:rows, t, :], pr[0:rows, first - a:b - a],
                              start=(t == 0), stop=True, skip_group_check=True).then_inc(s_pv, 1)

                def head(h, j, p, last):
                    pe.wait_ge(s_row[p], 16 * j + 16)
                    pe.wait_ge(s_v[p], j + 1)
                    pe.wait_ge(s_lo, 2 * h + 2)
                    scores(h, p, 0)
                    for u in range(NU):
                        if u + 1 < NU:
                            scores(h, p, u + 1)
                        if not last:
                            if u == FIRST:
                                pe.wait_ge(s_hi, 2 * h + 4)
                            for m in range(PER_UNIT * (u - FIRST), PER_UNIT * (u - FIRST + 1)):
                                if 0 <= m < NM:
                                    max_piece(h + 1, 1 - p, m)
                            if u == TURN_AT:
                                turn_maxima(h + 1, 1 - p)
                        values(h, p, u)

                pe.wait_ge(s_hi, 2)
                for m in range(NM):
                    max_piece(0, 0, m)
                turn_maxima(0, 0)
                with pe.Fori(0, heads // 2 - 1) as j:
                    head(2 * j, j, 0, False)
                    head(2 * j + 1, j, 1, False)
                last = heads // 2 - 1
                head(2 * last, last, 0, False)
                head(2 * last + 1, last, 1, True)

            @block.scalar
            def _(act):
                act.sem_inc(s_exp, R_S)

                def split_high(h, p, n):
                    if n == 0:
                        act.wait_ge(s_load, 16 * loads * (h + 1))
                    rows = ONE_ROW if n == 0 else k_all
                    act.copy(hi[n][p][0:rows, :], raw[n][0:rows, :]).then_inc(s_hi, 1)

                def head(h, p, last):
                    for u, (n, t, first, _) in enumerate(units):
                        a, b = HALVES[n]
                        rows = min(P, T - P * t)
                        act.wait_ge(s_sc, NU * h + u + 1)
                        act.wait_ge(s_pv, NU * h + u + 1)
                        act.activation(probs[(NU * p + u) % R_P][0:rows, first - a:b - a],
                                       ps_s[u % R_S][0:rows, first - a:b - a], ACT.Exp).then_inc(s_exp, 1)
                        if u in (0, 1) and not last:
                            split_high(h + 1, 1 - p, u)

                split_high(0, 0, 0)
                split_high(0, 0, 1)
                with act.Fori(0, heads // 2 - 1) as j:
                    head(2 * j, 0, False)
                    head(2 * j + 1, 1, False)
                head(heads - 2, 0, False)
                head(heads - 1, 1, True)

            @block.vector
            def _(dve):
                own = Steps(dve, st.sem("dve_step"))
                own(dve.memset(pm[:], 3.0 * MASKED))
                for p in range(2):
                    own(dve.memset(lo[0][p][ONE_ROW:k_all, :].bitcast(F32), 0.0))
                own.leave(1, 3)
                dve.sem_inc(s_rows, 1)
                dve.sem_inc(s_mxfree, R_S)
                for n in range(2):
                    dve.sem_inc(s_outfree[n], 1)

                def maxima_of(h, j, p, lag):
                    for m, (i, n, a, b) in enumerate(maxima):
                        dve.wait_ge(s_mx, NM * h + m + 1)
                        dve.tensor_reduce(pm[:, i, n:n + 1], ps_m[m % R_S][:, 0:b - a], AX.X,
                                          ALU.max).then_inc(s_mxfree, 1)
                    dve.wait_ge(s_mxfree, NM * h + NM + R_S)
                    dve.tensor_reduce(nm[p][:], pm[:], AX.X, ALU.max, negate=True).then_inc(s_nm, 1)
                    for n in range(2):
                        rows = ONE_ROW if n == 0 else k_all
                        dve.wait_ge(s_hi, 2 * h + n + 1)
                        dve.tensor_tensor(lo[n][p][0:rows, :], raw[n][0:rows, :],
                                          hi[n][p][0:rows, :].bitcast(F32), ALU.subtract).then_inc(s_lo, 1)
                    dve.wait_ge(s_nmt, h + 1)
                    if lag:
                        dve.wait_ge(s_row[p], 16 * j)
                    dve.tensor_copy(nm_rows[p][:], ps_t[0:NT, 0:P]).then_inc(s_rows, 1)

                def out_of(h, j, p):
                    for n, (a, b) in enumerate(HALVES):
                        end = [u for u in range(NU) if units[u][0] == n][-1]
                        dve.wait_ge(s_pv, NU * h + end + 1 + R_P)
                        own(dve.reciprocal(inv[:], ps_o[n][DH:P, :]))
                        dst = oT[DH * p:DH * p + DH, bass.ds(j, 1), a:b].rearrange("p a t -> p (a t)")
                        dve.tensor_tensor(dst, ps_o[n][0:DH, :], inv[:], ALU.mult).then_inc(s_outfree[n], 1)
                        dve.wait_ge(s_outfree[n], h + 2)

                maxima_of(0, 0, 0, False)

                def pair(j, first, last):
                    maxima_of(2 * j + 1, j, 1, not first)
                    out_of(2 * j, j, 0)
                    if not last:
                        maxima_of(2 * j + 2, j + 1, 0, True)
                    out_of(2 * j + 1, j, 1)

                pair(0, True, False)
                own.leave(1, 4)
                with dve.Fori(1, heads // 2 - 1) as j:
                    own.enter(j - 1, 4)
                    pair(j, False, False)
                own.leave(heads // 2 - 2, 4)
                pair(heads // 2 - 1, False, True)



def merge_branches(nc, w_in, outs, uT, branch, mergedT):
    NB = len(outs)
    kk = [n for _, n in branch]
    starts = [sum(kk[:b]) for b in range(NB)]
    NU = 2 * NB
    CREDIT = 2 * NU
    with stage(nc, "merge1") as st:
        wg = [st.sb(f"wg{p}", [P, NB, KD, P]) for p in range(2)]
        wy = [st.sb(f"wy{p}", [P, sum(kk), P]) for p in range(2)]
        sg = [st.sb(f"gate{b}", [P, BANK]) for b in range(NB)]
        pr = [st.sb(f"gated{b}", [P, BANK]) for b in range(NB)]
        ps_g, ps_y = st.banks("gates", NB), st.banks("branch", NB)
        s_w = st.sem_n("w_loaded")
        s_gy = st.sem("unit_ready")
        s_sg = st.sem("gate_ready")
        s_done = st.sem("unit_used")
        with nc.Block() as block:
            @block.sync
            def _(sp):
                gsrc = w_in[:, C_G1:C_G1 + NB * D].rearrange("(c p) (b n) -> b p c n", p=P, b=NB)
                with sp.Fori(0, KD // 2) as i:
                    for p in range(2):
                        m = P * (2 * i + p)
                        sp.wait_ge(s_gy, NU * (2 * i + p + 1))
                        for b in range(NB):
                            sp.dma_start(wg[p][:, b], gsrc[b, :, :, bass.ds(m, P)]).then_inc(s_w[p], 16)
                            sp.dma_start(wy[p][:, starts[b]:starts[b] + kk[b], :],
                                         chunked(outs[b])[:, :, bass.ds(m, P)]).then_inc(s_w[p], 16)

            @block.tensor
            def _(pe):
                pe.sem_inc(s_gy, CREDIT)
                with pe.Fori(0, KD // 2) as i:
                    for p in range(2):
                        pe.wait_ge(s_w[p], 32 * NB * i + 32 * NB)
                        for h, (a, z) in enumerate(HALVES):
                            for b, (of, n) in enumerate(branch):
                                pe.wait_ge(s_done, NU * (2 * i + p) + NB * h + b + 1)
                                products(pe, ps_g[b][:], [(wg[p][:, b, k, :], uT(k, a, z)) for k in range(KD)])
                                products(pe, ps_y[b][:], [(wy[p][:, starts[b] + k, :], of(k, a, z))
                                                          for k in range(n)]).then_inc(s_gy, 1)

            @block.scalar
            def _(act):
                with act.Fori(0, KD // 2) as i:
                    for p in range(2):
                        for u in range(NU):
                            act.wait_ge(s_gy, NU * (2 * i + p) + u + 1 + CREDIT)
                            act.activation(sg[u % NB][:], ps_g[u % NB][:], ACT.Sigmoid).then_inc(s_sg, 1)

            @block.vector
            def _(dve):
                own = Steps(dve, st.sem("dve_step"))
                dve.sem_inc(s_done, NB)
                per = 2 * 2 * (NB - 1)
                with dve.Fori(0, KD // 2) as i:
                    own.enter(i, per)
                    for p in range(2):
                        for h, (a, z) in enumerate(HALVES):
                            dst = mergedT[:, bass.ds(2 * i + p, 1), a:z].rearrange("p c t -> p (c t)")
                            for b in range(NB):
                                g = NU * (2 * i + p) + NB * h + b
                                dve.wait_ge(s_sg, g + 1)
                                dve.tensor_tensor(pr[b][:], ps_y[b][:], sg[b][:], ALU.mult).then_inc(s_done, 1)
                                dve.wait_ge(s_done, g + 1 + NB)
                                if b:
                                    own(dve.tensor_tensor(dst if b == NB - 1 else pr[0][:], pr[0][:], pr[b][:],
                                                          ALU.add))
                own.leave(KD // 2, per)


def output_and_router(nc, cst, name, mergedT, w_o, resid, g_row, routers, biases, h_out, v_out, logits):
    NL = NG + routers[1].shape[1]
    with stage(nc, name) as st:
        wo = st.sb("w", [P, KD, D])
        x = st.sb("h", [P, NT, D])
        g = st.sb("g", [P, D])
        v = [st.sb(f"v{q}", [P, D]) for q in range(2)]
        vT = [st.sb(f"vT{q}", [P, KD, P]) for q in range(2)]
        wr = st.sb("wr", [P, KD, NL])
        br = st.sb("br", [P, NL])
        junk = st.sb("squares", [P, D])
        ss, ms, rt, inv = (st.sb(n, [P, NT]) for n in ("sums", "mean", "root", "inverse"))
        acc = st.banks("acc", 4)
        turn = st.banks("turn", 2)
        lg = st.banks("logits", 2)
        s_w = st.sem("w_loaded")
        s_r = st.sem("router_loaded")
        s_x = st.sem_n("resid_loaded", NT)
        s_acc = st.sem("acc_ready")
        s_h = st.sem("h_ready")
        s_ss = st.sem("sum_ready")
        s_ms = st.sem("mean_ready")
        s_rt = st.sem("root_ready")
        s_inv = st.sem("inverse_ready")
        s_v = st.sem("v_ready")
        s_turn = st.sem("turned")
        s_vT = st.sem("vT_ready")
        s_lg = st.sem("logits_ready")
        s_lgfree = st.sem("logits_copied")
        s_sv = st.sem_n("v_stored")
        s_sh = st.sem("h_stored")
        with nc.Block() as block:
            @block.sync
            def _(sp):
                for k in range(KD):
                    sp.dma_start(wo[:, k, :], w_o[k * P:(k + 1) * P, :]).then_inc(s_w, 16)
                for t in range(NT):
                    sp.dma_start(x[:, t, :], resid[t * P:(t + 1) * P, :]).then_inc(s_x[t], 16)
                with nc.allow_non_contiguous_dma(reason="router columns"):
                    sp.dma_start(wr[:, :, 0:NG], chunked(routers[0])).then_inc(s_r, 16)
                    sp.dma_start(wr[:, :, NG:], chunked(routers[1])).then_inc(s_r, 16)
                    sp.dma_start(br[:, 0:NG], biases[0].to_broadcast((P, NG))).then_inc(s_r, 16)
                    sp.dma_start(br[:, NG:], biases[1].to_broadcast((P, NL - NG))).then_inc(s_r, 16)
                    sp.dma_start(g[:], g_row.to_broadcast((P, D))).then_inc(s_r, 16)
                for t in range(NT):
                    sp.wait_ge(s_h, 2 * t + 2)
                    sp.dma_start(h_out[t * P:(t + 1) * P, :], x[:, t, :]).then_inc(s_sh, 16)
                    sp.wait_ge(s_v, t + 1)
                    sp.dma_start(v_out[t * P:(t + 1) * P, :], v[t % 2][:]).then_inc(s_sv[t % 2], 16)
                sp.wait_ge(s_sh, 16 * NT)
                for q in range(2):
                    sp.wait_ge(s_sv[q], 16 * NT // 2)

            @block.tensor
            def _(pe):
                pe.wait_ge(s_w, 16 * KD)

                def project(t):
                    for h, (a, b) in enumerate(HALVES):
                        if t >= 2:
                            pe.wait_ge(s_h, 2 * (t - 2) + h + 1)
                        products(pe, acc[2 * (t % 2) + h][:],
                                 [(mergedT[:, k, t * P:(t + 1) * P], wo[:, k, a:b]) for k in range(KD)]
                                 ).then_inc(s_acc, 1)

                def turn_v(t):
                    pe.wait_ge(s_v, t + 1)
                    for h in range(2):
                        if t:
                            pe.wait_ge(s_vT, 2 * (t - 1) + h + 1)
                        for c in range(4):
                            k = 4 * h + c
                            last = pe.transpose(turn[h][:, c * P:(c + 1) * P], v[t % 2][:, k * P:(k + 1) * P],
                                                cst["ident"][:])
                        last.then_inc(s_turn, 1)

                def route(t):
                    if t == 0:
                        pe.wait_ge(s_r, 80)
                    pe.wait_ge(s_vT, 2 * t + 2)
                    if t >= 2:
                        pe.wait_ge(s_lgfree, t - 1)
                    products(pe, lg[t % 2][:, 0:NL],
                             [(vT[t % 2][:, k, :], wr[:, k, :]) for k in range(KD)]).then_inc(s_lg, 1)

                for t in range(NT + 2):
                    if t < NT:
                        project(t)
                    if 1 <= t <= NT:
                        turn_v(t - 1)
                    if t >= 2:
                        route(t - 2)

            @block.vector
            def _(dve):
                for t in range(NT + 2):
                    if t < NT:
                        dve.wait_ge(s_x[t], 16)
                        for h, (a, b) in enumerate(HALVES):
                            dve.wait_ge(s_acc, 2 * t + h + 1)
                            dve.tensor_tensor(x[:, t, a:b], x[:, t, a:b], acc[2 * (t % 2) + h][:],
                                              ALU.add).then_inc(s_h, 1)
                        dve.wait_ge(s_ss, t + 1)
                        dve.tensor_scalar(ms[:, t:t + 1], ss[:, t:t + 1], 1.0 / D, EPS, ALU.mult,
                                          ALU.add).then_inc(s_ms, 1)
                        dve.wait_ge(s_rt, t + 1)
                        dve.reciprocal(inv[:, t:t + 1], rt[:, t:t + 1]).then_inc(s_inv, 1)
                        dve.wait_ge(s_inv, t + 1)
                        if t == 0:
                            dve.wait_ge(s_r, 80)
                        else:
                            dve.wait_ge(s_turn, 2 * t - 2 if t >= 2 else 1)
                        if t >= 2:
                            dve.wait_ge(s_sv[t % 2], 16 * (t // 2))
                        dve.scalar_tensor_tensor(out=v[t % 2][:], in0=x[:, t, :], scalar=inv[:, t:t + 1],
                                                 in1=g[:], op0=ALU.mult, op1=ALU.mult).then_inc(s_v, 1)
                    if t >= 2:
                        dve.wait_ge(s_lg, t - 1)
                        dve.tensor_tensor(logits[:, t - 2, :], lg[t % 2][:, 0:NL], br[:],
                                          ALU.add).then_inc(s_lgfree, 1)

            @block.scalar
            def _(act):
                for t in range(NT + 1):
                    if t < NT:
                        act.wait_ge(s_h, 2 * t + 2)
                        act.activation(junk[:], x[:, t, :], ACT.Square, accum_out=ss[:, t:t + 1]).then_inc(s_ss, 1)
                        act.wait_ge(s_ms, t + 1)
                        act.activation(rt[:, t:t + 1], ms[:, t:t + 1], ACT.Sqrt).then_inc(s_rt, 1)
                    if t:
                        for h in range(2):
                            act.wait_ge(s_turn, 2 * (t - 1) + h + 1)
                            if t >= 3:
                                act.wait_ge(s_lg, t - 2)
                            act.copy(vT[(t - 1) % 2][:, 4 * h:4 * h + 4, :].rearrange("p c t -> p (c t)"),
                                     turn[h][:]).then_inc(s_vT, 1)



def block_count(experts):
    n = (2 * S + experts * (P - 1)) // P
    return n + n % 2


def route_tokens(nc, cst, name, experts, logits, ids_d, r):
    E, EG, NB = experts, experts // NG, block_count(experts)
    BIG = 1e30
    with stage(nc, name) as st:
        ones_e = st.sb("ones_e", [P, E])
        e_int, g_int = st.sb("e_int", [P, E], I32), st.sb("g_int", [P, NG], I32)
        t_int, b_int = st.sb("t_int", [P, NT], I32), st.sb("b_int", [P, NB], I32)
        e_desc, g_desc = st.sb("e_desc", [P, E]), st.sb("g_desc", [P, NG])
        t_id, b_id = st.sb("t_id", [P, NT]), st.sb("b_id", [P, NB])
        strict = st.sb("strict", [P, P])
        gx, goh, gpen = (st.sb(n, [P, NT, NG]) for n in ("gx", "goh", "gpen"))
        em, t3, oh1, oh2, both, place = (st.sb(n, [P, NT, E]) for n in ("em", "t3", "oh1", "oh2", "both", "place"))
        top, tmp, gmax, v1, v2, gw, ex, sl = (st.sb(n, [P, NT]) for n in
                                              ("top", "tmp", "gmax", "v1", "v2", "gw", "ex", "sl"))
        count, nb, ends = (st.sb(n, [P, E]) for n in ("count", "nb", "ends"))
        cmp = st.sb("cmp", [1, NB, E])
        be, pf = st.sb("be", [1, NB]), st.sb("pf", [1, 1])
        id_rows = st.sb("id_rows", [NB, P])
        ps_rank, ps_tot, ps_id = st.ps("rank"), st.ps("total"), st.ps("ids")
        s_const = st.sem("constants_ready")
        s_zero = st.sem("ids_cleared")
        s_exp = st.sem("exponent")
        s_both = st.sem("choices_ready")
        s_rank = st.sem("ranks_ready")
        s_slot = st.sem("slots_ready")
        s_scat = st.sem("ids_scattered")
        s_load = st.sem("ids_loaded")
        s_turn = st.sem("ids_turned")
        with nc.Block() as block:
            @block.gpsimd
            def _(pool):
                own = Steps(pool, st.sem("pool_step"))
                own(pool.memset(id_rows[:], 0.0))
                pool.iota(e_int[:], pattern=[[-1, E]], base=E, channel_multiplier=0)
                pool.iota(g_int[:], pattern=[[-1, NG]], base=NG, channel_multiplier=0)
                pool.iota(t_int[:], pattern=[[P, NT]], base=0, channel_multiplier=1)
                pool.iota(b_int[:], pattern=[[1, NB]], base=0, channel_multiplier=0)
                own(pool.memset(strict[:], 1.0))
                own(pool.affine_select(out=strict[:], in_=strict[:], compare_op=ALU.is_gt, fill=0.0, base=0,
                                       pattern=[[1, P]], channel_multiplier=-1))
                pool.sem_inc(s_const, 1)
                pool.wait_ge(s_slot, 2)
                pool.wait_ge(s_zero, 16)
                for k in range(2):
                    for t in range(NT):
                        pool.indirect_dma_start(
                            out=ids_d, out_offset=bass.IndirectOffsetOnAxis(ap=r["slots"][:, k, t:t + 1], axis=0),
                            in_=t_id[:, t:t + 1], in_offset=None).then_inc(s_scat, 16)

            @block.sync
            def _(sp):
                rows = ids_d.rearrange("(b p) a -> b (p a)", p=P)
                sp.wait_ge(s_const, 1)
                sp.dma_start(rows, id_rows[:]).then_inc(s_zero, 16)
                sp.wait_ge(s_zero, 16)
                sp.wait_ge(s_scat, 16 * 2 * NT)
                sp.dma_start(id_rows[:], rows).then_inc(s_load, 16)

            @block.tensor
            def _(pe):
                pe.wait_ge(s_both, 1)
                pe.wait_ge(s_const, 1)
                flat = both[:].rearrange("p t e -> p (t e)")
                pe.matmul(ps_rank[:, 0:NT * E], strict[:], flat, start=True, stop=True).then_inc(s_rank, 1)
                pe.matmul(ps_tot[:, 0:NT * E], cst["ones"][:], flat, start=True, stop=True).then_inc(s_rank, 1)
                pe.wait_ge(s_load, 16)
                pe.transpose(ps_id[:, 0:NB], id_rows[:], cst["ident"][0:NB, 0:NB]).then_inc(s_turn, 1)

            @block.scalar
            def _(act):
                act.wait_ge(s_exp, 1)
                act.activation(gx[:], gx[:], ACT.Exp).then_inc(s_exp, 1)
                act.wait_ge(s_exp, 3)
                act.activation(ex[:], ex[:], ACT.Exp).then_inc(s_exp, 1)

            @block.vector
            def _(dve):
                own = Steps(dve, st.sem("dve_step"))
                TT, TS = dve.tensor_tensor, dve.tensor_scalar

                def wide(ap, n):
                    return ap[:, :, None].broadcast_to((P, NT, n))

                def table(ap, n):
                    return ap[:, None, :].broadcast_to((P, NT, n))

                def best(src, n, desc, onehot, t, out):
                    own(dve.tensor_reduce(out[:], src, AX.X, ALU.max))
                    own(TT(t, src, wide(out[:], n), ALU.is_equal))
                    own(TT(t, t, table(desc[:], n), ALU.mult))
                    own(dve.tensor_reduce(top[:], t, AX.X, ALU.max))
                    own(TT(onehot[:], table(desc[:], n), wide(top[:], n), ALU.is_equal))

                own(dve.memset(ones_e[:], 1.0))
                dve.wait_ge(s_const, 1)
                for a, b in ((e_desc, e_int), (g_desc, g_int), (t_id, t_int), (b_id, b_int)):
                    own(dve.tensor_copy(a[:], b[:]))
                g, e = logits[:, :, 0:NG], logits[:, :, NG:NG + E]
                best(g, NG, g_desc, goh, gpen[:], gmax)
                TT(gx[:], g, wide(gmax[:], NG), ALU.subtract).then_inc(s_exp, 1)
                own(TS(gpen[:], goh[:], BIG, -BIG, ALU.mult, ALU.add))
                four = em[:].rearrange("p t (g e) -> p t g e", g=NG)
                own(TT(four, e.rearrange("p t (g e) -> p t g e", g=NG),
                       goh[:][:, :, :, None].broadcast_to((P, NT, NG, EG)), ALU.mult))
                own(TT(four, four, gpen[:][:, :, :, None].broadcast_to((P, NT, NG, EG)), ALU.add))
                best(em[:], E, e_desc, oh1, t3[:], v1)
                own(TS(t3[:], oh1[:], -1e5 * BIG, None, ALU.mult))
                own(TT(em[:], em[:], t3[:], ALU.add))
                best(em[:], E, e_desc, oh2, t3[:], v2)
                TT(both[:], oh1[:], oh2[:], ALU.add).then_inc(s_both, 1)
                dve.wait_ge(s_exp, 2)
                TT(ex[:], v2[:], v1[:], ALU.subtract).then_inc(s_exp, 1)
                own(dve.tensor_reduce(tmp[:], gx[:], AX.X, ALU.add))
                own(dve.reciprocal(gw[:], tmp[:]))
                dve.wait_ge(s_exp, 4)
                own(TS(tmp[:], ex[:], 1.0, None, ALU.add))
                own(dve.reciprocal(tmp[:], tmp[:]))
                own(TT(r["weights"][:, 0, :], gw[:], tmp[:], ALU.mult))
                own(TT(r["weights"][:, 1, :], r["weights"][:, 0, :], ex[:], ALU.mult))
                dve.wait_ge(s_rank, 2)
                tot = ps_tot[:, 0:NT * E].rearrange("p (t e) -> p t e", t=NT)
                own(dve.tensor_reduce(count[:], tot.rearrange("p t e -> p e t"), AX.X, ALU.add))
                own(TS(count[:], count[:], 1.0 / P, (P - 1.0) / (2 * P), ALU.mult, ALU.add))
                own(TS(nb[:], count[:], ROUND, ROUND, ALU.add, ALU.subtract))
                own(dve.tensor_tensor_scan(ends[:], ones_e[:], nb[:], 0.0, ALU.mult, ALU.add))
                own(TT(nb[:], ends[:], nb[:], ALU.subtract))
                own(TS(place[:, 0, :], nb[:], float(P), None, ALU.mult))
                for t in range(1, NT):
                    own(TT(place[:, t, :], place[:, t - 1, :], tot[:, t - 1, :], ALU.add))
                own(TT(place[:], place[:], ps_rank[:, 0:NT * E].rearrange("p (t e) -> p t e", t=NT), ALU.add))
                for k, oh in enumerate((oh1, oh2)):
                    own(TT(t3[:], oh[:], place[:], ALU.mult))
                    own(dve.tensor_reduce(sl[:], t3[:], AX.X, ALU.add))
                    dve.tensor_copy(r["slots"][:, k, :], sl[:]).then_inc(s_slot, 1)
                    dve.wait_ge(s_slot, k + 1)
                own(TT(cmp[:], ends[0:1, None, :].broadcast_to((1, NB, E)),
                       b_id[0:1, :, None].broadcast_to((1, NB, E)), ALU.is_le))
                own(dve.tensor_reduce(be[:], cmp[:], AX.X, ALU.add))
                own(TS(be[:], be[:], E - 1.0, None, ALU.min))
                own(dve.tensor_copy(r["expert"][:], be[:]))
                own(TS(pf[:], ends[0:1, E - 1:E], 0.5, 0.25, ALU.mult, ALU.add))
                own(TS(pf[:], pf[:], ROUND, ROUND, ALU.add, ALU.subtract))
                own(dve.tensor_copy(r["pairs"][:], pf[:]))
                dve.wait_ge(s_turn, 1)
                dve.tensor_copy(r["token"][:], ps_id[:, 0:NB])


def run_experts(nc, cst, name, experts, w1, w3, w2, v_d, y_d, r):
    NB = block_count(experts)
    KH = HID // P
    with stage(nc, name) as st:
        w13 = [st.sb(f"w13_{p}", [P, KD, 2 * HID]) for p in range(2)]
        wd = [st.sb(f"w2_{p}", [P, KH, D]) for p in range(2)]
        x = [st.sb(f"x{p}", [P, D]) for p in range(2)]
        idx = [st.sb(f"idx{p}", [P, 1], U32) for p in range(2)]
        xT = [st.sb(f"xT{p}", [P, KD, P]) for p in range(2)]
        sil = [st.sb(f"silu{p}", [P, HID]) for p in range(2)]
        he = [st.sb(f"h{p}", [P, HID]) for p in range(2)]
        hT = [st.sb(f"hT{p}", [P, KH, P]) for p in range(2)]
        y = [st.sb(f"y{p}", [P, D]) for p in range(2)]
        zero = st.sb("zero", [P, D])
        turn = [st.banks(f"turn{p}_", 2) for p in range(2)]
        up = st.banks("up", 2)
        down = [st.banks("down", 2), [turn[0][1], turn[1][1]]]
        s_idx = st.sem_n("idx_ready")
        s_x = st.sem_n("x_loaded")
        s_w13 = st.sem_n("w13_loaded")
        s_w2 = st.sem_n("w2_loaded")
        s_turn = st.sem_n("x_turned")
        s_xT = [st.sem_n("xT_by_dve"), st.sem_n("xT_by_act")]
        s_up = st.sem_n("up_ready")
        s_sil = st.sem_n("silu_ready")
        s_he = st.sem_n("h_ready")
        s_hturn = st.sem_n("h_turned")
        s_hT = st.sem_n("hT_ready")
        s_down = st.sem_n("down_ready")
        s_y = [st.sem_n("y_by_dve"), st.sem_n("y_by_act")]
        s_st = st.sem_n("y_stored")
        s_end = st.sem("ended")
        s_fill = st.sem("blocks_filled")
        s_zero = st.sem("zeros_ready")
        s_go = st.sem("gather_may_start")

        def pairs(eng):
            return eng.value_load(r["pairs"][0:1, 0:1], min_val=1, max_val=NB // 2)

        with nc.Block() as block:
            @block.sync
            def _(sp):
                up1, up3, dn = (w.rearrange("e (c p) n -> p e c n", p=P) for w in (w1, w3, w2))
                n_pairs = pairs(sp)
                with sp.Fori(0, n_pairs) as i:
                    e = [sp.value_load(r["expert"][0:1, bass.ds(2 * i + p, 1)], min_val=0, max_val=experts - 1)
                         for p in range(2)]
                    for p in range(2):
                        sp.wait_ge(s_up[p], i + 1)
                        for n, w in enumerate((up1, up3)):
                            sp.dma_start(w13[p][:, :, n * HID:(n + 1) * HID],
                                         w[:, bass.ds(e[p], 1)].rearrange("p a c n -> p (a c) n")).then_inc(s_w13[p], 16)
                    for p in range(2):
                        sp.wait_ge(s_down[p], 2 * i + 2)
                        sp.dma_start(wd[p][:], dn[:, bass.ds(e[p], 1)].rearrange("p a c n -> p (a c) n")).then_inc(s_w2[p], 16)
                        sp.sem_inc(s_fill, 16)
                sp.wait_ge(s_zero, 1)
                with sp.Fori(n_pairs, NB // 2 + 1) as i:
                    for p in range(2):
                        sp.dma_start(y_d[bass.ds((2 * i + p) * P, P), :], zero[:]).then_inc(s_fill, 16)
                sp.wait_ge(s_fill, 16 * (NB + 2))

            @block.gpsimd
            def _(pool):
                with pool.Fori(0, pairs(pool)) as i:
                    for p in range(2):
                        pool.wait_ge(s_turn[p], 2 * i + 2)
                        pool.tensor_copy(idx[p][:], r["token"][:, bass.ds(2 * i + p, 1)]).then_inc(s_idx[p], 1)
                        pool.wait_ge(s_idx[p], i + 1)
                        pool.sem_inc(s_go, 1)
                        pool.indirect_dma_start(
                            out=x[p][:], out_offset=None, in_=v_d,
                            in_offset=bass.IndirectOffsetOnAxis(ap=idx[p][:, 0:1], axis=0)).then_inc(s_x[p], 16)

            @block.tensor
            def _(pe):
                for p in range(2):
                    pe.sem_inc(s_turn[p], 2)
                    pe.sem_inc(s_up[p], 1)
                    pe.sem_inc(s_down[p], 2)
                with pe.Fori(0, pairs(pe)) as i:
                    for p in range(2):
                        pe.wait_ge(s_x[p], 16 * i + 16)
                        for eng in range(2):
                            pe.wait_ge(s_y[eng][1], i + 1)
                        for h in range(2):
                            for c in range(4):
                                k = 4 * h + c
                                last = pe.transpose(turn[p][h][:, c * P:(c + 1) * P], x[p][:, k * P:(k + 1) * P],
                                                    cst["ident"][:])
                            last.then_inc(s_turn[p], 1)
                    for p in range(2):
                        pe.wait_ge(s_w13[p], 32 * i + 32)
                        for eng in range(2):
                            pe.wait_ge(s_xT[eng][p], i + 1)
                        products(pe, up[p][:], [(xT[p][:, k, :], w13[p][:, k, :]) for k in range(KD)]).then_inc(s_up[p], 1)
                    for p in range(2):
                        pe.wait_ge(s_he[p], i + 1)
                        for k in range(KH):
                            last = pe.transpose(turn[p][0][:, k * P:(k + 1) * P], he[p][:, k * P:(k + 1) * P],
                                                cst["ident"][:])
                        last.then_inc(s_hturn[p], 1)
                    for p in range(2):
                        pe.wait_ge(s_w2[p], 16 * i + 16)
                        pe.wait_ge(s_hT[p], i + 1)
                        for h, (a, b) in enumerate(HALVES):
                            pe.wait_ge(s_y[h][p], i + 1)
                            products(pe, down[p][h][:], [(hT[p][:, k, :], wd[p][:, k, a:b])
                                                         for k in range(KH)]).then_inc(s_down[p], 1)

            def copy_half(eng, copy, e, i):
                for p in range(2):
                    eng.wait_ge(s_turn[p], 2 * i + e + 3)
                    copy(xT[p][:, 4 * e:4 * e + 4, :].rearrange("p c t -> p (c t)"), turn[p][e][:]).then_inc(s_xT[e][p], 1)

            def copy_y(eng, copy, e, i, p):
                a, b = HALVES[e]
                eng.wait_ge(s_down[p], 2 * i + e + 3)
                eng.wait_ge(s_st[p], 16 * i + 16)
                copy(y[p][:, a:b], down[p][e][:]).then_inc(s_y[e][p], 1)

            @block.vector
            def _(dve):
                for p in range(2):
                    dve.sem_inc(s_y[0][p], 1)
                    dve.sem_inc(s_y[1][p], 1)
                    dve.sem_inc(s_st[p], 16)
                dve.memset(zero[:], 0.0).then_inc(s_zero, 1)
                with dve.Fori(0, pairs(dve)) as i:
                    copy_half(dve, dve.tensor_copy, 0, i)
                    for p in range(2):
                        dve.wait_ge(s_sil[p], i + 1)
                        dve.tensor_tensor(he[p][:], up[p][:, HID:], sil[p][:], ALU.mult).then_inc(s_he[p], 1)
                    for p in range(2):
                        dve.wait_ge(s_hturn[p], i + 1)
                        dve.tensor_copy(hT[p][:].rearrange("p c t -> p (c t)"), turn[p][0][:, 0:HID]).then_inc(s_hT[p], 1)
                    for p in range(2):
                        copy_y(dve, dve.tensor_copy, 0, i, p)

            @block.scalar
            def _(act):
                n = pairs(act)
                with act.Fori(0, n) as i:
                    copy_half(act, act.copy, 1, i)
                    for p in range(2):
                        act.wait_ge(s_up[p], i + 2)
                        act.activation(sil[p][:], up[p][:, 0:HID], ACT.Silu).then_inc(s_sil[p], 1)
                    for p in range(2):
                        copy_y(act, act.copy, 1, i, p)
                    for p in range(2):
                        act.wait_ge(s_y[0][p], i + 2)
                        act.wait_ge(s_y[1][p], i + 2)
                        act.dma_start(y_d[bass.ds((2 * i + p) * P, P), :], y[p][:]).then_inc(s_st[p], 16)
                for p in range(2):
                    act.wait_ge(s_st[p], 16 * n + 16)
                    act.sem_inc(s_end, 1)


def combine(nc, name, r, h_d, y_d, g_row, out_d):
    with stage(nc, name) as st:
        h = st.sb("h", [P, NT, D])
        y = [[st.sb(f"y{k}_{q}", [P, D]) for q in range(2)] for k in range(2)]
        g = st.sb("g", [P, D])
        junk = st.sb("squares", [P, D])
        ss, ms, rt, inv = (st.sb(n, [P, NT]) for n in ("sums", "mean", "root", "inverse"))
        s_h = st.sem_n("h_loaded", NT)
        s_g = st.sem("g_loaded")
        s_y = [st.sem_n("y0_loaded"), st.sem_n("y1_loaded")]
        s_sum = st.sem("summed")
        s_ss, s_ms, s_rt, s_inv, s_out = (st.sem(n) for n in ("sum_ready", "mean_ready", "root_ready",
                                                             "inverse_ready", "out_ready"))
        s_st = st.sem("stored")
        with nc.Block() as block:
            @block.sync
            def _(sp):
                if g_row is not None:
                    sp.dma_start(g[:], g_row.to_broadcast((P, D))).then_inc(s_g, 16)
                for t in range(NT):
                    sp.dma_start(h[:, t, :], h_d[t * P:(t + 1) * P, :]).then_inc(s_h[t], 16)
                for t in range(NT):
                    sp.wait_ge(s_out if g_row is not None else s_sum, t + 1 if g_row is not None else 2 * t + 2)
                    sp.dma_start(out_d[t * P:(t + 1) * P, :], h[:, t, :]).then_inc(s_st, 16)
                sp.wait_ge(s_st, 16 * NT)

            @block.gpsimd
            def _(pool):
                for t in range(NT):
                    for k in range(2):
                        if t >= 2:
                            pool.wait_ge(s_sum, 2 * (t - 2) + k + 1)
                        pool.indirect_dma_start(
                            out=y[k][t % 2][:], out_offset=None, in_=y_d,
                            in_offset=bass.IndirectOffsetOnAxis(ap=r["slots"][:, k, t:t + 1], axis=0)
                        ).then_inc(s_y[k][t % 2], 16)

            @block.vector
            def _(dve):
                for t in range(NT):
                    dve.wait_ge(s_h[t], 16)
                    for k in range(2):
                        dve.wait_ge(s_y[k][t % 2], 16 * (t // 2 + 1))
                        dve.scalar_tensor_tensor(out=h[:, t, :], in0=y[k][t % 2][:],
                                                 scalar=r["weights"][:, k, t:t + 1], in1=h[:, t, :],
                                                 op0=ALU.mult, op1=ALU.add).then_inc(s_sum, 1)
                        dve.wait_ge(s_sum, 2 * t + k + 1)
                    if g_row is not None:
                        dve.wait_ge(s_ss, t + 1)
                        dve.tensor_scalar(ms[:, t:t + 1], ss[:, t:t + 1], 1.0 / D, EPS, ALU.mult,
                                          ALU.add).then_inc(s_ms, 1)
                        dve.wait_ge(s_rt, t + 1)
                        dve.reciprocal(inv[:, t:t + 1], rt[:, t:t + 1]).then_inc(s_inv, 1)
                        dve.wait_ge(s_inv, t + 1)
                        dve.wait_ge(s_g, 16)
                        dve.scalar_tensor_tensor(out=h[:, t, :], in0=h[:, t, :], scalar=inv[:, t:t + 1],
                                                 in1=g[:], op0=ALU.mult, op1=ALU.mult).then_inc(s_out, 1)

            if g_row is not None:
                @block.scalar
                def _(act):
                    for t in range(NT):
                        act.wait_ge(s_sum, 2 * t + 2)
                        act.activation(junk[:], h[:, t, :], ACT.Square, accum_out=ss[:, t:t + 1]).then_inc(s_ss, 1)
                        act.wait_ge(s_ms, t + 1)
                        act.activation(rt[:, t:t + 1], ms[:, t:t + 1], ACT.Sqrt).then_inc(s_rt, 1)



def recurrent_branch(nc, cst, col, w_in, wa, wx, uT, mergedT):
    BW = 256
    NCH = BW // P
    NB = D // BW
    CW = 4
    UNITS = 5 * 2 * NCH
    RING = 4
    src = chunked(w_in)
    with stage(nc, "rnn") as st:
        w3 = [st.sb(n, [P, KD, BW]) for n in ("wx", "wg", "wt")]
        wl = [st.sb(n, [P, NCH, BW]) for n in ("wr", "wi")]
        xr = st.sb("xr", [P, NCH, CW - 1 + S])
        xa = st.sb("xa", [P, NCH, S])
        ge, gt, rr, ii, aa = (st.sb(n, [P, NCH, S]) for n in ("gelu", "gate", "r", "i", "a"))
        cw, cb = st.sb("conv_w", [P, CW, NCH]), st.sb("conv_b", [P, NCH])
        ba, bx, lc, nlc = (st.sb(n, [P, NCH]) for n in ("ba", "bx", "lc", "nlc"))
        x8, m8, z8, q8, sp8 = (st.sb(n, [P, KD]) for n in ("x8", "m8", "z8", "q8", "sp8"))
        ps = st.banks("ps", RING)
        s_w = [st.sem(f"w{n}_loaded") for n in range(3)]
        s_wl = st.sem("lru_w_loaded")
        s_ps = st.sem("unit_ready")
        s_ev = st.sem("unit_copied")
        s_xa = st.sem("xa_ready")
        s_col = st.sem("columns_ready")
        s_x8 = st.sem("lambda_step")
        s_a = st.sem("a_ready")
        s_d = st.sem("ratio_ready")
        s_m = st.sem("mult_ready")
        s_done = st.sem("block_done")
        with nc.Block() as block:
            @block.sync
            def _(sp):
                with sp.Fori(0, NB) as q:
                    for n, c0 in enumerate((C_XR, C_GR, C_GT)):
                        sp.wait_ge(s_ps, UNITS * q + 2 * NCH * (n + 1))
                        sp.dma_start(w3[n][:], src[:, :, bass.ds(c0 + BW * q, BW)]).then_inc(s_w[n], 16)
                    sp.wait_ge(s_ps, UNITS * q + UNITS)
                    for n, w in enumerate((wa, wx)):
                        sp.dma_start(wl[n][:], w[bass.ds(q, 1)].rearrange("a (c p) n -> p (a c) n", p=P)).then_inc(s_wl, 16)

            @block.tensor
            def _(pe):
                pe.sem_inc(s_ps, UNITS)
                with pe.Fori(0, NB) as q:
                    u = 0
                    for n in range(3):
                        pe.wait_ge(s_w[n], 16 * q + 16)
                        for c in range(NCH):
                            for a, b in HALVES:
                                pe.wait_ge(s_ev, UNITS * q + u + 1)
                                products(pe, ps[u % RING][:], [(w3[n][:, k, c * P:(c + 1) * P], uT[:, k, a:b])
                                                               for k in range(KD)]).then_inc(s_ps, 1)
                                u += 1
                    pe.wait_ge(s_wl, 32 * q + 32)
                    pe.wait_ge(s_xa, NCH * q + NCH)
                    for n in range(2):
                        for c in range(NCH):
                            for a, b in HALVES:
                                pe.wait_ge(s_ev, UNITS * q + u + 1)
                                products(pe, ps[u % RING][:], [(wl[n][:, k, c * P:(c + 1) * P], xa[:, k, a:b])
                                                               for k in range(NCH)]).then_inc(s_ps, 1)
                                u += 1

            @block.scalar
            def _(act):
                act.wait_ge(s_x8, 1)
                act.activation(x8[:], x8[:], ACT.Exp).then_inc(s_x8, 1)
                act.sem_inc(s_ev, RING)
                with act.Fori(0, NB) as q:
                    act.wait_ge(s_done, q + 1)
                    u = 0
                    for n, (dst, f, bias) in enumerate(((xr, ACT.Copy, None), (ge, ACT.Gelu_apprx_tanh, None),
                                                        (gt, ACT.Sigmoid, None), (rr, ACT.Sigmoid, ba),
                                                        (ii, ACT.Sigmoid, bx))):
                        if n == 3:
                            act.wait_ge(s_col, q + 1)
                        for c in range(NCH):
                            for a, b in HALVES:
                                act.wait_ge(s_ps, UNITS * q + u + 1 + UNITS)
                                at = CW - 1 if n == 0 else 0
                                kw = dict(bias=bias[:, c:c + 1]) if bias is not None else {}
                                act.activation(dst[:, c, at + a:at + b], ps[u % RING][:], f, **kw).then_inc(s_ev, 1)
                                u += 1
                    act.wait_ge(s_ev, UNITS * q + UNITS + RING)
                    for c in range(NCH):
                        act.activation(aa[:, c, :], rr[:, c, :], ACT.Exp, scale=nlc[:, c:c + 1]).then_inc(s_a, 1)
                        act.wait_ge(s_a, 2 * NCH * q + 2 * c + 1)
                        act.activation(rr[:, c, :], rr[:, c, :], ACT.Tanh, scale=lc[:, c:c + 1]).then_inc(s_a, 1)
                    for c in range(NCH):
                        act.wait_ge(s_d, NCH * q + c + 1)
                        act.activation(rr[:, c, :], rr[:, c, :], ACT.Sqrt, scale=2.0).then_inc(s_m, 1)

            @block.vector
            def _(dve):
                own = Steps(dve, st.sem("dve_step"))
                TT, TS, STT = dve.tensor_tensor, dve.tensor_scalar, dve.scalar_tensor_tensor
                own(dve.memset(xr[:, :, 0:CW - 1], 0.0))
                lam = col["lru_lambda"]
                own(TS(m8[:], lam, -1.0, None, ALU.mult))
                TT(x8[:], m8[:], lam, ALU.min).then_inc(s_x8, 1)
                own(TS(m8[:], m8[:], 0.0, None, ALU.max))
                dve.wait_ge(s_x8, 2)
                own(TS(z8[:], x8[:], 2.0, None, ALU.add))
                own(dve.reciprocal(z8[:], z8[:]))
                own(TT(z8[:], z8[:], x8[:], ALU.mult))
                own(TT(q8[:], z8[:], z8[:], ALU.mult))
                own(dve.memset(sp8[:], 1.0 / 17))
                for d in range(15, 0, -2):
                    own(TT(sp8[:], sp8[:], q8[:], ALU.mult))
                    own(TS(sp8[:], sp8[:], 1.0 / d, None, ALU.add))
                own(TT(sp8[:], sp8[:], z8[:], ALU.mult))
                own(STT(out=sp8[:], in0=sp8[:], scalar=2.0, in1=m8[:], op0=ALU.mult, op1=ALU.add))
                own(TS(sp8[:], sp8[:], LRU_C, None, ALU.mult))
                own.leave(1, own.n)
                dve.sem_inc(s_done, 1)
                per = NCH * (CW - 1) + 2 + 2 * NCH + 4 * NCH - 1
                with dve.Fori(0, NB) as q:
                    own.enter(q, per)
                    at = bass.ds(NCH * q, NCH)
                    dve.tensor_copy(cw[:], col["conv_w2"].rearrange("p (j c) -> p j c", j=CW)[:, :, at])
                    for dst, name in ((cb, "conv_b2"), (ba, "lru_ba"), (bx, "lru_bx")):
                        dve.tensor_copy(dst[:], col[name][:, at])
                    dve.tensor_copy(lc[:], sp8[:, at])
                    TS(nlc[:], sp8[:, at], -1.0, None, ALU.mult).then_inc(s_col, 1)
                    dve.wait_ge(s_col, q + 1)
                    for c in range(NCH):
                        dve.wait_ge(s_ev, UNITS * q + 2 * c + 2 + RING)
                        own(TS(xa[:, c, :], xr[:, c, 0:S], cw[:, 0, c:c + 1], cb[:, c:c + 1], ALU.mult, ALU.add))
                        for j in range(1, CW):
                            ins = STT(out=xa[:, c, :], in0=xr[:, c, j:j + S], scalar=cw[:, j, c:c + 1],
                                      in1=xa[:, c, :], op0=ALU.mult, op1=ALU.add)
                            if j < CW - 1:
                                own(ins)
                            else:
                                ins.then_inc(s_xa, 1)
                    dve.wait_ge(s_ev, UNITS * q + 6 * NCH + RING)
                    own(TT(ge[:], ge[:], gt[:], ALU.mult))
                    dve.wait_ge(s_ev, UNITS * q + UNITS + RING)
                    dve.wait_ge(s_xa, NCH * q + NCH)
                    own(TT(ii[:], ii[:], xa[:], ALU.mult))
                    for c in range(NCH):
                        dve.wait_ge(s_a, 2 * NCH * q + 2 * c + 2)
                        own(TS(gt[:, c, :], rr[:, c, :], 1.0, None, ALU.add))
                        own(dve.reciprocal(gt[:, c, :], gt[:, c, :]))
                        TT(rr[:, c, :], rr[:, c, :], gt[:, c, :], ALU.mult).then_inc(s_d, 1)
                    for c in range(NCH):
                        dve.wait_ge(s_m, NCH * q + c + 1)
                        own(TT(ii[:, c, :], ii[:, c, :], rr[:, c, :], ALU.mult))
                        own(dve.tensor_tensor_scan(gt[:, c, :], aa[:, c, :], ii[:, c, :], 0.0, ALU.mult, ALU.add))
                        dst = mergedT[:, bass.ds(NCH * q + c, 1), :].rearrange("p a t -> p (a t)")
                        own(TT(ge[:, c, :], gt[:, c, :], ge[:, c, :], ALU.mult))
                        if c < NCH - 1:
                            own(TT(dst, dst, ge[:, c, :], ALU.add))
                        else:
                            TT(dst, dst, ge[:, c, :], ALU.add).then_inc(s_done, 1)
                    dve.wait_ge(s_done, q + 2)
                own.leave(NB, per)



def latents(nc, cst, col, lat, inv_l):
    parts = ((0, QL // P, QL), (QL // P, (QL + KVL) // P, KVL))
    with stage(nc, "latent") as st:
        sq = st.sb("squares", [P, (QL + KVL) // P, S])
        ms, rt = st.sb("mean", [P, NT, 2]), st.sb("root", [P, NT, 2])
        ps = st.ps("sums")
        s_sq, s_sum, s_ms, s_rt = (st.sem(n) for n in ("squared", "summed", "mean_ready", "root_ready"))
        with nc.Block() as block:
            @block.scalar
            def _(act):
                for c in range((QL + KVL) // P):
                    act.activation(sq[:, c, :], lat[:, c, :], ACT.Square).then_inc(s_sq, 1)
                act.wait_ge(s_ms, 2)
                act.activation(rt[:], ms[:], ACT.Sqrt).then_inc(s_rt, 1)

            @block.tensor
            def _(pe):
                pe.wait_ge(s_sq, (QL + KVL) // P)
                for t in range(NT):
                    for n, (a, b, _) in enumerate(parts):
                        products(pe, ps[:, 2 * t + n:2 * t + n + 1],
                                 [(sq[:, k, t * P:(t + 1) * P], cst["ones"][:, 0:1]) for k in range(a, b)]
                                 ).then_inc(s_sum, 1)

            @block.vector
            def _(dve):
                for c in range((QL + KVL) // P):
                    dve.wait_ge(s_sq, c + 1)
                    dve.tensor_scalar(lat[:, c, :], lat[:, c, :], col["latent_g"][:, c:c + 1], None, ALU.mult)
                dve.wait_ge(s_sum, 2 * NT)
                for n, (_, _, width) in enumerate(parts):
                    dve.tensor_scalar(ms[:, :, n], ps[:, 0:2 * NT].rearrange("p (t n) -> p t n", n=2)[:, :, n],
                                      1.0 / width, EPS, ALU.mult, ALU.add).then_inc(s_ms, 1)
                dve.wait_ge(s_rt, 1)
                dve.reciprocal(inv_l[:], rt[:])


def rope_tables(nc, positions, gains, tables):
    import numpy as np
    half = ROPE // 2
    freq = np.float32(10000.0) ** (-np.arange(half, dtype=np.float32) / np.float32(half))
    two_pi = 2 * np.pi
    c1 = 6.28125
    c2 = float(np.float32(np.round((two_pi - c1) * 2 ** 21) / 2 ** 21))
    c3 = float(np.float32(two_pi - c1 - c2))
    with stage(nc, "rope") as st:
        pos_i, pos = st.sb("pos_i", [P, NT], I32), st.sb("pos", [P, NT])
        fr = st.sb("freq", [P, half])
        g = st.sb("gains", [P, 2, ROPE])
        ang, k, sn, cs, ov = (st.sb(n, [P, NT, half]) for n in ("angle", "turns", "sin", "cos", "over"))
        s_in, s_r, s_trig = st.sem("loaded"), st.sem("angles_ready"), st.sem("trig_ready")
        with nc.Block() as block:
            @block.sync
            def _(sp):
                with nc.allow_non_contiguous_dma(reason="one position for each token"):
                    sp.dma_start(pos_i[:], positions.rearrange("a (t p) -> p (a t)", p=P)).then_inc(s_in, 16)
                for n in range(2):
                    sp.dma_start(g[:, n, :], gains[n][:, QKN:QKH].to_broadcast((P, ROPE))).then_inc(s_in, 16)

            @block.scalar
            def _(act):
                act.wait_ge(s_r, 1)
                act.activation(sn[:], ang[:], ACT.Sin).then_inc(s_trig, 1)
                act.wait_ge(s_r, 2)
                act.activation(cs[:], cs[:], ACT.Sin).then_inc(s_trig, 1)

            @block.vector
            def _(dve):
                own = Steps(dve, st.sem("dve_step"))
                TT, TS, STT = dve.tensor_tensor, dve.tensor_scalar, dve.scalar_tensor_tensor
                for j in range(half):
                    own(dve.memset(fr[:, j:j + 1], float(freq[j])))
                dve.wait_ge(s_in, 48)
                own(dve.tensor_copy(pos[:], pos_i[:]))
                own(TT(ang[:], pos[:, :, None].broadcast_to((P, NT, half)),
                       fr[:, None, :].broadcast_to((P, NT, half)), ALU.mult))
                own(TS(k[:], ang[:], 1.0 / two_pi, None, ALU.mult))
                own(TS(k[:], k[:], ROUND, ROUND, ALU.add, ALU.subtract))
                for c in (c1, c2, c3):
                    own(STT(out=ang[:], in0=k[:], scalar=-c, in1=ang[:], op0=ALU.mult, op1=ALU.add))
                own(TS(cs[:], ang[:], two_pi / 4, None, ALU.add))
                TS(ang[:], ang[:], 3.1415925, -3.1415925, ALU.min, ALU.max).then_inc(s_r, 1)
                own(TS(ov[:], cs[:], two_pi / 2, -two_pi, ALU.is_gt, ALU.mult))
                own(TT(cs[:], cs[:], ov[:], ALU.add))
                TS(cs[:], cs[:], 3.1415925, -3.1415925, ALU.min, ALU.max).then_inc(s_r, 1)
                dve.wait_ge(s_trig, 2)
                for n in range(2):
                    for i, (tr, h) in enumerate(((cs, 0), (sn, 1), (sn, 0), (cs, 1))):
                        gg = g[:, n, h * half:(h + 1) * half]
                        TT(tables[n][:, i], tr[:], gg[:, None, :].broadcast_to((P, NT, half)), ALU.mult)


def queries_keys_values(nc, cst, col, w_uq, w_ukv, lat, inv_l, kpe, tables, q_d, k_d, v):
    NQ, NKV = QL // P, KVL // P
    half = ROPE // 2
    QU, KU = H2 * QKH // BANK, H2 * (QKN + VH) // BANK
    NU = QU + KU
    HB = BANK // P
    KH = BANK // (QKN + VH)
    with stage(nc, "qkv") as st:
        wq = st.sb("wq", [P, NQ, H2 * QKH])
        wkv = st.sb("wkv", [P, NKV, H2 * (QKN + VH)])
        qk = [[st.sb(f"{n}{b}", [P, H2, QKH]) for b in range(2)] for n in ("q", "k")]
        sq = st.sb("squares", [P, H2, QKH])
        ss, ms, rt, iv = ([st.sb(f"{n}{i}", [P, H2]) for i in range(2)] for n in ("sums", "mean", "root", "inverse"))
        rot = [st.sb(f"rot{i}", [P, H2, half]) for i in range(4)]
        outT = [st.sb(f"outT{i}", [QKH, HB, P]) for i in range(4)]
        acc, turn = st.banks("acc", 4), st.banks("turn", 4)
        s_wq, s_wkv = st.sem("wq_loaded"), st.sem("wkv_loaded")
        s_acc = st.sem("acc_ready")
        s_q, s_kv = st.sem("q_copied"), st.sem("kv_copied")
        s_full = st.sem("k_complete")
        s_sq, s_ss, s_ms, s_rt = (st.sem(n) for n in ("squared", "summed", "mean_ready", "root_ready"))
        s_fin = st.sem("rotated")
        s_turn = st.sem("turned")
        s_out = st.sem("out_ready")
        s_st = st.sem_n("stored", 4)
        dests = (q_d.rearrange("h r s -> r h s"), k_d.rearrange("h r s -> r h s"))
        NB = H2 // HB
        with nc.Block() as block:
            @block.sync
            def _(sp):
                for k in range(NQ):
                    sp.dma_start(wq[:, k, :], w_uq[k * P:(k + 1) * P, :]).then_inc(s_wq, 16)
                for k in range(NKV):
                    sp.dma_start(wkv[:, k, :], w_ukv[k * P:(k + 1) * P, :]).then_inc(s_wkv, 16)
                for t in range(NT):
                    for m in range(2 * NB):
                        g = 2 * NB * t + m
                        sp.wait_ge(s_out, g + 1)
                        sp.dma_start(dests[m // NB][:, HB * (m % NB):HB * (m % NB + 1), t * P:(t + 1) * P],
                                     outT[g % 4][:]).then_inc(s_st[g % 4], 16)
                for n in range(4):
                    sp.wait_ge(s_st[n], 16 * 2 * NB * NT // 4)

            @block.tensor
            def _(pe):
                def project(t):
                    for u in range(NU):
                        g = NU * t + u
                        if g == 0:
                            pe.wait_ge(s_wq, 16 * NQ)
                        if g == QU:
                            pe.wait_ge(s_wkv, 16 * NKV)
                        if g >= 4:
                            t0, u0 = divmod(g - 4, NU)
                            if u0 < QU:
                                pe.wait_ge(s_q, QU * t0 + u0 + 1)
                            else:
                                pe.wait_ge(s_kv, 2 * (KU * t0 + u0 - QU + 1))
                        if u < QU:
                            pairs = [(lat[:, k, t * P:(t + 1) * P], wq[:, k, u * BANK:(u + 1) * BANK])
                                     for k in range(NQ)]
                        else:
                            pairs = [(lat[:, NQ + k, t * P:(t + 1) * P],
                                      wkv[:, k, (u - QU) * BANK:(u - QU + 1) * BANK]) for k in range(NKV)]
                        products(pe, acc[g % 4][:], pairs).then_inc(s_acc, 1)

                def turn_heads(t, i):
                    pe.wait_ge(s_fin, 2 * t + i + 1)
                    for m in range(NB):
                        g = 2 * NB * t + NB * i + m
                        if g >= 4:
                            pe.wait_ge(s_out, g - 3)
                        for h in range(HB):
                            last = pe.transpose(turn[g % 4][0:QKH, h * P:(h + 1) * P], qk[i][t % 2][:, HB * m + h, :],
                                                cst["ident"][:])
                        last.then_inc(s_turn, 1)

                for t in range(NT + 1):
                    if t < NT:
                        project(t)
                    if t:
                        turn_heads(t - 1, 0)
                        turn_heads(t - 1, 1)

            @block.scalar
            def _(act):
                def copy_heads(t):
                    for m in range(2 * NB):
                        g = 2 * NB * t + m
                        act.wait_ge(s_turn, g + 1)
                        if g >= 4:
                            act.wait_ge(s_st[g % 4], 16 * (g // 4))
                        act.activation(outT[g % 4][:].rearrange("p h t -> p (h t)"), turn[g % 4][0:QKH, :], ACT.Copy,
                                       scale=col["qk_g"][0:QKH, m // NB:m // NB + 1]).then_inc(s_out, 1)

                for t in range(NT):
                    for u in range(QU):
                        act.wait_ge(s_acc, NU * t + u + 1)
                        if t >= 2:
                            act.wait_ge(s_turn, 2 * NB * (t - 1))
                        act.activation(qk[0][t % 2][:].rearrange("p h d -> p (h d)")[:, u * BANK:(u + 1) * BANK],
                                       acc[(NU * t + u) % 4][:], ACT.Copy, scale=inv_l[:, t, 0:1]).then_inc(s_q, 1)
                    act.wait_ge(s_q, QU * t + QU)
                    if t:
                        act.wait_ge(s_ss, 2 * t)
                    act.activation(sq[:], qk[0][t % 2][:], ACT.Square).then_inc(s_sq, 1)
                    act.wait_ge(s_full, t + 1)
                    act.wait_ge(s_ss, 2 * t + 1)
                    act.activation(sq[:], qk[1][t % 2][:], ACT.Square).then_inc(s_sq, 1)
                    for i in range(2):
                        act.wait_ge(s_ms, 2 * t + i + 1)
                        act.activation(rt[i][:], ms[i][:], ACT.Sqrt).then_inc(s_rt, 1)
                    if t:
                        copy_heads(t - 1)
                copy_heads(NT - 1)

            @block.vector
            def _(dve):
                own = Steps(dve, st.sem("dve_step"))
                TT, TS = dve.tensor_tensor, dve.tensor_scalar
                for t in range(NT):
                    if t >= 2:
                        dve.wait_ge(s_turn, 2 * NB * (t - 1))
                    q_k = [qk[i][t % 2] for i in range(2)]
                    for u in range(KU):
                        dve.wait_ge(s_acc, NU * t + QU + u + 1)
                        kv = acc[(NU * t + QU + u) % 4][:].rearrange("p (h d) -> p h d", h=KH)
                        TS(q_k[1][:, KH * u:KH * (u + 1), 0:QKN], kv[:, :, 0:QKN], inv_l[:, t, 1:2], None,
                           ALU.mult).then_inc(s_kv, 1)
                        TS(v[:, t, KH * u * VH:KH * (u + 1) * VH].rearrange("p (h d) -> p h d", h=KH),
                           kv[:, :, QKN:], inv_l[:, t, 1:2], None, ALU.mult).then_inc(s_kv, 1)
                    dve.tensor_copy(q_k[1][:, :, QKN:QKH],
                                    kpe[:, t, None, :].broadcast_to((P, H2, ROPE))).then_inc(s_full, 1)
                    for i in range(2):
                        dve.wait_ge(s_sq, 2 * t + i + 1)
                        dve.tensor_reduce(ss[i][:], sq[:], AX.X, ALU.add).then_inc(s_ss, 1)
                        dve.wait_ge(s_ss, 2 * t + i + 1)
                        TS(ms[i][:], ss[i][:], 1.0 / QKH, EPS, ALU.mult, ALU.add).then_inc(s_ms, 1)
                    for i in range(2):
                        dve.wait_ge(s_rt, 2 * t + i + 1)
                        own(dve.reciprocal(iv[i][:], rt[i][:]))
                        own(TT(q_k[i][:], q_k[i][:], iv[i][:, :, None].broadcast_to((P, H2, QKH)), ALU.mult))
                        x1, x2 = q_k[i][:, :, QKN:QKN + half], q_k[i][:, :, QKN + half:QKH]
                        for n, (x, tab) in enumerate(((x1, 0), (x2, 1), (x1, 2), (x2, 3))):
                            last = TT(rot[n][:], x, tables[i][:, tab, t, None, :].broadcast_to((P, H2, half)), ALU.mult)
                            own(last)
                        own(TT(x1, rot[0][:], rot[1][:], ALU.subtract))
                        TT(x2, rot[2][:], rot[3][:], ALU.add).then_inc(s_fin, 1)
                        dve.wait_ge(s_fin, 2 * t + i + 1)


def gate_in_place(nc, w_in, c0, uT, oT):
    src = chunked(w_in)
    with stage(nc, "merge2") as st:
        wg = [st.sb(f"wg{p}", [P, KD, P]) for p in range(2)]
        sg = [st.sb(f"gate{u}", [P, BANK]) for u in range(4)]
        ps = st.banks("gates", 4)
        s_w = st.sem_n("w_loaded")
        s_g = st.sem("gates_ready")
        s_sg = st.sem("gate_ready")
        s_done = st.sem("gated")
        with nc.Block() as block:
            @block.sync
            def _(sp):
                with sp.Fori(0, KD // 2) as i:
                    for p in range(2):
                        sp.wait_ge(s_g, 2 * (2 * i + p + 1))
                        sp.dma_start(wg[p][:], src[:, :, bass.ds(c0 + P * (2 * i + p), P)]).then_inc(s_w[p], 16)

            @block.tensor
            def _(pe):
                pe.sem_inc(s_g, 4)
                with pe.Fori(0, KD // 2) as i:
                    for p in range(2):
                        pe.wait_ge(s_w[p], 16 * i + 16)
                        for h, (a, b) in enumerate(HALVES):
                            pe.wait_ge(s_done, 4 * i + 2 * p + h + 1)
                            products(pe, ps[2 * p + h][:], [(wg[p][:, k, :], uT[:, k, a:b]) for k in range(KD)]
                                     ).then_inc(s_g, 1)

            @block.scalar
            def _(act):
                with act.Fori(0, KD // 2) as i:
                    for u in range(4):
                        act.wait_ge(s_g, 4 * i + u + 5)
                        act.activation(sg[u][:], ps[u][:], ACT.Sigmoid).then_inc(s_sg, 1)

            @block.vector
            def _(dve):
                dve.sem_inc(s_done, 4)
                with dve.Fori(0, KD // 2) as i:
                    for u in range(4):
                        p, (a, b) = u // 2, HALVES[u % 2]
                        o = oT[:, bass.ds(2 * i + p, 1), a:b].rearrange("p c t -> p (c t)")
                        dve.wait_ge(s_sg, 4 * i + u + 1)
                        dve.tensor_tensor(o, sg[u][:], o, ALU.mult).then_inc(s_done, 1)



def routing_results(st, experts):
    NB = block_count(experts)
    return dict(weights=st.sb("weights", [P, 2, NT]), slots=st.sb("slots", [P, 2, NT], U32),
                pairs=st.sb("pairs", [1, 1], I32), expert=st.sb("expert", [1, NB], I32),
                token=st.sb("token", [P, NB], U32))


def moe(nc, cst, name, experts, logits, w1, w3, w2, h_d, v_d, g_row, out_d):
    NB = block_count(experts)
    ids_d = nc.dram_tensor(f"{name}_ids", (NB * P, 1), F32).ap()
    y_d = nc.dram_tensor(f"{name}_y", ((NB + 2) * P, D), F32).ap()
    with stage(nc, name) as st:
        r = routing_results(st, experts)
        route_tokens(nc, cst, f"{name}_route", experts, logits, ids_d, r)
        run_experts(nc, cst, f"{name}_run", experts, w1, w3, w2, v_d, y_d, r)
        combine(nc, f"{name}_sum", r, h_d, y_d, g_row, out_d)


def first_block(nc, cst, col, a, x2_d):
    h_d = nc.dram_tensor("h1", (S, D), F32).ap()
    v_d = nc.dram_tensor("v1", (S, D), F32).ap()
    negf_d = nc.dram_tensor("neg_f", (H1, T1), F32).ap()
    x = a["x"][0]
    w_in = a["w_in"][0]
    with stage(nc, "block1") as st:
        logits = st.sb("logits", [P, NT, NG + NE1])
        with ExitStack() as inner:
            def sb(name, shape, dt=F32):
                return inner.enter_context(nc.sbuf_tensor(name, shape, dt))
            uT = sb("uT1", [P, KD, T1])
            pT = sb("pT1", [P, 14, T1])
            oT = sb("oT1", [P, 4, S])
            norm_to_features(nc, cst, "norm1", [(a["meta"], META)] + [(x[t * P:(t + 1) * P, :], P) for t in range(NT)],
                             col["norm1_g"], uT, 0)
            project_features(nc, "proj1", w_in, 0, 14, uT, PIECES1, pT)
            forget_sums(nc, w_in, a["b_forget"], uT, negf_d)
            pool_and_conv(nc, cst, col, a["pool_w"][0], pT)
            with nc.sbuf_tensor("v1_tokens", [P, -(-T1 // P), H1 * DH], F32) as v:
                project_tokens(nc, "v1p", w_in, C_V1, H1 * DH, uT,
                               [(t * P, min(P, T1 - t * P)) for t in range(-(-T1 // P))], v)

                def load_head(sp, p, j, q_aug, k_aug, sem):
                    rows = slice(DH * p, DH * p + DH)
                    sp.dma_start(q_aug[0:DH, :], pT[rows, bass.ds(6 + j, 1), META:T1].rearrange("p c t -> p (c t)")).then_inc(sem, 16)
                    sp.dma_start(k_aug[0:DH, :], pT[rows, bass.ds(10 + j, 1), :].rearrange("p c t -> p (c t)")).then_inc(sem, 16)
                    sp.dma_start(k_aug[DH:DH + 1, :], negf_d[bass.ds(2 * j + p, 1), :]).then_inc(sem, 16)

                attention(nc, cst, "fox", H1, META, DH, cst["causal"], load_head, 3, v, oT, 1)
            mergedT = pT[:, 6:14, 0:S]
            merge_branches(nc, w_in, [a["w_out_a"][0], a["w_out_b"][0], a["w_out_c"][0]],
                           lambda k, x0, x1: uT[:, k, META + x0:META + x1],
                           [(lambda k, x0, x1: pT[:, k, META + x0:META + x1], 2),
                            (lambda k, x0, x1: pT[:, 2 + k, META + x0:META + x1], 2),
                            (lambda k, x0, x1: oT[:, k, x0:x1], 4)], mergedT)
            output_and_router(nc, cst, "out1", mergedT, a["w_o"][0], x, a["norm2_g"],
                              (a["router_g"][0], a["router_e"][0]), (a["router_g_b"], a["router_e_b"]),
                              h_d, v_d, logits)
        moe(nc, cst, "moe1", NE1, logits, a["exp_w1"][0], a["exp_w3"][0], a["exp_w2"][0], h_d, v_d,
            a["final_g"].rearrange("(a d) -> a d", a=1), x2_d)


def second_block(nc, cst, col, a, x_d, out):
    h_d = nc.dram_tensor("h2", (S, D), F32).ap()
    v_d = nc.dram_tensor("v2", (S, D), F32).ap()
    q_d = nc.dram_tensor("q2", (H2, QKH, S), F32).ap()
    k_d = nc.dram_tensor("k2", (H2, QKH, S), F32).ap()
    w_in = a["w_in_2"][0]
    with stage(nc, "block2") as st:
        logits = st.sb("logits", [P, NT, NG + NE2])
        merged_mem = ExitStack()
        oT = lat = merged_mem.enter_context(nc.sbuf_tensor("latents_then_oT2", [P, KD, S], F32))
        with ExitStack() as inner:
            def sb(name, shape, dt=F32):
                return inner.enter_context(nc.sbuf_tensor(name, shape, dt))
            uT = sb("uT2", [P, KD, S])
            norm_to_features(nc, cst, "norm3", [(x_d[t * P:(t + 1) * P, :], P) for t in range(NT)],
                             col["norm_mix_g"], uT, 0)
            v_mem = ExitStack()
            v = v_mem.enter_context(nc.sbuf_tensor("v2_tokens", [P, NT, H2 * VH], F32))
            with ExitStack() as latent_mem:
                def sbl(name, shape, dt=F32):
                    return latent_mem.enter_context(nc.sbuf_tensor(name, shape, dt))
                kpe = sbl("k_pe", [P, NT, ROPE])
                inv_l = sbl("inv_latent", [P, NT, 2])
                tables = [sbl(f"rope_{n}", [P, 4, NT, ROPE // 2]) for n in "qk"]
                project_features(nc, "proj2", w_in, C_QC, (QL + KVL) // P, uT, HALVES, lat)
                project_tokens(nc, "kpep", w_in, C_KPE, ROPE, uT, [(t * P, P) for t in range(NT)], kpe)
                latents(nc, cst, col, lat, inv_l)
                rope_tables(nc, a["positions_2"], (a["q_norm_g_2"], a["k_norm_g_2"]), tables)
                queries_keys_values(nc, cst, col, a["w_uq_2"][0], a["w_ukv_2"][0], lat, inv_l, kpe, tables,
                                    q_d, k_d, v)


            def load_head(sp, p, j, q_aug, k_aug, sem):
                for dst, src in ((q_aug, q_d), (k_aug, k_d)):
                    sp.dma_start(dst[0:QKH, :], src[bass.ds(2 * j + p, 1)].rearrange("a r s -> (a r) s")).then_inc(sem, 16)

            attention(nc, cst, "mla", H2, 0, QKH, cst["chunk"], load_head, 2, v, oT, 0)
            v_mem.close()
            gate_in_place(nc, w_in, C_GT + D, uT, oT)
            recurrent_branch(nc, cst, col, w_in, a["lru_wa_2"][0], a["lru_wx_2"][0], uT, oT)
        output_and_router(nc, cst, "out2", oT, a["w_out_2"][0], x_d, a["norm_ffn_g_2"],
                          (a["router_group_w_2"][0], a["router_expert_w_2"][0]),
                          (a["router_group_b_2"], a["router_expert_b_2"]), h_d, v_d, logits)
        merged_mem.close()
        moe(nc, cst, "moe2", NE2, logits, a["w_gate_2"][0], a["w_up_2"][0], a["w_down_2"][0], h_d, v_d,
            None, out)


def program(nc, a, out):
    x2_d = nc.dram_tensor("x2", (S, D), F32).ap()
    vectors = [("norm1_g", a["norm1_g"][0]), ("pool_b", a["pool_b"][0].rearrange("g c -> (g c)")),
               ("pool_scale", a["pool_scale"][0]), ("conv_w", a["conv_w"][0].rearrange("j c -> (j c)")),
               ("conv_b", a["conv_b"][0]), ("conv_ln_g", a["conv_ln_g"][0]), ("conv_ln_b", a["conv_ln_b"][0]),
               ("norm_mix_g", a["norm_mix_g_2"][0]), ("conv_w2", a["conv_w_2"][0].rearrange("j c -> (j c)")),
               ("conv_b2", a["conv_b_2"][0]), ("lru_ba", a["lru_ba_2"][0]), ("lru_bx", a["lru_bx_2"][0]),
               ("lru_lambda", a["lru_lambda_2"][0])]
    rows = [(n, row_of(ap, ap.shape[0] // P), ap.shape[0] // P, P) for n, ap in vectors]
    rows += [("latent_g", row_of(a["q_a_g_2"][0], QL // P), QL // P, P),
             ("kv_a_g", row_of(a["kv_a_g_2"][0], KVL // P), KVL // P, P),
             ("qk_g", a["q_norm_g_2"][:, 0:QKN], 1, QKN), ("k_g", a["k_norm_g_2"][:, 0:QKN], 1, QKN)]
    with stage(nc, "all") as st:
        cst, col = constants(nc, st, rows)
        first_block(nc, cst, col, a, x2_d)
        second_block(nc, cst, col, a, x2_d, out.rearrange("a s d -> (a s) d"))


def kernel(**inputs):
    import concourse.bacc as bacc
    import numpy as np
    from concourse.bass_utils import run_bass_kernel_spmd

    nc = bacc.Bacc("TRN2", target_bir_lowering=False, num_devices=1)
    arrays = {name: np.ascontiguousarray(a) for name, a in inputs.items()}
    handles = {name: nc.dram_tensor(name, a.shape, mybir.dt.from_np(a.dtype), kind="ExternalInput").ap()
               for name, a in arrays.items()}
    out = nc.dram_tensor("out", (1, S, D), F32, kind="ExternalOutput").ap()
    program(nc, handles, out)
    r = run_bass_kernel_spmd(nc, [arrays], core_ids=[0])
    return r.results[0]["out"]
```

```python
from contextlib import ExitStack, contextmanager

import concourse.bass as bass
from concourse import mybir

F32 = mybir.dt.float32
F32R = mybir.dt.float32r
BF16 = mybir.dt.bfloat16
I32 = mybir.dt.int32
U32 = mybir.dt.uint32
ALU = mybir.AluOpType
ACT = mybir.ActivationFunctionType
AX = mybir.AxisListType

P = 128
D = 1024
KD = D // P
S = 1024
NT = S // P
META = 16
BANK = 512
HALVES = [(0, BANK), (BANK, S)]
EPS = 1e-6
MASKED = -1e30
ROUND = 12582912.0

POOL_W, CONV_W1, TAPS = 256, 256, 31
C_Q1, C_K1, C_V1, C_FG, C_G1 = 768, 1280, 1792, 2304, 2312
H1, DH = 8, 64
T1 = S + META
AT_A, AT_BV, AT_Q, AT_K, AT_BG = 0, 2, 4, 8, 12
RUNS_MIX = [(0, AT_A, 4), (4, AT_BG, 2)]
RUNS_QK = [(6, AT_Q, 4, DH ** -0.5), (10, AT_K, 4, 1.0)]
PIECES1 = [(0, 352), (352, 704), (704, T1)]
NE1 = 16
C_XR, C_GR, C_QC, C_KPE, C_GT = 0, 1024, 2048, 3072, 3104
QL, KVL, ROPE = 768, 256, 32
H2, QKN, QKH, VH = 16, 64, 96, 64
LRU_C = 8.0
NE2 = 32
NG = 4
HID = 256
ONE_ROW = 96


class Steps:

    def __init__(self, eng, sem):
        self.eng, self.sem, self.total, self.base, self.n = eng, sem, 0, 0, 0

    def __call__(self, ins):
        ins.then_inc(self.sem, 1)
        self.n += 1
        self.eng.wait_ge(self.sem, self.base + self.n)

    def enter(self, i, per):
        self.base, self.n = i * per + self.total, 0

    def leave(self, passes, per):
        assert self.n == per, (self.n, per)
        self.total += passes * per
        self.base, self.n = self.total, 0


class Stage:

    def __init__(self, nc, name, ctx):
        self.nc, self.name, self.ctx, self.sems = nc, name, ctx, []

    def sb(self, name, shape, dt=F32):
        return self.ctx.enter_context(self.nc.sbuf_tensor(f"{self.name}_{name}", shape, dt))

    def ps(self, name, shape=(P, BANK), dt=F32):
        return self.ctx.enter_context(self.nc.psum_tensor(f"{self.name}_{name}", list(shape), dt))

    def banks(self, name, n):
        return [self.ps(f"{name}{i}") for i in range(n)]

    def sem(self, name):
        s = self.nc.alloc_semaphore(f"{self.name}_{name}")
        self.sems.append(s)
        return s

    def sem_n(self, name, n=2):
        return [self.sem(f"{name}{i}") for i in range(n)]


@contextmanager
def stage(nc, name):
    with ExitStack() as ctx:
        st = Stage(nc, name, ctx)
        yield st
    if st.sems:
        nc.clear_and_free_semaphores(st.sems)
        nc.all_engine_barrier()


def products(pe, out, pairs):
    for n, (lhsT, rhs) in enumerate(pairs):
        last = pe.matmul(out, lhsT, rhs, start=(n == 0), stop=(n == len(pairs) - 1))
    return last


def split_products(pe, out, pairs):
    n = 3 * len(pairs)
    k = 0
    for (lh, ll), (rh, rl) in pairs:
        for a, b in ((lh, rh), (lh, rl), (ll, rh)):
            last = pe.matmul(out, a, b, start=(k == 0), stop=(k == n - 1))
            k += 1
    return last


def split(eng, own, raw, high, low, step=False):
    if step:
        eng.sem_inc(own.sem, 1)
        own.n += 1
    own(eng.tensor_copy(high, raw))
    return eng.tensor_tensor(low, raw, high.bitcast(F32), ALU.subtract)


def row_of(ap, n):
    return ap.rearrange("(c p) -> c p", c=n)


def chunked(ap):
    return ap.rearrange("(c p) n -> p c n", p=P)



def constants(nc, st0, rows):
    ident = st0.sb("ident", [P, P])
    identb = st0.sb("identb", [P, P], BF16)
    ones = st0.sb("ones", [P, P])
    zeros = st0.sb("zeros", [P, 1])
    causal_qk = st0.sb("causal_qk", [P, P], BF16)
    causal_kq = st0.sb("causal_kq", [P, P], BF16)
    chunk_qk = st0.sb("chunk_qk", [P, P], BF16)
    chunk_kq = st0.sb("chunk_kq", [P, P], BF16)
    groups = [[], []]
    used = [0, 0]
    where = {}
    for name, ap, n, w in rows:
        g = 0 if used[0] + n <= P else 1
        groups[g].append((used[g], n, w, ap))
        where[name] = (g, used[g], n)
        used[g] += n
        assert used[g] <= P
    cols = [st0.sb(f"cols{g}", [P, P]) for g in range(2)]
    with stage(nc, "const") as st:
        stack = [st.sb(f"stack{g}", [P, P]) for g in range(2)]
        turned = [st.ps(f"turned{g}", (P, P)) for g in range(2)]
        s_zero = st.sem("zeroed")
        s_rows = st.sem("rows_loaded")
        s_one = st.sem("ident_ready")
        s_turn = st.sem("turned")
        s_cols = st.sem("cols_ready")
        with nc.Block() as block:
            @block.vector
            def _(dve):
                for g in range(2):
                    dve.memset(stack[g][:], 0.0).then_inc(s_zero, 1)
                dve.memset(ones[:], 1.0)
                dve.memset(zeros[:], 0.0)
                dve.memset(chunk_qk[:], 0.0).then_inc(s_cols, 1)
                dve.memset(chunk_kq[:], 0.0).then_inc(s_cols, 1)
                dve.wait_ge(s_cols, 2)
                dve.memset(chunk_qk[0:64, 64:P], MASKED)
                dve.memset(chunk_kq[64:P, 0:64], MASKED)
                for g in range(2):
                    dve.wait_ge(s_turn, g + 1)
                    dve.tensor_copy(cols[g][:], turned[g][:]).then_inc(s_cols, 1)
                dve.wait_ge(s_cols, 4)
                g, at, _ = where["qk_g"]
                qk = cols[g][:, at:at + 2]
                dve.memset(qk[QKN:QKH, :], 1.0).then_inc(s_cols, 1)
                dve.wait_ge(s_cols, 5)
                dve.tensor_scalar(qk[:, 0:1], qk[:, 0:1], float(QKH) ** -0.5, None, ALU.mult)

            @block.sync
            def _(sp):
                sp.wait_ge(s_zero, 2)
                for g in range(2):
                    for at, n, w, ap in groups[g]:
                        sp.dma_start(stack[g][at:at + n, 0:w], ap).then_inc(s_rows, 16)

            @block.gpsimd
            def _(pool):
                own = Steps(pool, st.sem("pool_step"))
                own(pool.memset(ident[:], 0.0))
                pool.affine_select(out=ident[:], in_=ident[:], compare_op=ALU.not_equal, fill=1.0,
                                   base=0, pattern=[[-1, P]], channel_multiplier=1).then_inc(s_one, 1)
                pool.wait_ge(s_one, 1)
                pool.tensor_copy(identb[:], ident[:])
                own(pool.memset(causal_qk[:], 0.0))
                pool.affine_select(out=causal_qk[:], in_=causal_qk[:], compare_op=ALU.is_ge,
                                   fill=MASKED, base=0, pattern=[[-1, P]], channel_multiplier=1)
                own(pool.memset(causal_kq[:], 0.0))
                pool.affine_select(out=causal_kq[:], in_=causal_kq[:], compare_op=ALU.is_ge,
                                   fill=MASKED, base=0, pattern=[[1, P]], channel_multiplier=-1)

            @block.tensor
            def _(pe):
                pe.wait_ge(s_one, 1)
                pe.wait_ge(s_rows, 16 * len(rows))
                for g in range(2):
                    pe.transpose(turned[g][:], stack[g][:], ident[:]).then_inc(s_turn, 1)
    out = {}
    for name, (g, at, n) in where.items():
        out[name] = cols[g][:, at:at + n]
    g, at, _ = where["qk_g"]
    out["qk_g"] = cols[g][:, at:at + 2]
    g, at, n = where["latent_g"]
    assert where["kv_a_g"][:2] == (g, at + n) and where["k_g"][:2] == (where["qk_g"][0], where["qk_g"][1] + 1)
    out["latent_g"] = cols[g][:, at:at + (QL + KVL) // P]
    return dict(ident=ident, identb=identb, ones=ones, zeros=zeros,
                causal=(causal_qk, causal_kq), chunk=(chunk_qk, chunk_kq)), out



def norm_to_features(nc, cst, name, load, g_row, uT, first, prefetch):
    n = len(load)
    R = 4
    with stage(nc, name) as st:
        x = [st.sb(f"x{t}", [P, D]) for t in range(R)]
        g = st.sb("gains", [P, D])
        junk = st.sb("squares", [P, D])
        ss = st.sb("sums", [P, n])
        ms = st.sb("mean", [P, n])
        root = st.sb("root", [P, n])
        inv = st.sb("inverse", [P, n])
        turn = [st.banks(f"turn{q}_", 2) for q in range(2)]
        s_g = st.sem("gain_loaded")
        s_pre = st.sem("prefetched")
        s_x = st.sem_n("x_loaded", R)
        s_sum = st.sem("sums_ready")
        s_mean = st.sem("mean_ready")
        s_root = st.sem("root_ready")
        s_inv = st.sem("inverse_ready")
        s_norm = st.sem("tile_scaled")
        s_turn = st.sem("turned")
        s_high = st.sem("high_copied")
        s_low = st.sem("low_ready")
        with nc.Block() as block:
            @block.sync
            def _(sp):
                for t, (ap, rows) in enumerate(load):
                    if t == 1:
                        sp.dma_start(g[:], g_row.to_broadcast((P, D))).then_inc(s_g, 16)
                    if t == R:
                        with nc.allow_non_contiguous_dma(reason="narrow operands"):
                            for dst, src in prefetch:
                                sp.dma_start(dst, src).then_inc(s_pre, 16)
                    if t >= R:
                        sp.wait_ge(s_turn, 2 * (t - R) + 2)
                    sp.dma_start(x[t % R][0:rows, :], ap).then_inc(s_x[t % R], 16)
                sp.wait_ge(s_pre, 16 * len(prefetch))

            def halves(t):
                rows = load[t][1]
                at = first + sum(r for _, r in load[:t])
                for h in range(2):
                    src = turn[t % 2][h][:].rearrange("p (c t) -> p c t", c=4)[:, :, 0:rows]
                    yield h, src, uT[0][:, 4 * h:4 * h + 4, at:at + rows], uT[1][:, 4 * h:4 * h + 4, at:at + rows]

            @block.scalar
            def _(act):
                def squares(t):
                    rows = load[t][1]
                    act.wait_ge(s_x[t % R], 16 * (t // R) + 16)
                    if t:
                        act.wait_ge(s_sum, t)
                    act.activation(junk[0:rows, :], x[t % R][0:rows, :], ACT.Square,
                                   accum_out=ss[0:rows, t:t + 1]).then_inc(s_sum, 1)

                squares(0)
                for t in range(n + 1):
                    if t + 1 < n:
                        squares(t + 1)
                    if t < n:
                        rows = load[t][1]
                        act.wait_ge(s_mean, t + 1)
                        act.activation(root[0:rows, t:t + 1], ms[0:rows, t:t + 1], ACT.Sqrt).then_inc(s_root, 1)
                    if t:
                        for h, src, high, low in halves(t - 1):
                            act.wait_ge(s_turn, 2 * (t - 1) + h + 1)
                            act.copy(high, src).then_inc(s_high, 1)

            @block.vector
            def _(dve):
                def mean(t):
                    rows = load[t][1]
                    dve.wait_ge(s_sum, t + 1)
                    dve.tensor_scalar(ms[0:rows, t:t + 1], ss[0:rows, t:t + 1], 1.0 / D, EPS, ALU.mult,
                                      ALU.add).then_inc(s_mean, 1)

                mean(0)
                for t in range(n + 1):
                    if t < n:
                        rows = load[t][1]
                        at = slice(t, t + 1)
                        if t + 1 < n:
                            mean(t + 1)
                        dve.wait_ge(s_root, t + 1)
                        dve.reciprocal(inv[0:rows, at], root[0:rows, at]).then_inc(s_inv, 1)
                        if t == 0:
                            dve.wait_ge(s_g, 16)
                        dve.wait_ge(s_inv, t + 1)
                        dve.scalar_tensor_tensor(out=x[t % R][0:rows, :], in0=x[t % R][0:rows, :],
                                                 scalar=inv[0:rows, at], in1=g[0:rows, :], op0=ALU.mult,
                                                 op1=ALU.mult).then_inc(s_norm, 1)
                    if t:
                        for h, src, high, low in halves(t - 1):
                            dve.wait_ge(s_high, 2 * (t - 1) + h + 1)
                            dve.tensor_tensor(low, src, high.bitcast(F32), ALU.subtract).then_inc(s_low, 1)

            @block.tensor
            def _(pe):
                for t, (_, rows) in enumerate(load):
                    pe.wait_ge(s_norm, t + 1)
                    for h in range(2):
                        if t >= 2:
                            pe.wait_ge(s_low, 2 * (t - 2) + h + 1)
                        for c in range(4):
                            f = 4 * h + c
                            last = pe.transpose(turn[t % 2][h][:, c * P:c * P + rows],
                                                x[t % R][0:rows, f * P:(f + 1) * P],
                                                cst["ident"][0:rows, 0:rows])
                        last.then_inc(s_turn, 1)


def project_features(nc, name, w, c0, runs, uT, pieces, out, spill=(), along=None):
    src = chunked(w)
    npc = len(pieces)
    share = [(npc + 1) // 2, npc // 2]
    with stage(nc, name) as st:
        raw = [st.sb(f"raw{p}", [P, KD, P]) for p in range(2)]
        wb = [[st.sb(f"w_{n}{p}", [P, KD, P], F32R) for n in ("high", "low")] for p in range(2)]
        acc = [st.banks(f"acc{p}_", npc) for p in range(2)]
        s_raw = st.sem_n("w_loaded")
        s_w = st.sem_n("w_split")
        s_acc = st.sem_n("acc_ready")
        s_free = [st.sem_n("free_by_dve"), st.sem_n("free_by_act")]
        s_spill = st.sem("spilled")
        other = along(st) if along else {}

        def passes(eng, body):
            done = 0
            for f, o, n in runs:
                with eng.Fori(0, n // 2) as i:
                    body(i + done, 2 * i + f, 2 * i + o)
                done += n // 2

        with nc.Block() as block:
            @block.sync
            def _(sp):
                def load(i, f, o):
                    for p in range(2):
                        at = f * P + (c0 + P * p)
                        sp.wait_ge(s_w[p], i + 1)
                        sp.dma_start(raw[p][:], src[:, :, bass.ds(at, P)]).then_inc(s_raw[p], 16)
                passes(sp, load)
                for dst, kept in spill:
                    sp.dma_start(dst, kept).then_inc(s_spill, 16)
                if spill:
                    sp.wait_ge(s_spill, 16 * len(spill))
                if "sync_end" in other:
                    other["sync_end"](sp)

            @block.gpsimd
            def _(pool):
                own = Steps(pool, st.sem("pool_step"))
                for p in range(2):
                    pool.sem_inc(s_w[p], 1)

                def split_weights(i, f, o):
                    own.enter(i, 2 * 2)
                    for p in range(2):
                        pool.wait_ge(s_raw[p], 16 * i + 16)
                        pool.wait_ge(s_acc[p], npc * i + 1)
                        split(pool, own, raw[p][:], wb[p][0][:], wb[p][1][:], True).then_inc(s_w[p], 1)
                passes(pool, split_weights)
                own.leave(sum(n // 2 for _, _, n in runs), 4)

            @block.tensor
            def _(pe):
                if "tensor" in other:
                    other["tensor"](pe)
                for p in range(2):
                    pe.sem_inc(s_acc[p], 1)

                def multiply(i, f, o):
                    for p in range(2):
                        pe.wait_ge(s_w[p], i + 2)
                        for n, (a, b) in enumerate(pieces):
                            pe.wait_ge(s_free[n % 2][p], share[n % 2] * i + n // 2 + 1)
                            split_products(pe, acc[p][n][:, 0:b - a],
                                           [([w[:, k, :] for w in wb[p]], [u[:, k, a:b] for u in uT])
                                            for k in range(KD)]).then_inc(s_acc[p], 1)
                passes(pe, multiply)
                if "tensor_end" in other:
                    other["tensor_end"](pe)

            def copy_out(eng, e):
                for p in range(2):
                    eng.sem_inc(s_free[e][p], share[e])

                def copies(i, f, o):
                    for p in range(2):
                        for n in range(e, npc, 2):
                            a, b = pieces[n]
                            eng.wait_ge(s_acc[p], npc * i + n + 2)
                            dst = out[:, bass.ds(o + p, 1), a:b].rearrange("p a t -> p (a t)")
                            if e:
                                ins = eng.copy(dst, acc[p][n][:, 0:b - a])
                            else:
                                ins = eng.tensor_copy(dst, acc[p][n][:, 0:b - a])
                            ins.then_inc(s_free[e][p], 1)
                passes(eng, copies)

            @block.vector
            def _(dve):
                if "vector" in other:
                    other["vector"](dve)
                copy_out(dve, 0)
                if "vector_end" in other:
                    other["vector_end"](dve)

            @block.scalar
            def _(act):
                if "scalar" in other:
                    other["scalar"](act)
                copy_out(act, 1)



def forget_sums(raw, bias, uT, neg_f):
    def along(st):
        wb = [st.sb(f"forget_w_{n}", [P, KD, H1], F32R) for n in ("high", "low")]
        z, e, neg, one = (st.sb(f"forget_{n}", [H1, T1]) for n in ("z", "e", "neg", "one"))
        acc = st.banks("forget_acc", 2)
        s_w = st.sem("forget_w_split")
        s_acc = st.sem("forget_acc_ready")
        s_z = st.sem("forget_z_ready")
        s_e = st.sem("exponent_ready")
        s_ln = st.sem("log_ready")
        s_neg = st.sem("sums_ready")
        s_out = st.sem("sums_stored")
        s_step = st.sem("dve_step")

        def sync_end(sp):
            sp.wait_ge(s_neg, 1)
            sp.dma_start(neg_f, neg[:]).then_inc(s_out, 16)
            sp.wait_ge(s_out, 16)

        def tensor(pe):
            pe.wait_ge(s_w, 1)
            for n, (a, b) in enumerate(PIECES1):
                if n == 2:
                    pe.wait_ge(s_z, 1)
                split_products(pe, acc[n % 2][0:H1, 0:b - a],
                               [([w[:, k, :] for w in wb], [u[:, k, a:b] for u in uT])
                                for k in range(KD)]).then_inc(s_acc, 1)

        def vector(dve):
            own = Steps(dve, s_step)
            dve.memset(one[:], 1.0)
            split(dve, own, raw[:], wb[0][:], wb[1][:]).then_inc(s_w, 1)
            for n, (a, b) in enumerate(PIECES1):
                dve.wait_ge(s_acc, n + 1)
                dve.tensor_scalar(z[:, a:b], acc[n % 2][0:H1, 0:b - a], bias[:], None, ALU.add).then_inc(s_z, 1)
            dve.wait_ge(s_z, 3)
            own(dve.tensor_scalar(neg[:], z[:], -1.0, None, ALU.mult))
            dve.tensor_tensor(e[:], z[:], neg[:], ALU.min).then_inc(s_e, 1)
            dve.wait_ge(s_ln, 2)
            own(dve.tensor_scalar(z[:], z[:], 0.0, None, ALU.min))
            own(dve.tensor_tensor(z[:], e[:], z[:], ALU.subtract))
            dve.tensor_tensor_scan(neg[:], one[:], z[:], 0.0, ALU.mult, ALU.add).then_inc(s_neg, 1)

        def scalar(act):
            act.wait_ge(s_e, 1)
            act.activation(e[:], e[:], ACT.Exp).then_inc(s_ln, 1)
            act.wait_ge(s_ln, 1)
            act.activation(e[:], e[:], ACT.Ln, bias=1.0).then_inc(s_ln, 1)

        return dict(sync_end=sync_end, tensor=tensor, vector=vector, scalar=scalar)
    return along


def mixers_and_projections(nc, cst, col, pool_w, w_in, runs, uT, pT, v):
    src = chunked(w_in)
    NPC = len(PIECES1)
    NCH = 2
    WINDOWS = (2, 4, 8, 16)
    GD = 64
    PAD = TAPS - 1 - META
    with stage(nc, "mixers") as st:
        glu = st.sb("glu", [P, NCH, PAD + T1])
        y = st.sb("y", [P, NCH, S])
        s2, s4 = st.sb("sum2", [P, T1]), st.sb("sum4", [P, T1])
        diff = st.sb("diff", [P, NCH, S])
        pw = st.sb("pool_w", [P, NCH, P])
        mean_w = st.sb("mean_w", [P, P])
        sq = glu[:, :, 0:S]
        rt = s2[:, 0:S]
        raw = [st.sb(f"raw{p}", [P, KD, P]) for p in range(2)]
        wb = [[st.sb(f"w_{n}{p}", [P, KD, P], F32R) for n in ("high", "low")] for p in range(2)]
        vT = [st.sb(f"vT{q}", [P, T1]) for q in range(2)]
        acc = st.banks("acc", NPC)
        ps = [st.banks(f"ps{c}_", 2) for c in range(2)]
        s_raw = st.sem_n("w_loaded")
        s_w = st.sem("w_split")
        s_acc = st.sem("acc_ready")
        s_free = st.sem("acc_free")
        turned = [*ps[1], st.ps("turned")]
        s_glu = st.sem("glu_ready")
        s_eps = st.sem("eps_added_then_inverse")
        s_turn = st.sem("v_turned")
        s_v = st.sem("v_ready")
        s_ev = st.sem("pool_copied")
        s_clear = st.sem("cleared")
        s_pw = st.sem("pool_w_loaded")
        s_sig = st.sem("gate_ready")
        s_diff = st.sem("diff_ready")
        s_pool = st.sem("pool_ready")
        s_y = st.sem("conv_ready")
        s_mean = st.sem("mean_ready")
        s_cent = st.sem("centred")
        s_sq = st.sem("squared")
        s_var = st.sem("variance_ready")
        s_root = st.sem("root_ready")
        s_norm = st.sem("normed")

        def passes(eng, body):
            done = 0
            for f, o, n, factor in runs:
                with eng.Fori(0, n // 2) as i:
                    body(i + done, 2 * i + f, 2 * i + o, factor)
                done += n // 2
            return done

        QK = sum(n for _, _, n, _ in runs)
        VC = H1 * DH // P
        groups = [(0, 4, P), (4, 4, P), (8, 1, T1 - 8 * P)]

        with nc.Block() as block:
            @block.sync
            def _(sp):
                sp.wait_ge(s_clear, 1)
                for g in range(4):
                    r = GD * (g % 2)
                    sp.dma_start(pw[r:r + GD, g // 2, r:r + GD], pool_w[g]).then_inc(s_pw, 16)

                def load(i, f, o, _):
                    for p in range(2):
                        at = f * P + P * p
                        sp.wait_ge(s_w, 2 * i + p + 1)
                        sp.dma_start(raw[p][:], src[:, :, bass.ds(at, P)]).then_inc(s_raw[p], 16)
                passes(sp, load)
                for c in range(VC):
                    sp.wait_ge(s_w, QK + c + 1)
                    sp.dma_start(raw[c % 2][:], src[:, :, C_V1 + c * P:C_V1 + (c + 1) * P]).then_inc(s_raw[c % 2], 16)

            @block.gpsimd
            def _(pool):
                own = Steps(pool, st.sem("pool_step"))
                pool.sem_inc(s_w, 2)

                def split_weights(i, f, o, _):
                    own.enter(i, 4)
                    for p in range(2):
                        pool.wait_ge(s_raw[p], 16 * i + 16)
                        pool.wait_ge(s_acc, NPC * (2 * i + p + 1))
                        split(pool, own, raw[p][:], wb[p][0][:], wb[p][1][:], True).then_inc(s_w, 1)
                own.leave(passes(pool, split_weights), 4)
                for c in range(VC):
                    g, p = QK + c, c % 2
                    pool.wait_ge(s_raw[p], 16 * (g // 2) + 16)
                    pool.wait_ge(s_acc, NPC * (g + 1))
                    split(pool, own, raw[p][:], wb[p][0][:], wb[p][1][:]).then_inc(s_w, 1)

            @block.scalar
            def _(act):
                for c in range(NCH):
                    act.activation(pT[:, AT_BG + c, :], pT[:, AT_BG + c, :], ACT.Sigmoid).then_inc(s_sig, 1)
                act.sem_inc(s_free, NPC)

                def copies(i, f, o, factor):
                    for p in range(2):
                        for n, (a, b) in enumerate(PIECES1):
                            act.wait_ge(s_acc, NPC * (2 * i + p) + n + 1 + 2 * NPC)
                            dst = pT[:, bass.ds(o + p, 1), a:b].rearrange("p c t -> p (c t)")
                            act.activation(dst, acc[n][:, 0:b - a], ACT.Copy, scale=factor).then_inc(s_free, 1)
                passes(act, copies)

                def norm_step(c):
                    if c == 1:
                        for k in range(NCH):
                            for h, (a, b) in enumerate(HALVES):
                                act.wait_ge(s_cent, 2 * k + h + 1)
                                act.activation(sq[:, k, a:b], y[:, k, a:b], ACT.Square).then_inc(s_sq, 1)
                    if c == 2:
                        for h, (a, b) in enumerate(HALVES):
                            act.wait_ge(s_eps, h + 1)
                            act.activation(rt[:, a:b], rt[:, a:b], ACT.Sqrt).then_inc(s_root, 1)
                    if c == 3:
                        for k in range(NCH):
                            act.wait_ge(s_norm, k + 1)
                            act.activation(pT[:, AT_BV + k, META:T1], y[:, k, :], ACT.Silu,
                                           bias=col["conv_ln_b"][:, k:k + 1], scale=col["conv_ln_g"][:, k:k + 1])

                act.wait_ge(s_glu, 1)
                for c in range(VC + 1):
                    if c < VC:
                        for n, (a, b) in enumerate(PIECES1):
                            act.wait_ge(s_acc, NPC * (QK + c) + n + 1 + 2 * NPC)
                            if c >= 2:
                                act.wait_ge(s_turn, len(groups) * (c - 1))
                            act.copy(vT[c % 2][:, a:b], acc[n][:, 0:b - a]).then_inc(s_free, 1)
                    if c:
                        for n, (t, m, rows) in enumerate(groups):
                            act.wait_ge(s_turn, len(groups) * (c - 1) + n + 1)
                            act.copy(v[0:rows, t:t + m, (c - 1) * P:c * P],
                                     turned[n][0:rows, 0:m * P].rearrange("p (t d) -> p t d", t=m)).then_inc(s_v, 1)
                    norm_step(c)

            @block.vector
            def _(dve):
                own = Steps(dve, st.sem("dve_step"))
                dve.memset(pw[:], 0.0).then_inc(s_clear, 1)
                dve.memset(mean_w[:], 1.0 / CONV_W1).then_inc(s_clear, 1)
                own(dve.memset(glu[:, :, 0:PAD], 0.0))
                for c in range(NCH):
                    x = pT[:, c, :]
                    own(dve.tensor_tensor(s2[:, 1:T1], x[:, 1:T1], x[:, 0:T1 - 1], ALU.add))
                    own(dve.tensor_tensor(s4[:, 3:T1], s2[:, 3:T1], s2[:, 1:T1 - 2], ALU.add))
                    if c:
                        own(dve.tensor_tensor(s2[:, 7:T1], s4[:, 7:T1], s4[:, 3:T1 - 4], ALU.add))
                        own(dve.tensor_tensor(s4[:, 15:T1], s2[:, 15:T1], s2[:, 7:T1 - 8], ALU.add))
                    for half, s in enumerate((s2, s4)):
                        r = slice(GD * half, GD * half + GD)
                        last = dve.scalar_tensor_tensor(
                            out=diff[r, c, :], in0=s[r, META:T1], scalar=1.0 / WINDOWS[2 * c + half],
                            in1=x[r, META:T1], op0=ALU.mult, op1=ALU.subtract)
                        last.then_inc(s_diff, 1)
                    dve.wait_ge(s_diff, 2 * c + 2)
                for c in range(NCH):
                    dve.wait_ge(s_sig, c + 1)
                    own(dve.tensor_tensor(glu[:, c, PAD:], pT[:, AT_BV + c, :], pT[:, AT_BG + c, :], ALU.mult))
                dve.sem_inc(s_glu, 1)
                for j in range(TAPS):
                    for c in range(NCH):
                        w = col["conv_w"][:, NCH * j + c:NCH * j + c + 1]
                        x = glu[:, c, j:j + S]
                        if j == 0:
                            ins = dve.tensor_scalar(y[:, c, :], x, w, col["conv_b"][:, c:c + 1], ALU.mult, ALU.add)
                        else:
                            dve.wait_ge(s_y, NCH * (j - 1) + c + 1)
                            ins = dve.scalar_tensor_tensor(out=y[:, c, :], in0=x, scalar=w, in1=y[:, c, :],
                                                           op0=ALU.mult, op1=ALU.add)
                        ins.then_inc(s_y, 1)
                for c in range(NCH):
                    for h, (a, b) in enumerate(HALVES):
                        dve.wait_ge(s_pool, 2 * c + h + 1)
                        dve.tensor_scalar(pT[:, c, META + a:META + b], ps[c][h][:], col["pool_b"][:, c:c + 1],
                                          col["pool_scale"][:, c:c + 1], ALU.add, ALU.mult).then_inc(s_ev, 1)
                dve.wait_ge(s_mean, 2)
                for c in range(NCH):
                    for h, (a, b) in enumerate(HALVES):
                        dve.tensor_tensor(y[:, c, a:b], y[:, c, a:b], ps[0][h][:], ALU.subtract).then_inc(s_cent, 1)
                for h, (a, b) in enumerate(HALVES):
                    dve.wait_ge(s_var, h + 1)
                    dve.tensor_scalar(rt[:, a:b], ps[0][h][:], EPS, None, ALU.add).then_inc(s_eps, 1)
                for h, (a, b) in enumerate(HALVES):
                    dve.wait_ge(s_root, h + 1)
                    dve.reciprocal(rt[:, a:b], rt[:, a:b]).then_inc(s_eps, 1)
                dve.wait_ge(s_eps, 4)
                for c in range(NCH):
                    dve.tensor_tensor(y[:, c, :], y[:, c, :], rt[:], ALU.mult).then_inc(s_norm, 1)

            @block.tensor
            def _(pe):
                pe.sem_inc(s_acc, 2 * NPC)

                def multiply(i, f, o, _):
                    for p in range(2):
                        pe.wait_ge(s_w, 2 * i + p + 3)
                        for n, (a, b) in enumerate(PIECES1):
                            pe.wait_ge(s_free, NPC * (2 * i + p) + n + 1)
                            split_products(pe, acc[n][:, 0:b - a],
                                           [([w[:, k, :] for w in wb[p]], [u[:, k, a:b] for u in uT])
                                            for k in range(KD)]).then_inc(s_acc, 1)
                passes(pe, multiply)
                pe.wait_ge(s_pw, 64)
                for k in range(NCH):
                    pe.wait_ge(s_diff, 2 * k + 2)
                    for h, (a, b) in enumerate(HALVES):
                        pe.matmul(ps[k][h][:], pw[:, k, :], diff[:, k, a:b], start=True, stop=True).then_inc(s_pool, 1)

                def norm_step(c):
                    if c == 1:
                        pe.wait_ge(s_clear, 2)
                        pe.wait_ge(s_y, NCH * TAPS)
                        pe.wait_ge(s_ev, 2 * NCH)
                        for h, (a, b) in enumerate(HALVES):
                            products(pe, ps[0][h][:], [(mean_w[:], y[:, k, a:b]) for k in range(NCH)]).then_inc(s_mean, 1)
                    if c == 2:
                        for h, (a, b) in enumerate(HALVES):
                            pe.wait_ge(s_sq, NCH + h + 1)
                            pe.wait_ge(s_cent, NCH + h + 1)
                            products(pe, ps[0][h][:], [(mean_w[:], sq[:, k, a:b]) for k in range(NCH)]).then_inc(s_var, 1)

                for c in range(VC + 1):
                    if c < VC:
                        pe.wait_ge(s_w, QK + c + 3)
                        for n, (a, b) in enumerate(PIECES1):
                            pe.wait_ge(s_free, NPC * (QK + c) + n + 1)
                            split_products(pe, acc[n][:, 0:b - a],
                                           [([w[:, k, :] for w in wb[c % 2]], [u[:, k, a:b] for u in uT])
                                            for k in range(KD)]).then_inc(s_acc, 1)
                    if c:
                        pe.wait_ge(s_free, NPC * (QK + c + 1))
                        if c == 1:
                            pe.wait_ge(s_ev, 2 * NCH)
                        for n, (t, m, rows) in enumerate(groups):
                            if c > 1:
                                pe.wait_ge(s_v, len(groups) * (c - 2) + n + 1)
                            for q in range(m):
                                last = pe.transpose(turned[n][0:rows, q * P:(q + 1) * P],
                                                    vT[(c - 1) % 2][:, (t + q) * P:(t + q) * P + rows], cst["ident"][:])
                            last.then_inc(s_turn, 1)
                    norm_step(c)



def attention(nc, cst, name, heads, off, dq, masks, load_head, loads, v, oT, bias_row, prefetch=None):
    mask_qk, mask_kq = masks
    T = S + off
    NK = -(-T // P)
    k_max = dq + bias_row
    k_all = ONE_ROW + 1
    cuts = [0] + [c for c in (off + P * (BANK // P - (1 if off else 0)),
                              off + P * (2 * (BANK // P) - (1 if off else 0))) if c < T] + [T]
    maxima = []
    for i in range(NT):
        end = off + P * (i + 1)
        maxima += [(i, n, a, min(b, end)) for n, (a, b) in enumerate(zip(cuts, cuts[1:])) if a < end]
    units = []
    for n, (a, b) in enumerate(HALVES):
        for t in range(NK):
            d0 = P * t - off
            if d0 < b:
                units.append((n, t, max(a, d0), (max(a, d0), min(b, d0 + P)) if d0 + P > a else None))
    NM, NU = len(maxima), len(units)
    NPC = len(cuts) - 1
    R_M, R_P = 2, 4
    R_S = 3 if NU % 3 == 0 else 2
    PER_UNIT, FIRST = 2, 1
    TURN_AT = FIRST + -(-NM // PER_UNIT) + 1
    assert NM % R_M == 0 and NU % R_S == 0 and 2 * NU % R_P == 0 and TURN_AT < NU
    with stage(nc, name) as st:
        raw = [st.sb("q", [k_all, S]), st.sb("k", [k_all, T])]
        hi = [[st.sb(f"{n}_hi{p}", [k_all, w], F32R) for p in range(2)] for n, w in (("q", S), ("k", T))]
        lo = [[st.sb(f"{n}_lo{p}", [k_all, w], F32R) for p in range(2)] for n, w in (("q", S), ("k", T))]
        v_aug = [st.sb(f"v{p}", [P, NK, P]) for p in range(2)]
        probs = [st.sb(f"probs{r}", [P, BANK]) for r in range(R_P)]
        pm = st.sb("piece_max", [P, NT, NPC])
        nm = [st.sb(f"neg_max{p}", [P, NT]) for p in range(2)]
        nm_rows = [st.sb(f"neg_rows{p}", [NT, P], F32R) for p in range(2)]
        inv = st.sb("inverse", [DH, BANK])
        ps_m = st.banks("max", R_M)
        ps_s = st.banks("scores", R_S)
        ps_o = st.banks("out", 2)
        ps_t = st.ps("turned")
        s_init = st.sem("initialised")
        s_load = st.sem("head_loaded")
        s_pre = st.sem("prefetched")
        s_hi = st.sem("high_ready")
        s_lo = st.sem("low_ready")
        s_row = st.sem_n("max_row_loaded")
        s_v = st.sem_n("v_copied")
        s_mx = st.sem("max_scores_ready")
        s_mxfree = st.sem("max_bank_free")
        s_nm = st.sem("neg_max_ready")
        s_nmt = st.sem("neg_max_turned")
        s_rows = st.sem("neg_rows_ready")
        s_sc = st.sem("scores_ready")
        s_exp = st.sem("probs_ready")
        s_pv = st.sem("probs_used")
        s_outfree = st.sem_n("out_bank_free")
        with nc.Block() as block:
            @block.sync
            def _(sp):
                sp.wait_ge(s_init, 1)

                def row_of_maxima(h, p):
                    sp.wait_ge(s_rows, h + 2)
                    sp.dma_start(hi[0][p][ONE_ROW:ONE_ROW + 1, :].bitcast(F32), nm_rows[p][:].bitcast(F32)).then_inc(s_row[p], 16)

                load_head(sp, 0, 0, raw[0], raw[1], s_load)
                sp.wait_ge(s_lo, 2)
                load_head(sp, 1, 0, raw[0], raw[1], s_load)
                row_of_maxima(0, 0)

                def pair(j, last):
                    row_of_maxima(2 * j + 1, 1)
                    if prefetch:
                        for dst, src in prefetch:
                            sp.dma_start(dst(j), src(j)).then_inc(s_pre, 16)
                    if not last:
                        sp.wait_ge(s_lo, 2 * (2 * j + 2))
                        load_head(sp, 0, j + 1, raw[0], raw[1], s_load)
                        row_of_maxima(2 * j + 2, 0)
                        sp.wait_ge(s_lo, 2 * (2 * j + 3))
                        load_head(sp, 1, j + 1, raw[0], raw[1], s_load)

                with sp.Fori(0, heads // 2 - 1) as j:
                    pair(j, False)
                pair(heads // 2 - 1, True)
                if prefetch:
                    sp.wait_ge(s_pre, 16 * len(prefetch) * heads // 2)

            @block.gpsimd
            def _(pool):
                own = Steps(pool, st.sem("pool_step"))
                for r in raw:
                    own(pool.memset(r[64:k_all, :], 0.0))
                if bias_row:
                    own(pool.memset(raw[0][DH:DH + 1, :], 1.0))
                own(pool.memset(raw[1][ONE_ROW:ONE_ROW + 1, :], 1.0))
                pool.sem_inc(s_init, 1)
                for p in range(2):
                    own(pool.memset(v_aug[p][:, :, DH:P], 1.0))

                def copy_v(p, j):
                    for t in range(NK):
                        rows = min(P, T - P * t)
                        at = bass.ds((2 * j + p) * DH, DH)
                        last = pool.tensor_copy(v_aug[p][0:rows, t, 0:DH], v[0:rows, t, at])
                    last.then_inc(s_v[p], 1)

                for p in range(2):
                    copy_v(p, 0)
                with pool.Fori(0, heads // 2 - 1) as j:
                    for p in range(2):
                        pool.wait_ge(s_pv, NU * (2 * j + p + 1) + R_P)
                        copy_v(p, j + 1)

            @block.tensor
            def _(pe):
                pe.sem_inc(s_pv, R_P)

                def max_piece(h, p, m):
                    i, n, a, b = maxima[m]
                    pe.wait_ge(s_mxfree, NM * h + m + 1)
                    out = ps_m[m % R_M]
                    d = off + P * i
                    ins = pe.matmul(out[:, 0:b - a], hi[0][p][0:k_max, P * i:P * i + P],
                                    hi[1][p][0:k_max, a:b], start=True, stop=True)
                    if a <= d < b:
                        ins = pe.matmul(out[:, d - a:d - a + P], cst["identb"][:], mask_qk[:],
                                        start=False, stop=True, skip_group_check=True)
                    ins.then_inc(s_mx, 1)

                def turn_maxima(h, p):
                    pe.wait_ge(s_nm, h + 1)
                    pe.wait_ge(s_rows, h + 1)
                    pe.transpose(ps_t[0:NT, 0:P], nm[p][:], cst["ident"][:]).then_inc(s_nmt, 1)

                def scores(h, p, u):
                    n, t, first, masked = units[u]
                    a, b = HALVES[n]
                    rows = min(P, T - P * t)
                    pe.wait_ge(s_exp, NU * h + u + 1)
                    out = ps_s[u % R_S]
                    ks, qs = slice(P * t, P * t + rows), slice(first, b)
                    ins = products(pe, out[0:rows, first - a:b - a],
                                   [(hi[1][p][:, ks], hi[0][p][:, qs]), (hi[1][p][:, ks], lo[0][p][:, qs]),
                                    (lo[1][p][:, ks], hi[0][p][:, qs])])
                    if masked:
                        c0, c1 = masked
                        m0 = c0 - (P * t - off)
                        ins = pe.matmul(out[0:rows, c0 - a:c1 - a], cst["identb"][:, 0:rows],
                                        mask_kq[:, m0:m0 + c1 - c0],
                                        start=False, stop=True, skip_group_check=True)
                    ins.then_inc(s_sc, 1)

                def values(h, p, u):
                    n, t, first, _ = units[u]
                    a, b = HALVES[n]
                    rows = min(P, T - P * t)
                    if t == 0:
                        pe.wait_ge(s_outfree[n], h + 1)
                    pe.wait_ge(s_exp, NU * h + u + 1 + R_S)
                    pr = probs[(NU * p + u) % R_P]
                    pe.matmul(ps_o[n][:, first - a:b - a], v_aug[p][0:rows, t, :], pr[0:rows, first - a:b - a],
                              start=(t == 0), stop=True, skip_group_check=True).then_inc(s_pv, 1)

                def head(h, j, p, last):
                    pe.wait_ge(s_row[p], 16 * j + 16)
                    pe.wait_ge(s_v[p], j + 1)
                    pe.wait_ge(s_lo, 2 * h + 2)
                    for u in range(R_S - 1):
                        scores(h, p, u)
                    for u in range(NU):
                        if u + R_S - 1 < NU:
                            scores(h, p, u + R_S - 1)
                        if not last:
                            if u == FIRST:
                                pe.wait_ge(s_hi, 2 * h + 4)
                            for m in range(PER_UNIT * (u - FIRST), PER_UNIT * (u - FIRST + 1)):
                                if 0 <= m < NM:
                                    max_piece(h + 1, 1 - p, m)
                            if u == TURN_AT:
                                turn_maxima(h + 1, 1 - p)
                        values(h, p, u)

                pe.wait_ge(s_hi, 2)
                for m in range(NM):
                    max_piece(0, 0, m)
                turn_maxima(0, 0)
                with pe.Fori(0, heads // 2 - 1) as j:
                    head(2 * j, j, 0, False)
                    head(2 * j + 1, j, 1, False)
                last = heads // 2 - 1
                head(2 * last, last, 0, False)
                head(2 * last + 1, last, 1, True)

            @block.scalar
            def _(act):
                act.sem_inc(s_exp, R_S)

                def split_high(h, p, n):
                    if n == 0:
                        act.wait_ge(s_load, 16 * loads * (h + 1))
                    rows = ONE_ROW if n == 0 else k_all
                    act.copy(hi[n][p][0:rows, :], raw[n][0:rows, :]).then_inc(s_hi, 1)

                def head(h, p, last):
                    for u, (n, t, first, _) in enumerate(units):
                        a, b = HALVES[n]
                        rows = min(P, T - P * t)
                        act.wait_ge(s_sc, NU * h + u + 1)
                        act.wait_ge(s_pv, NU * h + u + 1)
                        act.activation(probs[(NU * p + u) % R_P][0:rows, first - a:b - a],
                                       ps_s[u % R_S][0:rows, first - a:b - a], ACT.Exp).then_inc(s_exp, 1)
                        if u in (0, 1) and not last:
                            split_high(h + 1, 1 - p, u)

                split_high(0, 0, 0)
                split_high(0, 0, 1)
                with act.Fori(0, heads // 2 - 1) as j:
                    head(2 * j, 0, False)
                    head(2 * j + 1, 1, False)
                head(heads - 2, 0, False)
                head(heads - 1, 1, True)

            @block.vector
            def _(dve):
                own = Steps(dve, st.sem("dve_step"))
                own(dve.memset(pm[:], 3.0 * MASKED))
                for p in range(2):
                    own(dve.memset(lo[0][p][ONE_ROW:k_all, :].bitcast(F32), 0.0))
                own.leave(1, 3)
                dve.sem_inc(s_rows, 1)
                dve.sem_inc(s_mxfree, R_M)
                for n in range(2):
                    dve.sem_inc(s_outfree[n], 1)

                def maxima_of(h, j, p, lag):
                    for m, (i, n, a, b) in enumerate(maxima):
                        dve.wait_ge(s_mx, NM * h + m + 1)
                        dve.tensor_reduce(pm[:, i, n:n + 1], ps_m[m % R_M][:, 0:b - a], AX.X,
                                          ALU.max).then_inc(s_mxfree, 1)
                    dve.wait_ge(s_mxfree, NM * h + NM + R_M)
                    dve.tensor_reduce(nm[p][:], pm[:], AX.X, ALU.max, negate=True).then_inc(s_nm, 1)
                    for n in range(2):
                        rows = ONE_ROW if n == 0 else k_all
                        dve.wait_ge(s_hi, 2 * h + n + 1)
                        dve.tensor_tensor(lo[n][p][0:rows, :], raw[n][0:rows, :],
                                          hi[n][p][0:rows, :].bitcast(F32), ALU.subtract).then_inc(s_lo, 1)
                    dve.wait_ge(s_nmt, h + 1)
                    if lag:
                        dve.wait_ge(s_row[p], 16 * j)
                    dve.tensor_copy(nm_rows[p][:], ps_t[0:NT, 0:P]).then_inc(s_rows, 1)

                def out_of(h, j, p):
                    for n, (a, b) in enumerate(HALVES):
                        end = [u for u in range(NU) if units[u][0] == n][-1]
                        dve.wait_ge(s_pv, NU * h + end + 1 + R_P)
                        own(dve.reciprocal(inv[:], ps_o[n][DH:P, :]))
                        dst = oT[DH * p:DH * p + DH, bass.ds(j, 1), a:b].rearrange("p a t -> p (a t)")
                        dve.tensor_tensor(dst, ps_o[n][0:DH, :], inv[:], ALU.mult).then_inc(s_outfree[n], 1)
                        dve.wait_ge(s_outfree[n], h + 2)

                maxima_of(0, 0, 0, False)

                def pair(j, first, last):
                    maxima_of(2 * j + 1, j, 1, not first)
                    out_of(2 * j, j, 0)
                    if not last:
                        maxima_of(2 * j + 2, j + 1, 0, True)
                    out_of(2 * j + 1, j, 1)

                pair(0, True, False)
                own.leave(1, 4)
                with dve.Fori(1, heads // 2 - 1) as j:
                    own.enter(j - 1, 4)
                    pair(j, False, False)
                own.leave(heads // 2 - 2, 4)
                pair(heads // 2 - 1, False, True)



def merge_branches(nc, w_in, outs, uT, branch, mergedT):
    NB = len(outs)
    kk = [n for _, n in branch]
    starts = [sum(kk[:b]) for b in range(NB)]
    NU = 2 * NB
    CREDIT = 2 * NU
    with stage(nc, "merge1") as st:
        raw = [st.sb(f"raw{q}", [P, KD, P]) for q in range(2)]
        wg = [[st.sb(f"wg_{n}{b}", [P, KD, P], F32R) for n in ("high", "low")] for b in range(NB)]
        wy = [st.sb(f"wy{p}", [P, sum(kk), P]) for p in range(2)]
        sg = [st.sb(f"gate{b}", [P, BANK]) for b in range(NB)]
        pr = [st.sb(f"gated{b}", [P, BANK]) for b in range(NB)]
        ps_g, ps_y = st.banks("gates", NB), st.banks("branch", NB)
        s_raw = st.sem_n("gate_w_loaded")
        s_w = st.sem_n("branch_w_loaded")
        s_go = st.sem("may_load")
        s_split = st.sem("gate_w_split")
        s_gy = st.sem("unit_ready")
        s_sg = st.sem("gate_ready")
        s_done = st.sem("unit_used")
        with nc.Block() as block:
            @block.sync
            def _(sp):
                gsrc = w_in[:, C_G1:C_G1 + NB * D].rearrange("(c p) (b n) -> b p c n", p=P, b=NB)
                with sp.Fori(0, KD // 2) as i:
                    for p in range(2):
                        m = P * (2 * i + p)
                        for b in range(NB):
                            u = NB * p + b
                            sp.wait_ge(s_split, 2 * NB * i + u + 1)
                            sp.dma_start(raw[u % 2][:], gsrc[b, :, :, bass.ds(m, P)]).then_inc(s_raw[u % 2], 16)
                            if b == 0:
                                sp.wait_ge(s_gy, NU * (2 * i + p + 1))
                                sp.sem_inc(s_go, 1)
                                for n in range(NB):
                                    sp.dma_start(wy[p][:, starts[n]:starts[n] + kk[n], :],
                                                 chunked(outs[n])[:, :, bass.ds(m, P)]).then_inc(s_w[p], 16)

            @block.gpsimd
            def _(pool):
                own = Steps(pool, st.sem("pool_step"))
                pool.sem_inc(s_split, 2)
                with pool.Fori(0, KD // 2) as i:
                    own.enter(i, 2 * 2 * NB)
                    for p in range(2):
                        for b in range(NB):
                            u = NB * p + b
                            pool.wait_ge(s_raw[u % 2], 16 * NB * i + 16 * (u // 2) + 16)
                            pool.wait_ge(s_gy, NU * (2 * i + p + 1) + NB + b + 1)
                            split(pool, own, raw[u % 2][:], wg[b][0][:], wg[b][1][:], True).then_inc(s_split, 1)
                own.leave(KD // 2, 2 * 2 * NB)

            @block.tensor
            def _(pe):
                pe.sem_inc(s_gy, CREDIT)
                with pe.Fori(0, KD // 2) as i:
                    for p in range(2):
                        for h, (a, z) in enumerate(HALVES):
                            for b, (of, n) in enumerate(branch):
                                pe.wait_ge(s_done, NU * (2 * i + p) + NB * h + b + 1)
                                if h == 0:
                                    pe.wait_ge(s_split, NB * (2 * i + p) + b + 3)
                                split_products(pe, ps_g[b][:], [([w[:, k, :] for w in wg[b]], uT(k, a, z))
                                                                for k in range(KD)])
                                if h == 0 and b == 0:
                                    pe.wait_ge(s_w[p], 16 * NB * i + 16 * NB)
                                products(pe, ps_y[b][:], [(wy[p][:, starts[b] + k, :], of(k, a, z))
                                                          for k in range(n)]).then_inc(s_gy, 1)

            @block.scalar
            def _(act):
                with act.Fori(0, KD // 2) as i:
                    for p in range(2):
                        for u in range(NU):
                            act.wait_ge(s_gy, NU * (2 * i + p) + u + 1 + CREDIT)
                            act.activation(sg[u % NB][:], ps_g[u % NB][:], ACT.Sigmoid).then_inc(s_sg, 1)

            @block.vector
            def _(dve):
                own = Steps(dve, st.sem("dve_step"))
                dve.sem_inc(s_done, NB)
                per = 2 * 2 * (NB - 1)
                with dve.Fori(0, KD // 2) as i:
                    own.enter(i, per)
                    for p in range(2):
                        for h, (a, z) in enumerate(HALVES):
                            dst = mergedT[:, bass.ds(2 * i + p, 1), a:z].rearrange("p c t -> p (c t)")
                            for b in range(NB):
                                g = NU * (2 * i + p) + NB * h + b
                                dve.wait_ge(s_sg, g + 1)
                                dve.tensor_tensor(pr[b][:], ps_y[b][:], sg[b][:], ALU.mult).then_inc(s_done, 1)
                                dve.wait_ge(s_done, g + 1 + NB)
                                if b:
                                    own(dve.tensor_tensor(dst if b == NB - 1 else pr[0][:], pr[0][:], pr[b][:],
                                                          ALU.add))
                own.leave(KD // 2, per)


def output_and_router(nc, cst, name, mergedT, w_o, resid, g_row, routers, biases, h_out, v_out, logits):
    NL = NG + routers[1].shape[1]
    R_X = 4
    with stage(nc, name) as st:
        raw = [st.sb(f"raw{q}", [P, D]) for q in range(2)]
        wo = [st.sb(f"w_{n}", [P, KD, D], F32R) for n in ("high", "low")]
        m_hl = [[st.sb(f"merged_{n}{q}", [P, KD, P], F32R) for n in ("high", "low")] for q in range(2)]
        x = st.sb("h", [P, R_X, D])
        g = st.sb("g", [P, D])
        v = [st.sb(f"v{q}", [P, D]) for q in range(2)]
        vT = [st.sb(f"vT{q}", [P, KD, P]) for q in range(2)]
        wr = st.sb("wr", [P, KD, NL])
        br = st.sb("br", [P, NL])
        junk = st.sb("squares", [P, D])
        ss, ms, rt, inv = (st.sb(n, [P, NT]) for n in ("sums", "mean", "root", "inverse"))
        acc = st.banks("acc", 4)
        turn = st.banks("turn", 2)
        lg = st.banks("logits", 2)
        s_raw = st.sem_n("w_loaded")
        s_high = st.sem("w_high_ready")
        s_w = st.sem("w_split")
        s_m = st.sem("merged_split")
        s_r = st.sem("router_loaded")
        s_x = st.sem_n("resid_loaded", R_X)
        s_acc = st.sem("acc_ready")
        s_h = st.sem("h_ready")
        s_ss = st.sem("sum_ready")
        s_ms = st.sem("mean_ready")
        s_rt = st.sem("root_ready")
        s_inv = st.sem("inverse_ready")
        s_v = st.sem("v_ready")
        s_turn = st.sem("turned")
        s_vT = st.sem("vT_ready")
        s_lg = st.sem("logits_ready")
        s_lgfree = st.sem("logits_copied")
        s_sv = st.sem_n("v_stored")
        s_sh = st.sem_n("h_stored", R_X)
        with nc.Block() as block:
            @block.sync
            def _(sp):
                for k in range(KD):
                    if k >= 2:
                        sp.wait_ge(s_w, k - 1)
                    sp.dma_start(raw[k % 2][:], w_o[k * P:(k + 1) * P, :]).then_inc(s_raw[k % 2], 16)
                for t in range(R_X):
                    sp.dma_start(x[:, t, :], resid[t * P:(t + 1) * P, :]).then_inc(s_x[t], 16)
                with nc.allow_non_contiguous_dma(reason="router columns"):
                    sp.dma_start(wr[:, :, 0:NG], chunked(routers[0])).then_inc(s_r, 16)
                    sp.dma_start(wr[:, :, NG:], chunked(routers[1])).then_inc(s_r, 16)
                    sp.dma_start(br[:, 0:NG], biases[0].to_broadcast((P, NG))).then_inc(s_r, 16)
                    sp.dma_start(br[:, NG:], biases[1].to_broadcast((P, NL - NG))).then_inc(s_r, 16)
                    sp.dma_start(g[:], g_row.to_broadcast((P, D))).then_inc(s_r, 16)
                for t in range(NT):
                    sp.wait_ge(s_h, 2 * t + 2)
                    sp.dma_start(h_out[t * P:(t + 1) * P, :], x[:, t % R_X, :]).then_inc(s_sh[t % R_X], 16)
                    sp.wait_ge(s_v, t + 1)
                    sp.dma_start(v_out[t * P:(t + 1) * P, :], v[t % 2][:]).then_inc(s_sv[t % 2], 16)
                    if t and t + R_X - 1 < NT:
                        r = (t - 1) % R_X
                        sp.wait_ge(s_sh[r], 16 * ((t - 1) // R_X) + 16)
                        sp.dma_start(x[:, r, :], resid[(t - 1 + R_X) * P:(t + R_X) * P, :]).then_inc(s_x[r], 16)
                for r in range(R_X):
                    sp.wait_ge(s_sh[r], 16 * NT // R_X)
                for q in range(2):
                    sp.wait_ge(s_sv[q], 16 * NT // 2)

            @block.tensor
            def _(pe):
                def project_first():
                    pe.wait_ge(s_m, 2)
                    for k in range(KD):
                        pe.wait_ge(s_w, k + 1)
                        for t in range(2):
                            for h, (a, b) in enumerate(HALVES):
                                (mh, ml), (wh, wl) = m_hl[t], wo
                                out = acc[2 * t + h][:]
                                pe.matmul(out, mh[:, k, :], wh[:, k, a:b], start=(k == 0), stop=False)
                                pe.matmul(out, mh[:, k, :], wl[:, k, a:b], start=False, stop=False)
                                last = pe.matmul(out, ml[:, k, :], wh[:, k, a:b], start=False, stop=(k == KD - 1))
                                if k == KD - 1:
                                    last.then_inc(s_acc, 1)

                def project(t):
                    pe.wait_ge(s_m, t + 1)
                    for h, (a, b) in enumerate(HALVES):
                        pe.wait_ge(s_h, 2 * (t - 2) + h + 1)
                        split_products(pe, acc[2 * (t % 2) + h][:],
                                       [([m[:, k, :] for m in m_hl[t % 2]], [w[:, k, a:b] for w in wo])
                                        for k in range(KD)]).then_inc(s_acc, 1)

                def turn_v(t):
                    pe.wait_ge(s_v, t + 1)
                    for h in range(2):
                        if t:
                            pe.wait_ge(s_vT, 2 * (t - 1) + h + 1)
                        for c in range(4):
                            k = 4 * h + c
                            last = pe.transpose(turn[h][:, c * P:(c + 1) * P], v[t % 2][:, k * P:(k + 1) * P],
                                                cst["ident"][:])
                        last.then_inc(s_turn, 1)

                def route(t):
                    if t == 0:
                        pe.wait_ge(s_r, 80)
                    pe.wait_ge(s_vT, 2 * t + 2)
                    if t >= 2:
                        pe.wait_ge(s_lgfree, t - 1)
                    products(pe, lg[t % 2][:, 0:NL],
                             [(vT[t % 2][:, k, :], wr[:, k, :]) for k in range(KD)]).then_inc(s_lg, 1)

                project_first()
                for t in range(NT + 2):
                    if 2 <= t < NT:
                        project(t)
                    if 1 <= t <= NT:
                        turn_v(t - 1)
                    if t >= 2:
                        route(t - 2)

            @block.gpsimd
            def _(pool):
                own = Steps(pool, st.sem("pool_step"))
                for t in range(1, NT):
                    if t >= 2:
                        pool.wait_ge(s_acc, 2 * (t - 2) + 2)
                    split(pool, own, mergedT[:, :, t * P:(t + 1) * P], m_hl[t % 2][0][:],
                          m_hl[t % 2][1][:]).then_inc(s_m, 1)

            @block.vector
            def _(dve):
                split(dve, Steps(dve, st.sem("dve_step")), mergedT[:, :, 0:P], m_hl[0][0][:],
                      m_hl[0][1][:]).then_inc(s_m, 1)
                for k in range(KD):
                    dve.wait_ge(s_high, k + 1)
                    dve.tensor_tensor(wo[1][:, k, :], raw[k % 2][:], wo[0][:, k, :].bitcast(F32),
                                      ALU.subtract).then_inc(s_w, 1)
                for t in range(NT + 2):
                    if t < NT:
                        dve.wait_ge(s_x[t % R_X], 16 * (t // R_X) + 16)
                        for h, (a, b) in enumerate(HALVES):
                            dve.wait_ge(s_acc, 2 * t + h + 1)
                            dve.tensor_tensor(x[:, t % R_X, a:b], x[:, t % R_X, a:b], acc[2 * (t % 2) + h][:],
                                              ALU.add).then_inc(s_h, 1)
                        dve.wait_ge(s_ss, t + 1)
                        dve.tensor_scalar(ms[:, t:t + 1], ss[:, t:t + 1], 1.0 / D, EPS, ALU.mult,
                                          ALU.add).then_inc(s_ms, 1)
                        dve.wait_ge(s_rt, t + 1)
                        dve.reciprocal(inv[:, t:t + 1], rt[:, t:t + 1]).then_inc(s_inv, 1)
                        dve.wait_ge(s_inv, t + 1)
                        if t == 0:
                            dve.wait_ge(s_r, 80)
                        else:
                            dve.wait_ge(s_turn, 2 * t - 2 if t >= 2 else 1)
                        if t >= 2:
                            dve.wait_ge(s_sv[t % 2], 16 * (t // 2))
                        dve.scalar_tensor_tensor(out=v[t % 2][:], in0=x[:, t % R_X, :], scalar=inv[:, t:t + 1],
                                                 in1=g[:], op0=ALU.mult, op1=ALU.mult).then_inc(s_v, 1)
                    if t >= 2:
                        dve.wait_ge(s_lg, t - 1)
                        dve.tensor_tensor(logits[:, t - 2, :], lg[t % 2][:, 0:NL], br[:],
                                          ALU.add).then_inc(s_lgfree, 1)

            @block.scalar
            def _(act):
                for k in range(KD):
                    act.wait_ge(s_raw[k % 2], 16 * (k // 2) + 16)
                    act.copy(wo[0][:, k, :], raw[k % 2][:]).then_inc(s_high, 1)
                for t in range(NT + 1):
                    if t < NT:
                        act.wait_ge(s_h, 2 * t + 2)
                        act.activation(junk[:], x[:, t % R_X, :], ACT.Square, accum_out=ss[:, t:t + 1]).then_inc(s_ss, 1)
                        act.wait_ge(s_ms, t + 1)
                        act.activation(rt[:, t:t + 1], ms[:, t:t + 1], ACT.Sqrt).then_inc(s_rt, 1)
                    if t:
                        for h in range(2):
                            act.wait_ge(s_turn, 2 * (t - 1) + h + 1)
                            if t >= 3:
                                act.wait_ge(s_lg, t - 2)
                            act.copy(vT[(t - 1) % 2][:, 4 * h:4 * h + 4, :].rearrange("p c t -> p (c t)"),
                                     turn[h][:]).then_inc(s_vT, 1)



def block_count(experts):
    n = (2 * S + experts * (P - 1)) // P
    return n + -n % blocks_of_pass(experts)


def blocks_of_pass(experts):
    return 4 if S * 2 // experts >= P else 2


def route_tokens(nc, cst, name, experts, logits, ids_d, r):
    E, EG, NB, B = experts, experts // NG, block_count(experts), blocks_of_pass(experts)
    BIG = 1e30
    with stage(nc, name) as st:
        ones_e = st.sb("ones_e", [P, E])
        e_int, g_int = st.sb("e_int", [P, E], I32), st.sb("g_int", [P, NG], I32)
        t_int, b_int = st.sb("t_int", [P, NT], I32), st.sb("b_int", [P, NB], I32)
        e_desc, g_desc = st.sb("e_desc", [P, E]), st.sb("g_desc", [P, NG])
        t_id, b_id = st.sb("t_id", [P, NT]), st.sb("b_id", [P, NB])
        strict = st.sb("strict", [P, P])
        gx, goh, gpen = (st.sb(n, [P, NT, NG]) for n in ("gx", "goh", "gpen"))
        em, t3, oh1, oh2, both, place = (st.sb(n, [P, NT, E]) for n in ("em", "t3", "oh1", "oh2", "both", "place"))
        top, tmp, gmax, v1, v2, gw, ex, sl = (st.sb(n, [P, NT]) for n in
                                              ("top", "tmp", "gmax", "v1", "v2", "gw", "ex", "sl"))
        count, nb, ends = (st.sb(n, [P, E]) for n in ("count", "nb", "ends"))
        cmp = st.sb("cmp", [1, NB, E])
        be, pf = st.sb("be", [1, NB]), st.sb("pf", [1, 1])
        id_rows = st.sb("id_rows", [NB, P])
        ps_rank, ps_tot, ps_id = st.ps("rank"), st.ps("total"), st.ps("ids")
        s_const = st.sem("constants_ready")
        s_zero = st.sem("ids_cleared")
        s_exp = st.sem("exponent")
        s_both = st.sem("choices_ready")
        s_rank = st.sem("ranks_ready")
        s_slot = st.sem("slots_ready")
        s_scat = st.sem("ids_scattered")
        s_load = st.sem("ids_loaded")
        s_turn = st.sem("ids_turned")
        with nc.Block() as block:
            @block.gpsimd
            def _(pool):
                own = Steps(pool, st.sem("pool_step"))
                own(pool.memset(id_rows[:], 0.0))
                pool.iota(e_int[:], pattern=[[-1, E]], base=E, channel_multiplier=0)
                pool.iota(g_int[:], pattern=[[-1, NG]], base=NG, channel_multiplier=0)
                pool.iota(t_int[:], pattern=[[P, NT]], base=0, channel_multiplier=1)
                pool.iota(b_int[:], pattern=[[1, NB]], base=0, channel_multiplier=0)
                own(pool.memset(strict[:], 1.0))
                own(pool.affine_select(out=strict[:], in_=strict[:], compare_op=ALU.is_gt, fill=0.0, base=0,
                                       pattern=[[1, P]], channel_multiplier=-1))
                pool.sem_inc(s_const, 1)
                pool.wait_ge(s_slot, 2)
                pool.wait_ge(s_zero, 16)
                for k in range(2):
                    for t in range(NT):
                        pool.indirect_dma_start(
                            out=ids_d, out_offset=bass.IndirectOffsetOnAxis(ap=r["slots"][:, k, t:t + 1], axis=0),
                            in_=t_id[:, t:t + 1], in_offset=None).then_inc(s_scat, 16)

            @block.sync
            def _(sp):
                rows = ids_d.rearrange("(b p) a -> b (p a)", p=P)
                sp.wait_ge(s_const, 1)
                sp.dma_start(rows, id_rows[:]).then_inc(s_zero, 16)
                sp.wait_ge(s_zero, 16)
                sp.wait_ge(s_scat, 16 * 2 * NT)
                sp.dma_start(id_rows[:], rows).then_inc(s_load, 16)

            @block.tensor
            def _(pe):
                pe.wait_ge(s_both, 1)
                pe.wait_ge(s_const, 1)
                flat = both[:].rearrange("p t e -> p (t e)")
                pe.matmul(ps_rank[:, 0:NT * E], strict[:], flat, start=True, stop=True).then_inc(s_rank, 1)
                pe.matmul(ps_tot[:, 0:NT * E], cst["ones"][:], flat, start=True, stop=True).then_inc(s_rank, 1)
                pe.wait_ge(s_load, 16)
                pe.transpose(ps_id[:, 0:NB], id_rows[:], cst["ident"][0:NB, 0:NB]).then_inc(s_turn, 1)

            @block.scalar
            def _(act):
                act.wait_ge(s_exp, 1)
                act.activation(gx[:], gx[:], ACT.Exp).then_inc(s_exp, 1)
                act.wait_ge(s_exp, 3)
                act.activation(ex[:], ex[:], ACT.Exp).then_inc(s_exp, 1)

            @block.vector
            def _(dve):
                own = Steps(dve, st.sem("dve_step"))
                TT, TS = dve.tensor_tensor, dve.tensor_scalar

                def wide(ap, n):
                    return ap[:, :, None].broadcast_to((P, NT, n))

                def table(ap, n):
                    return ap[:, None, :].broadcast_to((P, NT, n))

                def best(src, n, desc, onehot, t, out):
                    own(dve.tensor_reduce(out[:], src, AX.X, ALU.max))
                    own(TT(t, src, wide(out[:], n), ALU.is_equal))
                    own(TT(t, t, table(desc[:], n), ALU.mult))
                    own(dve.tensor_reduce(top[:], t, AX.X, ALU.max))
                    own(TT(onehot[:], table(desc[:], n), wide(top[:], n), ALU.is_equal))

                own(dve.memset(ones_e[:], 1.0))
                dve.wait_ge(s_const, 1)
                for a, b in ((e_desc, e_int), (g_desc, g_int), (t_id, t_int), (b_id, b_int)):
                    own(dve.tensor_copy(a[:], b[:]))
                g, e = logits[:, :, 0:NG], logits[:, :, NG:NG + E]
                best(g, NG, g_desc, goh, gpen[:], gmax)
                TT(gx[:], g, wide(gmax[:], NG), ALU.subtract).then_inc(s_exp, 1)
                own(TS(gpen[:], goh[:], BIG, -BIG, ALU.mult, ALU.add))
                four = em[:].rearrange("p t (g e) -> p t g e", g=NG)
                own(TT(four, e.rearrange("p t (g e) -> p t g e", g=NG),
                       goh[:][:, :, :, None].broadcast_to((P, NT, NG, EG)), ALU.mult))
                own(TT(four, four, gpen[:][:, :, :, None].broadcast_to((P, NT, NG, EG)), ALU.add))
                best(em[:], E, e_desc, oh1, t3[:], v1)
                own(TS(t3[:], oh1[:], -1e5 * BIG, None, ALU.mult))
                own(TT(em[:], em[:], t3[:], ALU.add))
                best(em[:], E, e_desc, oh2, t3[:], v2)
                TT(both[:], oh1[:], oh2[:], ALU.add).then_inc(s_both, 1)
                dve.wait_ge(s_exp, 2)
                TT(ex[:], v2[:], v1[:], ALU.subtract).then_inc(s_exp, 1)
                own(dve.tensor_reduce(tmp[:], gx[:], AX.X, ALU.add))
                own(dve.reciprocal(gw[:], tmp[:]))
                dve.wait_ge(s_exp, 4)
                own(TS(tmp[:], ex[:], 1.0, None, ALU.add))
                own(dve.reciprocal(tmp[:], tmp[:]))
                own(TT(r["weights"][:, 0, :], gw[:], tmp[:], ALU.mult))
                own(TT(r["weights"][:, 1, :], r["weights"][:, 0, :], ex[:], ALU.mult))
                dve.wait_ge(s_rank, 2)
                tot = ps_tot[:, 0:NT * E].rearrange("p (t e) -> p t e", t=NT)
                own(dve.tensor_reduce(count[:], tot.rearrange("p t e -> p e t"), AX.X, ALU.add))
                own(TS(count[:], count[:], 1.0 / P, (P - 1.0) / (2 * P), ALU.mult, ALU.add))
                own(TS(nb[:], count[:], ROUND, ROUND, ALU.add, ALU.subtract))
                own(dve.tensor_tensor_scan(ends[:], ones_e[:], nb[:], 0.0, ALU.mult, ALU.add))
                own(TT(nb[:], ends[:], nb[:], ALU.subtract))
                own(TS(place[:, 0, :], nb[:], float(P), None, ALU.mult))
                for t in range(1, NT):
                    own(TT(place[:, t, :], place[:, t - 1, :], tot[:, t - 1, :], ALU.add))
                own(TT(place[:], place[:], ps_rank[:, 0:NT * E].rearrange("p (t e) -> p t e", t=NT), ALU.add))
                for k, oh in enumerate((oh1, oh2)):
                    own(TT(t3[:], oh[:], place[:], ALU.mult))
                    own(dve.tensor_reduce(sl[:], t3[:], AX.X, ALU.add))
                    dve.tensor_copy(r["slots"][:, k, :], sl[:]).then_inc(s_slot, 1)
                    dve.wait_ge(s_slot, k + 1)
                own(TT(cmp[:], ends[0:1, None, :].broadcast_to((1, NB, E)),
                       b_id[0:1, :, None].broadcast_to((1, NB, E)), ALU.is_le))
                own(dve.tensor_reduce(be[:], cmp[:], AX.X, ALU.add))
                own(TS(be[:], be[:], E - 1.0, None, ALU.min))
                own(dve.tensor_copy(r["expert"][:], be[:]))
                own(TS(pf[:], ends[0:1, E - 1:E], 1.0 / B, (B - 1.0) / (2 * B), ALU.mult, ALU.add))
                own(TS(pf[:], pf[:], ROUND, ROUND, ALU.add, ALU.subtract))
                own(dve.tensor_copy(r["passes"][:], pf[:]))
                dve.wait_ge(s_turn, 1)
                dve.tensor_copy(r["token"][:], ps_id[:, 0:NB])


def run_experts(nc, cst, name, experts, w1, w3, w2, v_d, y_d, r):
    NB = block_count(experts)
    B = blocks_of_pass(experts)
    K = B // 2
    KH = HID // P
    with stage(nc, name) as st:
        w13 = [st.sb(f"w13_{b}", [P, KD, 2 * HID]) for b in range(B)]
        wd = [st.sb(f"w2_{b}", [P, KH, D]) for b in range(B)]
        x = [st.sb(f"x{b}", [P, D]) for b in range(B)]
        idx = [st.sb(f"idx{b}", [P, 1], U32) for b in range(B)]
        y = [st.sb(f"y{b}", [P, D]) for b in range(B)]
        xT = [st.sb(f"xT{p}", [P, KD, P]) for p in range(2)]
        sil = [st.sb(f"silu{p}", [P, HID]) for p in range(2)]
        he = [st.sb(f"h{p}", [P, HID]) for p in range(2)]
        hT = [st.sb(f"hT{p}", [P, KH, P]) for p in range(2)]
        zero = st.sb("zero", [P, D])
        turn = [st.banks(f"turn{p}_", 2) for p in range(2)]
        up = st.banks("up", 2)
        down = [st.banks("down", 2), [turn[0][1], turn[1][1]]]
        s_idx = st.sem_n("idx_ready", B)
        s_x = st.sem_n("x_loaded", B)
        s_w13 = st.sem_n("w13_loaded", B)
        s_w2 = st.sem_n("w2_loaded", B)
        s_st = st.sem_n("y_stored", B)
        s_turn = st.sem_n("x_turned")
        s_xT = [st.sem_n("xT_by_dve"), st.sem_n("xT_by_act")]
        s_up = st.sem_n("up_ready")
        s_sil = st.sem_n("silu_ready")
        s_he = st.sem_n("h_ready")
        s_hturn = st.sem_n("h_turned")
        s_hT = st.sem_n("hT_ready")
        s_down = st.sem_n("down_ready")
        s_y = [st.sem_n("y_by_dve"), st.sem_n("y_by_act")]
        s_end = st.sem("ended")
        s_fill = st.sem("blocks_filled")
        s_zero = st.sem("zeros_ready")
        s_go = st.sem("gather_may_start")

        def passes(eng):
            return eng.value_load(r["passes"][0:1, 0:1], min_val=1, max_val=NB // B)

        with nc.Block() as block:
            @block.sync
            def _(sp):
                up1, up3, dn = (w.rearrange("e (c p) n -> p e c n", p=P) for w in (w1, w3, w2))
                n_passes = passes(sp)
                with sp.Fori(0, n_passes) as i:
                    e = [sp.value_load(r["expert"][0:1, bass.ds(B * i + b, 1)], min_val=0, max_val=experts - 1)
                         for b in range(B)]
                    for k in range(K):
                        for p in range(2):
                            b = 2 * k + p
                            sp.wait_ge(s_up[p], K * i + k + 1)
                            for n, w in enumerate((up1, up3)):
                                sp.dma_start(w13[b][:, :, n * HID:(n + 1) * HID],
                                             w[:, bass.ds(e[b], 1)].rearrange("p a c n -> p (a c) n")).then_inc(s_w13[b], 16)
                        for p in range(2):
                            b = 2 * k + p
                            sp.wait_ge(s_down[p], 2 * (K * i + k) + 2)
                            sp.dma_start(wd[b][:], dn[:, bass.ds(e[b], 1)].rearrange("p a c n -> p (a c) n")).then_inc(s_w2[b], 16)
                            sp.sem_inc(s_fill, 16)
                sp.wait_ge(s_zero, 1)
                with sp.Fori(n_passes, NB // B + 1) as i:
                    for b in range(B):
                        sp.dma_start(y_d[bass.ds((B * i + b) * P, P), :], zero[:]).then_inc(s_fill, 16)
                sp.wait_ge(s_fill, 16 * (NB + B))

            @block.gpsimd
            def _(pool):
                with pool.Fori(0, passes(pool)) as i:
                    for k in range(K):
                        for p in range(2):
                            b = 2 * k + p
                            pool.wait_ge(s_turn[p], 2 * (K * i + k) + 2)
                            pool.tensor_copy(idx[b][:], r["token"][:, bass.ds(B * i + b, 1)]).then_inc(s_idx[b], 1)
                            pool.wait_ge(s_idx[b], i + 1)
                            pool.sem_inc(s_go, 1)
                            pool.indirect_dma_start(
                                out=x[b][:], out_offset=None, in_=v_d,
                                in_offset=bass.IndirectOffsetOnAxis(ap=idx[b][:, 0:1], axis=0)).then_inc(s_x[b], 16)

            @block.tensor
            def _(pe):
                for p in range(2):
                    pe.sem_inc(s_turn[p], 2 * K)
                    pe.sem_inc(s_up[p], K)
                    pe.sem_inc(s_down[p], 2 * K)

                def turn_rows(i, k):
                    for p in range(2):
                        b = 2 * k + p
                        pe.wait_ge(s_x[b], 16 * i + 16)
                        for eng in range(2):
                            pe.wait_ge(s_y[eng][1], K * i + k + 1)
                        for h in range(2):
                            for c in range(4):
                                f = 4 * h + c
                                last = pe.transpose(turn[p][h][:, c * P:(c + 1) * P], x[b][:, f * P:(f + 1) * P],
                                                    cst["ident"][:])
                            last.then_inc(s_turn[p], 1)

                def multiply(i, k):
                    g = K * i + k
                    for p in range(2):
                        b = 2 * k + p
                        pe.wait_ge(s_w13[b], 32 * i + 32)
                        for eng in range(2):
                            pe.wait_ge(s_xT[eng][p], g + 1)
                        products(pe, up[p][:], [(xT[p][:, c, :], w13[b][:, c, :]) for c in range(KD)]).then_inc(s_up[p], 1)
                    for p in range(2):
                        pe.wait_ge(s_he[p], g + 1)
                        for c in range(KH):
                            last = pe.transpose(turn[p][0][:, c * P:(c + 1) * P], he[p][:, c * P:(c + 1) * P],
                                                cst["ident"][:])
                        last.then_inc(s_hturn[p], 1)
                    for p in range(2):
                        b = 2 * k + p
                        pe.wait_ge(s_w2[b], 16 * i + 16)
                        pe.wait_ge(s_hT[p], g + 1)
                        for h, (a, z) in enumerate(HALVES):
                            pe.wait_ge(s_y[h][p], g + 1)
                            products(pe, down[p][h][:], [(hT[p][:, c, :], wd[b][:, c, a:z])
                                                         for c in range(KH)]).then_inc(s_down[p], 1)

                with pe.Fori(0, passes(pe)) as i:
                    for k in range(K):
                        turn_rows(i, k)
                        multiply(i, k)

            def copy_half(eng, copy, e, g):
                for p in range(2):
                    eng.wait_ge(s_turn[p], 2 * g + e + 1 + 2 * K)
                    copy(xT[p][:, 4 * e:4 * e + 4, :].rearrange("p c t -> p (c t)"), turn[p][e][:]).then_inc(s_xT[e][p], 1)

            def copy_y(eng, copy, e, i, k, p):
                a, z = HALVES[e]
                b = 2 * k + p
                eng.wait_ge(s_down[p], 2 * (K * i + k) + e + 1 + 2 * K)
                eng.wait_ge(s_st[b], 16 * i + 16)
                copy(y[b][:, a:z], down[p][e][:]).then_inc(s_y[e][p], 1)

            @block.vector
            def _(dve):
                for p in range(2):
                    dve.sem_inc(s_y[0][p], 1)
                    dve.sem_inc(s_y[1][p], 1)
                for b in range(B):
                    dve.sem_inc(s_st[b], 16)
                dve.memset(zero[:], 0.0).then_inc(s_zero, 1)
                with dve.Fori(0, passes(dve)) as i:
                    for k in range(K):
                        g = K * i + k
                        copy_half(dve, dve.tensor_copy, 0, g)
                        for p in range(2):
                            dve.wait_ge(s_sil[p], g + 1)
                            dve.tensor_tensor(he[p][:], up[p][:, HID:], sil[p][:], ALU.mult).then_inc(s_he[p], 1)
                        for p in range(2):
                            dve.wait_ge(s_hturn[p], g + 1)
                            dve.tensor_copy(hT[p][:].rearrange("p c t -> p (c t)"), turn[p][0][:, 0:HID]).then_inc(s_hT[p], 1)
                        for p in range(2):
                            copy_y(dve, dve.tensor_copy, 0, i, k, p)

            @block.scalar
            def _(act):
                n = passes(act)
                with act.Fori(0, n) as i:
                    for k in range(K):
                        g = K * i + k
                        copy_half(act, act.copy, 1, g)
                        for p in range(2):
                            act.wait_ge(s_up[p], g + 1 + K)
                            act.activation(sil[p][:], up[p][:, 0:HID], ACT.Silu).then_inc(s_sil[p], 1)
                        for p in range(2):
                            copy_y(act, act.copy, 1, i, k, p)
                        for p in range(2):
                            b = 2 * k + p
                            act.wait_ge(s_y[0][p], g + 2)
                            act.wait_ge(s_y[1][p], g + 2)
                            act.dma_start(y_d[bass.ds((B * i + b) * P, P), :], y[b][:]).then_inc(s_st[b], 16)
                for b in range(B):
                    act.wait_ge(s_st[b], 16 * n + 16)
                    act.sem_inc(s_end, 1)


def combine(nc, name, r, h_d, y_d, g_row, out_d):
    with stage(nc, name) as st:
        h = st.sb("h", [P, NT, D])
        y = [[st.sb(f"y{k}_{q}", [P, D]) for q in range(2)] for k in range(2)]
        g = st.sb("g", [P, D])
        junk = st.sb("squares", [P, D])
        ss, ms, rt, inv = (st.sb(n, [P, NT]) for n in ("sums", "mean", "root", "inverse"))
        s_h = st.sem_n("h_loaded", NT)
        s_g = st.sem("g_loaded")
        s_y = [st.sem_n("y0_loaded"), st.sem_n("y1_loaded")]
        s_sum = st.sem("summed")
        s_ss, s_ms, s_rt, s_inv, s_out = (st.sem(n) for n in ("sum_ready", "mean_ready", "root_ready",
                                                             "inverse_ready", "out_ready"))
        s_st = st.sem("stored")
        with nc.Block() as block:
            @block.sync
            def _(sp):
                if g_row is not None:
                    sp.dma_start(g[:], g_row.to_broadcast((P, D))).then_inc(s_g, 16)
                for t in range(NT):
                    sp.dma_start(h[:, t, :], h_d[t * P:(t + 1) * P, :]).then_inc(s_h[t], 16)
                for t in range(NT):
                    sp.wait_ge(s_out if g_row is not None else s_sum, t + 1 if g_row is not None else 2 * t + 2)
                    sp.dma_start(out_d[t * P:(t + 1) * P, :], h[:, t, :]).then_inc(s_st, 16)
                sp.wait_ge(s_st, 16 * NT)

            @block.gpsimd
            def _(pool):
                for t in range(NT):
                    for k in range(2):
                        if t >= 2:
                            pool.wait_ge(s_sum, 2 * (t - 2) + k + 1)
                        pool.indirect_dma_start(
                            out=y[k][t % 2][:], out_offset=None, in_=y_d,
                            in_offset=bass.IndirectOffsetOnAxis(ap=r["slots"][:, k, t:t + 1], axis=0)
                        ).then_inc(s_y[k][t % 2], 16)

            @block.vector
            def _(dve):
                for t in range(NT):
                    dve.wait_ge(s_h[t], 16)
                    for k in range(2):
                        dve.wait_ge(s_y[k][t % 2], 16 * (t // 2 + 1))
                        dve.scalar_tensor_tensor(out=h[:, t, :], in0=y[k][t % 2][:],
                                                 scalar=r["weights"][:, k, t:t + 1], in1=h[:, t, :],
                                                 op0=ALU.mult, op1=ALU.add).then_inc(s_sum, 1)
                        dve.wait_ge(s_sum, 2 * t + k + 1)
                    if g_row is not None:
                        dve.wait_ge(s_ss, t + 1)
                        dve.tensor_scalar(ms[:, t:t + 1], ss[:, t:t + 1], 1.0 / D, EPS, ALU.mult,
                                          ALU.add).then_inc(s_ms, 1)
                        dve.wait_ge(s_rt, t + 1)
                        dve.reciprocal(inv[:, t:t + 1], rt[:, t:t + 1]).then_inc(s_inv, 1)
                        dve.wait_ge(s_inv, t + 1)
                        dve.wait_ge(s_g, 16)
                        dve.scalar_tensor_tensor(out=h[:, t, :], in0=h[:, t, :], scalar=inv[:, t:t + 1],
                                                 in1=g[:], op0=ALU.mult, op1=ALU.mult).then_inc(s_out, 1)

            if g_row is not None:
                @block.scalar
                def _(act):
                    for t in range(NT):
                        act.wait_ge(s_sum, 2 * t + 2)
                        act.activation(junk[:], h[:, t, :], ACT.Square, accum_out=ss[:, t:t + 1]).then_inc(s_ss, 1)
                        act.wait_ge(s_ms, t + 1)
                        act.activation(rt[:, t:t + 1], ms[:, t:t + 1], ACT.Sqrt).then_inc(s_rt, 1)



def recurrent_branch(nc, cst, col, w_in, wa, wx, uT, mergedT, scratch):
    BW = 256
    NCH = BW // P
    NB = D // BW
    CW = 4
    UNITS = 6 * 2 * NCH
    LRU_UNITS = 2 * 2 * NCH
    RING = 4
    NW = 4 * NCH
    R_W = 2

    def units_through(j):
        return 2 * (j + 1) + (LRU_UNITS if j >= NW - NCH else 0)

    src = chunked(w_in)
    with stage(nc, "rnn") as st:
        raw = [st.sb(f"raw{j}", [P, KD, P]) for j in range(2)]
        w3 = [[st.sb(f"w_{n}{j}", [P, KD, P], F32R) for n in ("high", "low")] for j in range(R_W)]
        wl = [st.sb(n, [P, NCH, BW]) for n in ("wr", "wi")]
        xr = st.sb("xr", [P, NCH, CW - 1 + S])
        xa = st.sb("xa", [P, NCH, S])
        ge, gt, rr, ii = (scratch[:, NCH * n:NCH * (n + 1), :] for n in range(4))
        aa = st.sb("a", [P, NCH, S])
        gm = st.sb("gate_1", [P, NCH, S])
        cw, cb = st.sb("conv_w", [P, CW, NCH]), st.sb("conv_b", [P, NCH])
        ba, bx, lc, nlc = (st.sb(n, [P, NCH]) for n in ("ba", "bx", "lc", "nlc"))
        x8, m8, z8, q8, sp8 = (st.sb(n, [P, KD]) for n in ("x8", "m8", "z8", "q8", "sp8"))
        ps = st.banks("ps", RING)
        s_raw = st.sem_n("w_loaded")
        s_w = st.sem("w_split")
        s_wl = st.sem("lru_w_loaded")
        s_ps = st.sem("unit_ready")
        s_ev = st.sem("unit_copied")
        s_xa = st.sem("xa_ready")
        s_col = st.sem("columns_ready")
        s_x8 = st.sem("lambda_step")
        s_a = st.sem("a_ready")
        s_d = st.sem("ratio_ready")
        s_m = st.sem("mult_ready")
        s_done = st.sem("block_done")
        with nc.Block() as block:
            @block.sync
            def _(sp):
                with sp.Fori(0, NB) as q:
                    for j in range(NW):
                        if j == NW - NCH:
                            sp.wait_ge(s_ps, UNITS * q + UNITS)
                            for n, w in enumerate((wa, wx)):
                                sp.dma_start(wl[n][:], w[bass.ds(q, 1)].rearrange("a (c p) n -> p (a c) n", p=P)).then_inc(s_wl, 16)
                        c0 = (C_XR, C_GR, C_GT, C_GT + D)[j // NCH] + P * (j % NCH)
                        sp.wait_ge(s_w, NW * q + j + 1)
                        sp.dma_start(raw[j % 2][:], src[:, :, bass.ds(c0 + BW * q, P)]).then_inc(s_raw[j % 2], 16)

            @block.gpsimd
            def _(pool):
                own = Steps(pool, st.sem("pool_step"))
                pool.sem_inc(s_w, 2)
                with pool.Fori(0, NB) as q:
                    own.enter(q, 2 * NW)
                    for j in range(NW):
                        pool.wait_ge(s_raw[j % 2], 16 * (NW // 2) * q + 16 * (j // 2) + 16)
                        used = units_through(j - R_W) if j >= R_W else units_through(NW + j - R_W) - UNITS
                        pool.wait_ge(s_ps, UNITS * q + used + UNITS)
                        split(pool, own, raw[j % 2][:], w3[j % R_W][0][:], w3[j % R_W][1][:], True).then_inc(s_w, 1)
                own.leave(NB, 2 * NW)

            @block.tensor
            def _(pe):
                pe.sem_inc(s_ps, UNITS)
                with pe.Fori(0, NB) as q:
                    def multiply_u(j):
                        pe.wait_ge(s_w, NW * q + j + 3)
                        for h, (a, b) in enumerate(HALVES):
                            u = units_through(j) - 2 + h
                            pe.wait_ge(s_ev, UNITS * q + u + 1)
                            split_products(pe, ps[u % RING][:],
                                           [([w[:, k, :] for w in w3[j % R_W]], [x[:, k, a:b] for x in uT])
                                            for k in range(KD)]).then_inc(s_ps, 1)

                    for j in range(NW - NCH):
                        multiply_u(j)
                    u = units_through(NW - NCH - 1)
                    pe.wait_ge(s_wl, 32 * q + 32)
                    pe.wait_ge(s_xa, NCH * q + 2 * NCH)
                    for n in range(2):
                        for c in range(NCH):
                            for a, b in HALVES:
                                pe.wait_ge(s_ev, UNITS * q + u + 1)
                                products(pe, ps[u % RING][:], [(wl[n][:, k, c * P:(c + 1) * P], xa[:, k, a:b])
                                                               for k in range(NCH)]).then_inc(s_ps, 1)
                                u += 1
                    for j in range(NW - NCH, NW):
                        multiply_u(j)

            @block.scalar
            def _(act):
                act.wait_ge(s_x8, 1)
                act.activation(x8[:], x8[:], ACT.Exp).then_inc(s_x8, 1)
                act.sem_inc(s_ev, RING)
                with act.Fori(0, NB) as q:
                    act.wait_ge(s_xa, NCH * q + NCH)
                    u = 0
                    kinds = ((xr, ACT.Copy, None), (ge, ACT.Gelu_apprx_tanh, None), (gt, ACT.Sigmoid, None),
                             (rr, ACT.Sigmoid, ba), (ii, ACT.Sigmoid, bx))
                    for n, (dst, f, bias) in enumerate(kinds):
                        if n == 1:
                            act.wait_ge(s_done, q + 1)
                        if n == 3:
                            act.wait_ge(s_col, q + 1)
                        for c in range(NCH):
                            for a, b in HALVES:
                                act.wait_ge(s_ps, UNITS * q + u + 1 + UNITS)
                                at = CW - 1 if n == 0 else 0
                                kw = dict(bias=bias[:, c:c + 1]) if bias is not None else {}
                                act.activation(dst[:, c, at + a:at + b], ps[u % RING][:], f, **kw).then_inc(s_ev, 1)
                                u += 1
                    act.wait_ge(s_ev, UNITS * q + u + RING)
                    for c in range(NCH):
                        act.activation(aa[:, c, :], rr[:, c, :], ACT.Exp, scale=nlc[:, c:c + 1]).then_inc(s_a, 1)
                        act.wait_ge(s_a, 2 * NCH * q + 2 * c + 1)
                        act.activation(rr[:, c, :], rr[:, c, :], ACT.Tanh, scale=lc[:, c:c + 1]).then_inc(s_a, 1)
                    for c in range(NCH):
                        act.wait_ge(s_d, NCH * q + c + 1)
                        act.activation(rr[:, c, :], rr[:, c, :], ACT.Sqrt, scale=2.0).then_inc(s_m, 1)
                    for c in range(NCH):
                        for a, b in HALVES:
                            act.wait_ge(s_ps, UNITS * q + u + 1 + UNITS)
                            act.activation(gm[:, c, a:b], ps[u % RING][:], ACT.Sigmoid).then_inc(s_ev, 1)
                            u += 1

            @block.vector
            def _(dve):
                own = Steps(dve, st.sem("dve_step"))
                TT, TS, STT = dve.tensor_tensor, dve.tensor_scalar, dve.scalar_tensor_tensor
                own(dve.memset(xr[:, :, 0:CW - 1], 0.0))
                lam = col["lru_lambda"]
                own(TS(m8[:], lam, -1.0, None, ALU.mult))
                TT(x8[:], m8[:], lam, ALU.min).then_inc(s_x8, 1)
                own(TS(m8[:], m8[:], 0.0, None, ALU.max))
                dve.wait_ge(s_x8, 2)
                own(TS(z8[:], x8[:], 2.0, None, ALU.add))
                own(dve.reciprocal(z8[:], z8[:]))
                own(TT(z8[:], z8[:], x8[:], ALU.mult))
                own(TT(q8[:], z8[:], z8[:], ALU.mult))
                own(dve.memset(sp8[:], 1.0 / 17))
                for d in range(15, 0, -2):
                    own(TT(sp8[:], sp8[:], q8[:], ALU.mult))
                    own(TS(sp8[:], sp8[:], 1.0 / d, None, ALU.add))
                own(TT(sp8[:], sp8[:], z8[:], ALU.mult))
                own(STT(out=sp8[:], in0=sp8[:], scalar=2.0, in1=m8[:], op0=ALU.mult, op1=ALU.add))
                own(TS(sp8[:], sp8[:], LRU_C, None, ALU.mult))
                own.leave(1, own.n)
                dve.sem_inc(s_done, 1)
                dve.sem_inc(s_xa, NCH)
                per = NCH * (CW - 1) + 2 + 2 * NCH + 5 * NCH - 1
                with dve.Fori(0, NB) as q:
                    own.enter(q, per)
                    at = bass.ds(NCH * q, NCH)
                    dve.tensor_copy(cw[:], col["conv_w2"].rearrange("p (j c) -> p j c", j=CW)[:, :, at])
                    for dst, name in ((cb, "conv_b2"), (ba, "lru_ba"), (bx, "lru_bx")):
                        dve.tensor_copy(dst[:], col[name][:, at])
                    dve.tensor_copy(lc[:], sp8[:, at])
                    TS(nlc[:], sp8[:, at], -1.0, None, ALU.mult).then_inc(s_col, 1)
                    dve.wait_ge(s_col, q + 1)
                    for c in range(NCH):
                        dve.wait_ge(s_ev, UNITS * q + 2 * c + 2 + RING)
                        own(TS(xa[:, c, :], xr[:, c, 0:S], cw[:, 0, c:c + 1], cb[:, c:c + 1], ALU.mult, ALU.add))
                        for j in range(1, CW):
                            ins = STT(out=xa[:, c, :], in0=xr[:, c, j:j + S], scalar=cw[:, j, c:c + 1],
                                      in1=xa[:, c, :], op0=ALU.mult, op1=ALU.add)
                            if j < CW - 1:
                                own(ins)
                            else:
                                ins.then_inc(s_xa, 1)
                    dve.wait_ge(s_ev, UNITS * q + 6 * NCH + RING)
                    own(TT(ge[:], ge[:], gt[:], ALU.mult))
                    dve.wait_ge(s_ev, UNITS * q + UNITS - 2 * NCH + RING)
                    dve.wait_ge(s_xa, NCH * q + 2 * NCH)
                    own(TT(ii[:], ii[:], xa[:], ALU.mult))
                    for c in range(NCH):
                        dve.wait_ge(s_a, 2 * NCH * q + 2 * c + 2)
                        own(TS(gt[:, c, :], rr[:, c, :], 1.0, None, ALU.add))
                        own(dve.reciprocal(gt[:, c, :], gt[:, c, :]))
                        TT(rr[:, c, :], rr[:, c, :], gt[:, c, :], ALU.mult).then_inc(s_d, 1)
                    for c in range(NCH):
                        dve.wait_ge(s_m, NCH * q + c + 1)
                        own(TT(ii[:, c, :], ii[:, c, :], rr[:, c, :], ALU.mult))
                        own(dve.tensor_tensor_scan(gt[:, c, :], aa[:, c, :], ii[:, c, :], 0.0, ALU.mult, ALU.add))
                        dst = mergedT[:, bass.ds(NCH * q + c, 1), :].rearrange("p a t -> p (a t)")
                        own(TT(ge[:, c, :], gt[:, c, :], ge[:, c, :], ALU.mult))
                        dve.wait_ge(s_ev, UNITS * q + UNITS - 2 * (NCH - 1 - c) + RING)
                        own(TT(dst, dst, gm[:, c, :], ALU.mult))
                        if c < NCH - 1:
                            own(TT(dst, dst, ge[:, c, :], ALU.add))
                        else:
                            TT(dst, dst, ge[:, c, :], ALU.add).then_inc(s_done, 1)
                    dve.wait_ge(s_done, q + 2)
                own.leave(NB, per)



def rotations_and_rotated_key(cst, raw, pos_i, g, tables, uT, kpe):
    import numpy as np
    half = ROPE // 2
    freq = np.float32(10000.0) ** (-np.arange(half, dtype=np.float32) / np.float32(half))
    two_pi = 2 * np.pi
    c1 = 6.28125
    c2 = float(np.float32(np.round((two_pi - c1) * 2 ** 21) / 2 ** 21))
    c3 = float(np.float32(two_pi - c1 - c2))

    def along(st):
        wb = [st.sb(f"kpe_w_{n}", [P, KD, ROPE], F32R) for n in ("high", "low")]
        kT = st.sb("kpeT", [ROPE, S])
        acc = st.banks("kpe_acc", 2)
        turned = st.ps("kpe_turned")
        s_split, s_acc = st.sem("kpe_w_split"), st.sem("kpe_acc_ready")
        s_kT, s_turn = st.sem("kpeT_ready"), st.sem("kpe_turned")
        pos = st.sb("pos", [P, NT])
        fr = st.sb("freq", [P, half])
        ang, k, sn, cs, ov = (st.sb(n, [P, NT, half]) for n in ("angle", "turns", "sin", "cos", "over"))
        s_r, s_trig = st.sem("angles_ready"), st.sem("trig_ready")
        s_step = st.sem("dve_step")

        def tensor(pe):
            pe.wait_ge(s_split, 1)
            for h, (a, b) in enumerate(HALVES):
                split_products(pe, acc[h][0:ROPE, :],
                               [([w[:, c, :] for w in wb], [u[:, c, a:b] for u in uT])
                                for c in range(KD)]).then_inc(s_acc, 1)

        def tensor_end(pe):
            pe.wait_ge(s_kT, 2)
            for t in range(NT):
                last = pe.transpose(turned[:, t * ROPE:(t + 1) * ROPE], kT[:, t * P:(t + 1) * P],
                                    cst["ident"][0:ROPE, 0:ROPE])
            last.then_inc(s_turn, 1)

        def vector_end(dve):
            dve.wait_ge(s_turn, 1)
            dve.tensor_copy(kpe[:].rearrange("p t r -> p (t r)"), turned[:, 0:NT * ROPE])

        def scalar(act):
            act.wait_ge(s_r, 1)
            act.activation(sn[:], ang[:], ACT.Sin).then_inc(s_trig, 1)
            act.wait_ge(s_r, 2)
            act.activation(cs[:], cs[:], ACT.Sin).then_inc(s_trig, 1)

        def vector(dve):
            own = Steps(dve, s_step)
            TT, TS, STT = dve.tensor_tensor, dve.tensor_scalar, dve.scalar_tensor_tensor
            split(dve, own, raw[:], wb[0][:], wb[1][:]).then_inc(s_split, 1)
            for j in range(half):
                own(dve.memset(fr[:, j:j + 1], float(freq[j])))
            own(dve.tensor_copy(pos[:], pos_i[:]))
            own(TT(ang[:], pos[:, :, None].broadcast_to((P, NT, half)),
                   fr[:, None, :].broadcast_to((P, NT, half)), ALU.mult))
            own(TS(k[:], ang[:], 1.0 / two_pi, None, ALU.mult))
            own(TS(k[:], k[:], ROUND, ROUND, ALU.add, ALU.subtract))
            for c in (c1, c2, c3):
                own(STT(out=ang[:], in0=k[:], scalar=-c, in1=ang[:], op0=ALU.mult, op1=ALU.add))
            own(TS(cs[:], ang[:], two_pi / 4, None, ALU.add))
            TS(ang[:], ang[:], 3.1415925, -3.1415925, ALU.min, ALU.max).then_inc(s_r, 1)
            own(TS(ov[:], cs[:], two_pi / 2, -two_pi, ALU.is_gt, ALU.mult))
            own(TT(cs[:], cs[:], ov[:], ALU.add))
            TS(cs[:], cs[:], 3.1415925, -3.1415925, ALU.min, ALU.max).then_inc(s_r, 1)
            dve.wait_ge(s_trig, 2)
            for n in range(2):
                for i, (tr, h) in enumerate(((cs, 0), (sn, 1), (sn, 0), (cs, 1))):
                    gg = g[:, n, h * half:(h + 1) * half]
                    TT(tables[n][:, i], tr[:], gg[:, None, :].broadcast_to((P, NT, half)), ALU.mult)
            for h, (a, b) in enumerate(HALVES):
                dve.wait_ge(s_acc, h + 1)
                dve.tensor_copy(kT[:, a:b], acc[h][0:ROPE, :]).then_inc(s_kT, 1)

        return dict(tensor=tensor, tensor_end=tensor_end, vector=vector, vector_end=vector_end, scalar=scalar)
    return along


def queries_keys_values(nc, cst, col, w_uq, w_ukv, lat, inv_l, kpe, tables, q_d, k_d, v):
    NQ, NKV = QL // P, KVL // P
    half = ROPE // 2
    QU, KU = H2 * QKH // BANK, H2 * (QKN + VH) // BANK
    NU = QU + KU
    HB = BANK // P
    KH = BANK // (QKN + VH)
    with stage(nc, "qkv") as st:
        wq = st.sb("wq", [P, NQ, H2 * QKH])
        wkv = st.sb("wkv", [P, NKV, H2 * (QKN + VH)])
        qk = [[st.sb(f"{n}{b}", [P, H2, QKH]) for b in range(2)] for n in ("q", "k")]
        sq = st.sb("squares", [P, H2, QKH])
        ss, ms, rt, iv = ([st.sb(f"{n}{i}", [P, H2]) for i in range(2)] for n in ("sums", "mean", "root", "inverse"))
        rot = [st.sb(f"rot{i}", [P, H2, half]) for i in range(4)]
        outT = [st.sb(f"outT{i}", [QKH, HB, P]) for i in range(4)]
        acc, turn = st.banks("acc", 4), st.banks("turn", 4)
        lat_sq, lat_sum = v[:], turn[3]
        lat_parts = ((0, NQ, QL), (NQ, NQ + NKV, KVL))
        lat_ms, lat_rt = st.sb("latent_mean", [P, NT, 2]), st.sb("latent_root", [P, NT, 2])
        s_lsq, s_lsum, s_lms, s_lrt = (st.sem(n) for n in ("latents_squared", "latents_summed", "latents_mean",
                                                           "latents_root"))
        s_lat = st.sem("latents_ready")
        s_wq, s_wkv = st.sem("wq_loaded"), st.sem("wkv_loaded")
        s_acc = st.sem("acc_ready")
        s_q, s_kv = st.sem("q_copied"), st.sem("kv_copied")
        s_full = st.sem("k_complete")
        s_sq, s_ss, s_ms, s_rt = (st.sem(n) for n in ("squared", "summed", "mean_ready", "root_ready"))
        s_fin = st.sem("rotated")
        s_turn = st.sem("turned")
        s_out = st.sem("out_ready")
        s_st = st.sem_n("stored", 4)
        dests = (q_d.rearrange("h r s -> r h s"), k_d.rearrange("h r s -> r h s"))
        NB = H2 // HB
        with nc.Block() as block:
            @block.sync
            def _(sp):
                for k in range(NQ):
                    sp.dma_start(wq[:, k, :], w_uq[k * P:(k + 1) * P, :]).then_inc(s_wq, 16)
                for k in range(NKV):
                    sp.dma_start(wkv[:, k, :], w_ukv[k * P:(k + 1) * P, :]).then_inc(s_wkv, 16)
                for t in range(NT):
                    for m in range(2 * NB):
                        g = 2 * NB * t + m
                        sp.wait_ge(s_out, g + 1)
                        sp.dma_start(dests[m // NB][:, HB * (m % NB):HB * (m % NB + 1), t * P:(t + 1) * P],
                                     outT[g % 4][:]).then_inc(s_st[g % 4], 16)
                for n in range(4):
                    sp.wait_ge(s_st[n], 16 * 2 * NB * NT // 4)

            @block.tensor
            def _(pe):
                pe.wait_ge(s_lsq, NQ + NKV)
                for t in range(NT):
                    for n, (a, b, _) in enumerate(lat_parts):
                        products(pe, lat_sum[:, 2 * t + n:2 * t + n + 1],
                                 [(lat_sq[:, k, t * P:(t + 1) * P], cst["ones"][:, 0:1]) for k in range(a, b)]
                                 ).then_inc(s_lsum, 1)

                def project(t, units):
                    for u in units:
                        g = NU * t + u
                        if g == 0:
                            pe.wait_ge(s_lat, NQ + NKV)
                            pe.wait_ge(s_wq, 16 * NQ)
                        if g == QU:
                            pe.wait_ge(s_wkv, 16 * NKV)
                        if g >= 4:
                            t0, u0 = divmod(g - 4, NU)
                            if u0 < QU:
                                pe.wait_ge(s_q, QU * t0 + u0 + 1)
                            else:
                                pe.wait_ge(s_kv, 2 * (KU * t0 + u0 - QU + 1))
                        if u < QU:
                            pairs = [(lat[:, k, t * P:(t + 1) * P], wq[:, k, u * BANK:(u + 1) * BANK])
                                     for k in range(NQ)]
                        else:
                            pairs = [(lat[:, NQ + k, t * P:(t + 1) * P],
                                      wkv[:, k, (u - QU) * BANK:(u - QU + 1) * BANK]) for k in range(NKV)]
                        products(pe, acc[g % 4][:], pairs).then_inc(s_acc, 1)

                def turn_heads(t, i):
                    pe.wait_ge(s_fin, 2 * t + i + 1)
                    for m in range(NB):
                        g = 2 * NB * t + NB * i + m
                        if g >= 4:
                            pe.wait_ge(s_out, g - 3)
                        for h in range(HB):
                            last = pe.transpose(turn[g % 4][0:QKH, h * P:(h + 1) * P], qk[i][t % 2][:, HB * m + h, :],
                                                cst["ident"][:])
                        last.then_inc(s_turn, 1)

                for t in range(NT + 1):
                    if t < NT:
                        project(t, range(QU))
                    if t:
                        turn_heads(t - 1, 0)
                        turn_heads(t - 1, 1)
                    if t < NT:
                        project(t, range(QU, NU))

            @block.scalar
            def _(act):
                def copy_heads(t):
                    for m in range(2 * NB):
                        g = 2 * NB * t + m
                        act.wait_ge(s_turn, g + 1)
                        if g >= 4:
                            act.wait_ge(s_st[g % 4], 16 * (g // 4))
                        act.activation(outT[g % 4][:].rearrange("p h t -> p (h t)"), turn[g % 4][0:QKH, :], ACT.Copy,
                                       scale=col["qk_g"][0:QKH, m // NB:m // NB + 1]).then_inc(s_out, 1)

                for c in range(NQ + NKV):
                    act.activation(lat_sq[:, c, :], lat[:, c, :], ACT.Square).then_inc(s_lsq, 1)
                act.wait_ge(s_lms, 2)
                act.activation(lat_rt[:], lat_ms[:], ACT.Sqrt).then_inc(s_lrt, 1)
                act.wait_ge(s_lrt, 2)
                for t in range(NT):
                    for u in range(QU):
                        act.wait_ge(s_acc, NU * t + u + 1)
                        if t >= 2:
                            act.wait_ge(s_turn, 2 * NB * (t - 1))
                        act.activation(qk[0][t % 2][:].rearrange("p h d -> p (h d)")[:, u * BANK:(u + 1) * BANK],
                                       acc[(NU * t + u) % 4][:], ACT.Copy, scale=inv_l[:, t, 0:1]).then_inc(s_q, 1)
                    if t:
                        copy_heads(t - 1)
                    act.wait_ge(s_q, QU * t + QU)
                    if t:
                        act.wait_ge(s_ss, 2 * t)
                    act.activation(sq[:], qk[0][t % 2][:], ACT.Square).then_inc(s_sq, 1)
                    act.wait_ge(s_full, t + 1)
                    act.wait_ge(s_ss, 2 * t + 1)
                    act.activation(sq[:], qk[1][t % 2][:], ACT.Square).then_inc(s_sq, 1)
                    for i in range(2):
                        act.wait_ge(s_ms, 2 * t + i + 1)
                        act.activation(rt[i][:], ms[i][:], ACT.Sqrt).then_inc(s_rt, 1)
                copy_heads(NT - 1)

            @block.vector
            def _(dve):
                own = Steps(dve, st.sem("dve_step"))
                TT, TS = dve.tensor_tensor, dve.tensor_scalar
                for c in range(NQ + NKV):
                    dve.wait_ge(s_lsq, c + 1)
                    TS(lat[:, c, :], lat[:, c, :], col["latent_g"][:, c:c + 1], None, ALU.mult).then_inc(s_lat, 1)
                dve.wait_ge(s_lsum, 2 * NT)
                for n, (_, _, width) in enumerate(lat_parts):
                    TS(lat_ms[:, :, n], lat_sum[:, 0:2 * NT].rearrange("p (t n) -> p t n", n=2)[:, :, n],
                       1.0 / width, EPS, ALU.mult, ALU.add).then_inc(s_lms, 1)
                dve.wait_ge(s_lrt, 1)
                dve.reciprocal(inv_l[:], lat_rt[:]).then_inc(s_lrt, 1)
                dve.wait_ge(s_lrt, 2)
                for t in range(NT):
                    if t >= 2:
                        dve.wait_ge(s_turn, 2 * NB * (t - 1))
                    q_k = [qk[i][t % 2] for i in range(2)]
                    for u in range(KU):
                        dve.wait_ge(s_acc, NU * t + QU + u + 1)
                        kv = acc[(NU * t + QU + u) % 4][:].rearrange("p (h d) -> p h d", h=KH)
                        TS(q_k[1][:, KH * u:KH * (u + 1), 0:QKN], kv[:, :, 0:QKN], inv_l[:, t, 1:2], None,
                           ALU.mult).then_inc(s_kv, 1)
                        TS(v[:, t, KH * u * VH:KH * (u + 1) * VH].rearrange("p (h d) -> p h d", h=KH),
                           kv[:, :, QKN:], inv_l[:, t, 1:2], None, ALU.mult).then_inc(s_kv, 1)
                    dve.tensor_copy(q_k[1][:, :, QKN:QKH],
                                    kpe[:, t, None, :].broadcast_to((P, H2, ROPE))).then_inc(s_full, 1)
                    for i in range(2):
                        dve.wait_ge(s_sq, 2 * t + i + 1)
                        dve.tensor_reduce(ss[i][:], sq[:], AX.X, ALU.add).then_inc(s_ss, 1)
                        dve.wait_ge(s_ss, 2 * t + i + 1)
                        TS(ms[i][:], ss[i][:], 1.0 / QKH, EPS, ALU.mult, ALU.add).then_inc(s_ms, 1)
                    for i in range(2):
                        dve.wait_ge(s_rt, 2 * t + i + 1)
                        own(dve.reciprocal(iv[i][:], rt[i][:]))
                        own(TT(q_k[i][:], q_k[i][:], iv[i][:, :, None].broadcast_to((P, H2, QKH)), ALU.mult))
                        x1, x2 = q_k[i][:, :, QKN:QKN + half], q_k[i][:, :, QKN + half:QKH]
                        for n, (x, tab) in enumerate(((x1, 0), (x2, 1), (x1, 2), (x2, 3))):
                            last = TT(rot[n][:], x, tables[i][:, tab, t, None, :].broadcast_to((P, H2, half)), ALU.mult)
                            own(last)
                        own(TT(x1, rot[0][:], rot[1][:], ALU.subtract))
                        TT(x2, rot[2][:], rot[3][:], ALU.add).then_inc(s_fin, 1)
                        dve.wait_ge(s_fin, 2 * t + i + 1)



def routing_results(st, experts):
    NB = block_count(experts)
    return dict(weights=st.sb("weights", [P, 2, NT]), slots=st.sb("slots", [P, 2, NT], U32),
                passes=st.sb("passes", [1, 1], I32), expert=st.sb("expert", [1, NB], I32),
                token=st.sb("token", [P, NB], U32))


def moe(nc, cst, name, experts, logits, w1, w3, w2, h_d, v_d, g_row, out_d):
    NB, B = block_count(experts), blocks_of_pass(experts)
    ids_d = nc.dram_tensor(f"{name}_ids", (NB * P, 1), F32).ap()
    y_d = nc.dram_tensor(f"{name}_y", ((NB + B) * P, D), F32).ap()
    with stage(nc, name) as st:
        r = routing_results(st, experts)
        route_tokens(nc, cst, f"{name}_route", experts, logits, ids_d, r)
        run_experts(nc, cst, f"{name}_run", experts, w1, w3, w2, v_d, y_d, r)
        combine(nc, f"{name}_sum", r, h_d, y_d, g_row, out_d)


def first_block(nc, cst, col, a, x2_d):
    h_d = nc.dram_tensor("h1", (S, D), F32).ap()
    v_d = nc.dram_tensor("v1", (S, D), F32).ap()
    negf_d = nc.dram_tensor("neg_f", (H1, T1), F32).ap()
    x = a["x"][0]
    w_in = a["w_in"][0]
    with stage(nc, "block1") as st:
        logits = st.sb("logits", [P, NT, NG + NE1])
        with ExitStack() as inner:
            def sb(name, shape, dt=F32):
                return inner.enter_context(nc.sbuf_tensor(name, shape, dt))
            NTK = -(-T1 // P)
            flat = sb("features1", [P, AT_BG * T1 + NTK * H1 * DH])
            pT = flat[:, 0:(AT_K + KD) * T1].rearrange("p (c t) -> p c t", t=T1)
            v = flat[:, AT_BG * T1:].rearrange("p (t n) -> p t n", t=NTK)
            oT = pT[:, AT_Q:AT_Q + 4, 0:S]
            mergedT = pT[:, AT_K:AT_K + KD, 0:S]
            fg_w, fg_b = sb("forget_w", [P, KD, H1]), sb("forget_b", [H1, 1])
            uT_mem = ExitStack()
            uT = [uT_mem.enter_context(nc.sbuf_tensor(f"uT1_{n}", [P, KD, T1], F32R)) for n in ("high", "low")]
            norm_to_features(nc, cst, "norm1", [(a["meta"], META)] + [(x[t * P:(t + 1) * P, :], P) for t in range(NT)],
                             a["norm1_g"], uT, 0,
                             [(fg_w[:], chunked(w_in)[:, :, C_FG:C_FG + H1]),
                              (fg_b[:], a["b_forget"].rearrange("a h -> h a"))])
            project_features(nc, "proj1", w_in, 0, RUNS_MIX, uT, PIECES1, pT,
                             along=forget_sums(fg_w, fg_b, uT, negf_d))
            mixers_and_projections(nc, cst, col, a["pool_w"][0], w_in, RUNS_QK, uT, pT, v)
            def load_head(sp, p, j, q_aug, k_aug, sem):
                rows = slice(DH * p, DH * p + DH)
                sp.dma_start(q_aug[0:DH, :], pT[rows, bass.ds(AT_Q + j, 1), META:T1].rearrange("p c t -> p (c t)")).then_inc(sem, 16)
                sp.dma_start(k_aug[0:DH, :], pT[rows, bass.ds(AT_K + j, 1), :].rearrange("p c t -> p (c t)")).then_inc(sem, 16)
                sp.dma_start(k_aug[DH:DH + 1, :], negf_d[bass.ds(2 * j + p, 1), :]).then_inc(sem, 16)

            attention(nc, cst, "fox", H1, META, DH, cst["causal"], load_head, 3, v, oT, 1)
            merge_branches(nc, w_in, [a["w_out_a"][0], a["w_out_b"][0], a["w_out_c"][0]],
                           lambda k, x0, x1: [u[:, k, META + x0:META + x1] for u in uT],
                           [(lambda k, x0, x1: pT[:, AT_A + k, META + x0:META + x1], 2),
                            (lambda k, x0, x1: pT[:, AT_BV + k, META + x0:META + x1], 2),
                            (lambda k, x0, x1: oT[:, k, x0:x1], 4)], mergedT)
            uT_mem.close()
            output_and_router(nc, cst, "out1", mergedT, a["w_o"][0], x, a["norm2_g"],
                              (a["router_g"][0], a["router_e"][0]), (a["router_g_b"], a["router_e_b"]),
                              h_d, v_d, logits)
        moe(nc, cst, "moe1", NE1, logits, a["exp_w1"][0], a["exp_w3"][0], a["exp_w2"][0], h_d, v_d,
            a["final_g"].rearrange("(a d) -> a d", a=1), x2_d)


def second_block(nc, cst, col, a, x_d, out):
    h_d = nc.dram_tensor("h2", (S, D), F32).ap()
    v_d = nc.dram_tensor("v2", (S, D), F32).ap()
    q_d = nc.dram_tensor("q2", (H2, QKH, S), F32).ap()
    k_d = nc.dram_tensor("k2", (H2, QKH, S), F32).ap()
    u_d = [nc.dram_tensor(f"u2_{n}", (P, KD, S), F32).ap() for n in ("high", "low")]
    w_in = a["w_in_2"][0]
    with stage(nc, "block2") as st:
        logits = st.sb("logits", [P, NT, NG + NE2])
        mem = ExitStack()
        oT = lat = mem.enter_context(nc.sbuf_tensor("latents_then_oT2", [P, KD, S], F32))
        v_mem = ExitStack()
        v = v_mem.enter_context(nc.sbuf_tensor("v2_tokens", [P, NT, H2 * VH], F32))
        with ExitStack() as latent_mem:
            def sb(name, shape, dt=F32):
                return latent_mem.enter_context(nc.sbuf_tensor(name, shape, dt))
            kpe = sb("k_pe", [P, NT, ROPE])
            inv_l = sb("inv_latent", [P, NT, 2])
            tables = [sb(f"rope_{n}", [P, 4, NT, ROPE // 2]) for n in "qk"]
            kpe_w = sb("k_pe_w", [P, KD, ROPE])
            pos_i = sb("positions", [P, NT], I32)
            rot_g = sb("rotated_gains", [P, 2, ROPE])
            with ExitStack() as u_mem:
                uT = [u_mem.enter_context(nc.sbuf_tensor(f"uT2_{n}", [P, KD, S], F32R)) for n in ("high", "low")]
                norm_to_features(nc, cst, "norm3", [(x_d[t * P:(t + 1) * P, :], P) for t in range(NT)],
                                 a["norm_mix_g_2"], uT, 0,
                                 [(kpe_w[:], chunked(w_in)[:, :, C_KPE:C_KPE + ROPE]),
                                  (pos_i[:], a["positions_2"].rearrange("a (t p) -> p (a t)", p=P))]
                                 + [(rot_g[:, n, :], g[:, QKN:QKH].to_broadcast((P, ROPE)))
                                    for n, g in enumerate((a["q_norm_g_2"], a["k_norm_g_2"]))])
                project_features(nc, "proj2", w_in, C_QC, [(0, 0, (QL + KVL) // P)], uT, HALVES, lat,
                                 [(u_d[n], uT[n][:].bitcast(F32)) for n in range(2)],
                                 rotations_and_rotated_key(cst, kpe_w, pos_i, rot_g, tables, uT, kpe))
            queries_keys_values(nc, cst, col, a["w_uq_2"][0], a["w_ukv_2"][0], lat, inv_l, kpe, tables,
                                q_d, k_d, v)
        with ExitStack() as u_mem:
            uT = [u_mem.enter_context(nc.sbuf_tensor(f"uT2_again_{n}", [P, KD, S], F32R)) for n in ("high", "low")]

            def load_head(sp, p, j, q_aug, k_aug, sem):
                for dst, src in ((q_aug, q_d), (k_aug, k_d)):
                    sp.dma_start(dst[0:QKH, :], src[bass.ds(2 * j + p, 1)].rearrange("a r s -> (a r) s")).then_inc(sem, 16)

            attention(nc, cst, "mla", H2, 0, QKH, cst["chunk"], load_head, 2, v, oT, 0,
                      [(lambda j, n=n: uT[n][:, bass.ds(j, 1), :].bitcast(F32),
                        lambda j, n=n: u_d[n][:, bass.ds(j, 1), :]) for n in range(2)])
            recurrent_branch(nc, cst, col, w_in, a["lru_wa_2"][0], a["lru_wx_2"][0], uT, oT, v)
        v_mem.close()
        output_and_router(nc, cst, "out2", oT, a["w_out_2"][0], x_d, a["norm_ffn_g_2"],
                          (a["router_group_w_2"][0], a["router_expert_w_2"][0]),
                          (a["router_group_b_2"], a["router_expert_b_2"]), h_d, v_d, logits)
        mem.close()
        moe(nc, cst, "moe2", NE2, logits, a["w_gate_2"][0], a["w_up_2"][0], a["w_down_2"][0], h_d, v_d,
            None, out)


def program(nc, a, out):
    x2_d = nc.dram_tensor("x2", (S, D), F32).ap()
    vectors = [("pool_b", a["pool_b"][0].rearrange("g c -> (g c)")),
               ("pool_scale", a["pool_scale"][0]), ("conv_w", a["conv_w"][0].rearrange("j c -> (j c)")),
               ("conv_b", a["conv_b"][0]), ("conv_ln_g", a["conv_ln_g"][0]), ("conv_ln_b", a["conv_ln_b"][0]),
               ("conv_w2", a["conv_w_2"][0].rearrange("j c -> (j c)")),
               ("conv_b2", a["conv_b_2"][0]), ("lru_ba", a["lru_ba_2"][0]), ("lru_bx", a["lru_bx_2"][0]),
               ("lru_lambda", a["lru_lambda_2"][0])]
    rows = [(n, row_of(ap, ap.shape[0] // P), ap.shape[0] // P, P) for n, ap in vectors]
    rows += [("latent_g", row_of(a["q_a_g_2"][0], QL // P), QL // P, P),
             ("kv_a_g", row_of(a["kv_a_g_2"][0], KVL // P), KVL // P, P),
             ("qk_g", a["q_norm_g_2"][:, 0:QKN], 1, QKN), ("k_g", a["k_norm_g_2"][:, 0:QKN], 1, QKN)]
    with stage(nc, "all") as st:
        cst, col = constants(nc, st, rows)
        first_block(nc, cst, col, a, x2_d)
        second_block(nc, cst, col, a, x2_d, out.rearrange("a s d -> (a s) d"))


def kernel(**inputs):
    import concourse.bacc as bacc
    import numpy as np
    from concourse.bass_utils import run_bass_kernel_spmd

    nc = bacc.Bacc("TRN2", target_bir_lowering=False, num_devices=1)
    arrays = {name: np.ascontiguousarray(a) for name, a in inputs.items()}
    handles = {name: nc.dram_tensor(name, a.shape, mybir.dt.from_np(a.dtype), kind="ExternalInput").ap()
               for name, a in arrays.items()}
    out = nc.dram_tensor("out", (1, S, D), F32, kind="ExternalOutput").ap()
    program(nc, handles, out)
    r = run_bass_kernel_spmd(nc, [arrays], core_ids=[0])
    return r.results[0]["out"]
```
